# Optimizing a Trainium2 kernel written in Bass

```python
import jax, jax.numpy as jnp
from jax import lax
import numpy as np

D_MODEL = 1024
BATCH = 1
SEQ = 512
DEPTH = 1

D_MIX = D_MODEL
D_RG = D_MIX // 2
D_SC = D_MIX - D_RG
RG_HEADS = 8
RG_HEAD_DIM = D_RG // RG_HEADS
RG_CONV = 4
RG_C = 8.0
SC_GROUPS = 8
SC_CONV = 3
D_IN_PROJ = 2 * D_RG + 3 * D_SC
N_GROUPS = 4
EXPERTS_PER_GROUP = 8
N_EXPERTS = N_GROUPS * EXPERTS_PER_GROUP
TOP_K = 2
D_EXPERT = D_MODEL // 4
LN_EPS = 1e-5
DEEPNORM_ALPHA = (2 * DEPTH) ** 0.25
DEEPNORM_BETA = (8 * DEPTH) ** -0.25

kernel_name = "hymba_rglru_shortconv_hmoe_deepnorm"

def layer_norm(x, g, b):
    xf = x.astype(jnp.float32)
    mu = jnp.mean(xf, axis=-1, keepdims=True)
    var = jnp.mean(jnp.square(xf - mu), axis=-1, keepdims=True)
    y = (xf - mu) * lax.rsqrt(var + LN_EPS) * g.astype(jnp.float32) + b.astype(jnp.float32)
    return y.astype(x.dtype)

def causal_depthwise_conv(x, w):
    k, c = w.shape
    rhs = w.astype(x.dtype)[:, None, :]
    return lax.conv_general_dilated(
        x, rhs, window_strides=(1,), padding=[(k - 1, 0)],
        dimension_numbers=("NWC", "WIO", "NWC"), feature_group_count=c)

def _linear_recurrence_combine(e1, e2):
    a1, b1 = e1
    a2, b2 = e2
    return (a1 * a2, a2 * b1 + b2)

def rg_lru(xc, gate_a_w, gate_a_b, gate_x_w, gate_x_b, lam):
    bsz, s, _ = xc.shape
    xh = xc.reshape(bsz, s, RG_HEADS, RG_HEAD_DIM)
    r = jax.nn.sigmoid(jnp.einsum("bshi,hij->bshj", xh, gate_a_w).reshape(bsz, s, D_RG) + gate_a_b)
    i = jax.nn.sigmoid(jnp.einsum("bshi,hij->bshj", xh, gate_x_w).reshape(bsz, s, D_RG) + gate_x_b)
    r = r.astype(jnp.float32)
    i = i.astype(jnp.float32)
    log_a = -RG_C * r * jax.nn.softplus(-lam.astype(jnp.float32))
    a = jnp.exp(log_a)
    mult = jnp.sqrt(-jnp.expm1(2.0 * log_a))
    u = mult * (i * xc.astype(jnp.float32))
    _, h = lax.associative_scan(_linear_recurrence_combine, (a, u), axis=1)
    return h.astype(xc.dtype)

def hybrid_token_mixer(x, w_in, rg_conv_w, rg_conv_b, rg_gate_a_w, rg_gate_a_b,
                       rg_gate_x_w, rg_gate_x_b, rg_lambda, sc_conv_w, w_out):
    proj = jnp.einsum("bsd,de->bse", x, w_in)
    splits = [D_RG, 2 * D_RG, 2 * D_RG + D_SC, 2 * D_RG + 2 * D_SC]
    rg_x, rg_gate, sc_b, sc_c, sc_v = jnp.split(proj, splits, axis=-1)
    xc = causal_depthwise_conv(rg_x, rg_conv_w) + rg_conv_b
    h = rg_lru(xc, rg_gate_a_w, rg_gate_a_b, rg_gate_x_w, rg_gate_x_b, rg_lambda)
    y_rg = h * jax.nn.gelu(rg_gate)
    y_sc = sc_b * causal_depthwise_conv(sc_c * sc_v, sc_conv_w)
    y = jnp.concatenate([y_rg, y_sc], axis=-1)
    return jnp.einsum("bse,ed->bsd", y, w_out)

def hierarchical_moe(x, router_group_w, router_group_b, router_expert_w, router_expert_b,
                     exp_w_gate, exp_w_up, exp_w_down):
    bsz, s, d = x.shape
    t = x.reshape(bsz * s, d)
    g_logits = (t @ router_group_w + router_group_b).astype(jnp.float32)
    g_prob = jax.nn.softmax(g_logits, axis=-1)
    g_top_p, g_idx = lax.top_k(g_prob, 1)
    e_logits = (t @ router_expert_w + router_expert_b).astype(jnp.float32)
    e_logits = e_logits.reshape(-1, N_GROUPS, EXPERTS_PER_GROUP)
    e_sel = jnp.take_along_axis(e_logits, g_idx[:, :, None], axis=1)[:, 0]
    e_top_v, e_top_i = lax.top_k(e_sel, TOP_K)
    weights = jax.nn.softmax(e_top_v, axis=-1) * g_top_p
    global_idx = g_idx * EXPERTS_PER_GROUP + e_top_i
    combine = jnp.sum(jax.nn.one_hot(global_idx, N_EXPERTS, dtype=jnp.float32) * weights[..., None], axis=1)
    combine = combine.astype(x.dtype)
    hg = jnp.einsum("td,edf->tef", t, exp_w_gate)
    hu = jnp.einsum("td,edf->tef", t, exp_w_up)
    hid = jax.nn.silu(hg) * hu * combine[:, :, None]
    out = jnp.einsum("tef,efd->td", hid, exp_w_down)
    return out.reshape(bsz, s, d)

def setup_inputs(seed: int = 0) -> dict:
    key = jax.random.key(seed)
    ks = jax.random.split(key, 24)
    f32 = jnp.float32
    nrm = lambda k, shape, scale: jax.random.normal(k, shape, f32) * scale
    x = jax.random.normal(ks[0], (BATCH, SEQ, D_MODEL), f32)
    w_in = nrm(ks[1], (D_MODEL, D_IN_PROJ), D_MODEL ** -0.5)
    rg_conv_w = nrm(ks[2], (RG_CONV, D_RG), RG_CONV ** -0.5)
    rg_conv_b = nrm(ks[3], (D_RG,), 0.02)
    rg_gate_a_w = nrm(ks[4], (RG_HEADS, RG_HEAD_DIM, RG_HEAD_DIM), RG_HEAD_DIM ** -0.5)
    rg_gate_a_b = nrm(ks[5], (D_RG,), 0.02)
    rg_gate_x_w = nrm(ks[6], (RG_HEADS, RG_HEAD_DIM, RG_HEAD_DIM), RG_HEAD_DIM ** -0.5)
    rg_gate_x_b = nrm(ks[7], (D_RG,), 0.02)
    u = jax.random.uniform(ks[8], (D_RG,), f32, 0.9, 0.999)
    sq = u ** (1.0 / RG_C)
    rg_lambda = jnp.log(sq) - jnp.log1p(-sq)
    sc_conv_w = nrm(ks[9], (SC_CONV, D_SC), SC_CONV ** -0.5)
    w_out = nrm(ks[10], (D_MIX, D_MODEL), D_MIX ** -0.5) * DEEPNORM_BETA
    ln1_g = 1.0 + nrm(ks[11], (D_MODEL,), 0.02)
    ln1_b = nrm(ks[12], (D_MODEL,), 0.02)
    router_group_w = nrm(ks[13], (D_MODEL, N_GROUPS), D_MODEL ** -0.5)
    router_group_b = nrm(ks[14], (N_GROUPS,), 0.01)
    router_expert_w = nrm(ks[15], (D_MODEL, N_EXPERTS), D_MODEL ** -0.5)
    router_expert_b = nrm(ks[16], (N_EXPERTS,), 0.01)
    exp_w_gate = nrm(ks[17], (N_EXPERTS, D_MODEL, D_EXPERT), D_MODEL ** -0.5)
    exp_w_up = nrm(ks[18], (N_EXPERTS, D_MODEL, D_EXPERT), D_MODEL ** -0.5)
    exp_w_down = nrm(ks[19], (N_EXPERTS, D_EXPERT, D_MODEL), D_EXPERT ** -0.5) * DEEPNORM_BETA
    ln2_g = 1.0 + nrm(ks[20], (D_MODEL,), 0.02)
    ln2_b = nrm(ks[21], (D_MODEL,), 0.02)
    return {"x": x, "w_in": w_in, "rg_conv_w": rg_conv_w, "rg_conv_b": rg_conv_b,
            "rg_gate_a_w": rg_gate_a_w, "rg_gate_a_b": rg_gate_a_b,
            "rg_gate_x_w": rg_gate_x_w, "rg_gate_x_b": rg_gate_x_b,
            "rg_lambda": rg_lambda, "sc_conv_w": sc_conv_w, "w_out": w_out,
            "ln1_g": ln1_g, "ln1_b": ln1_b,
            "router_group_w": router_group_w, "router_group_b": router_group_b,
            "router_expert_w": router_expert_w, "router_expert_b": router_expert_b,
            "exp_w_gate": exp_w_gate, "exp_w_up": exp_w_up, "exp_w_down": exp_w_down,
            "ln2_g": ln2_g, "ln2_b": ln2_b}

def reference(x, w_in, rg_conv_w, rg_conv_b, rg_gate_a_w, rg_gate_a_b, rg_gate_x_w,
              rg_gate_x_b, rg_lambda, sc_conv_w, w_out, ln1_g, ln1_b,
              router_group_w, router_group_b, router_expert_w, router_expert_b,
              exp_w_gate, exp_w_up, exp_w_down, ln2_g, ln2_b):
    h = x
    for _ in range(DEPTH):
        mix = hybrid_token_mixer(h, w_in, rg_conv_w, rg_conv_b, rg_gate_a_w, rg_gate_a_b,
                                 rg_gate_x_w, rg_gate_x_b, rg_lambda, sc_conv_w, w_out)
        h = layer_norm(DEEPNORM_ALPHA * h + mix, ln1_g, ln1_b)
        ffn = hierarchical_moe(h, router_group_w, router_group_b, router_expert_w,
                               router_expert_b, exp_w_gate, exp_w_up, exp_w_down)
        h = layer_norm(DEEPNORM_ALPHA * h + ffn, ln2_g, ln2_b)
    return h


_drawn_inputs = setup_inputs


def setup_inputs(seed=0):
    import zlib

    import numpy as np

    out = dict(_drawn_inputs(seed))
    spreads = {}
    factors = {'rg_gate_a_b': 36.758,
     'rg_gate_x_b': 35.302,
     'router_group_b': 18.269,
     'router_expert_b': 8.0,
     'ln2_g': 8.72,
     'ln2_b': 8.116}
    for name, (base, spread) in spreads.items():
        noise = np.random.default_rng([zlib.crc32(name.encode()), seed]).standard_normal(out[name].shape)
        drawn = base * np.exp(spread * noise) if base else spread * noise
        out[name] = __import__('jax').numpy.asarray(drawn.astype(out[name].dtype))
    for name, factor in factors.items():
        out[name] = (out[name] * factor).astype(out[name].dtype)
    return out
```

```python
from contextlib import ExitStack

import concourse.bass as bass
from concourse import mybir

F32 = mybir.dt.float32
F32R = mybir.dt.float32r
BF16 = mybir.dt.bfloat16
U32 = mybir.dt.uint32
I32 = mybir.dt.int32
ALU = mybir.AluOpType
ACT = mybir.ActivationFunctionType
AX = mybir.AxisListType.X

P = 128
BLOCK = 64
RING = 6
TOP_K = 2
RG_C = 8.0
LN_EPS = 1e-5
ALPHA = 2.0 ** 0.25
FAR = 1e30
RNE = 12582912.0
NO_ROW = 1048576.0
LOG_TERMS = 9


def hybrid_moe_layer(
    nc, x, w_in, rg_conv_w, rg_conv_b, rg_gate_a_w, rg_gate_a_b, rg_gate_x_w, rg_gate_x_b,
    rg_lambda, sc_conv_w, w_out, ln1_g, ln1_b, router_group_w, router_group_b,
    router_expert_w, router_expert_b, exp_w_gate, exp_w_up, exp_w_down, ln2_g, ln2_b, out,
):
    _, T, D = x.shape
    RG_TAPS, D_RG = rg_conv_w.shape
    SC_TAPS, D_SC = sc_conv_w.shape
    N_GROUPS = router_group_w.shape[1]
    N_EXP, _, F = exp_w_gate.shape
    PER_GROUP = N_EXP // N_GROUPS
    NR = N_GROUPS + N_EXP
    TT = T // P
    KT = D // P
    CT = D_RG // P
    H = D // 2
    CHUNK = 2048
    WCOLS = CHUNK // KT
    N_IN = 5 * D_RG // WCOLS
    N_OUT = D * D // P // CHUNK
    N_CHUNKS = N_IN + N_OUT
    HL = 3
    PER_BLOCK = D_RG // WCOLS
    MAX_OVER = TOP_K * T // BLOCK
    ITEMS = N_EXP + MAX_OVER
    assert T == 512 and D == 1024 and D_RG == D_SC == 512 and F == 256 and N_OUT == 4
    PARAMS = RG_TAPS + 4 + SC_TAPS
    P_RGW, P_RGB, P_AB, P_XB, P_LAM, P_SCW = 0, RG_TAPS, RG_TAPS + 1, RG_TAPS + 2, RG_TAPS + 3, RG_TAPS + 4

    with ExitStack() as ctx:
        base = -(-nc.sbuf_base // 64) * 64
        place = [base]

        def at(name, shape, dt, offset):
            return nc.alloc_sbuf_tensor_at(name, shape, dt, offset=offset)

        def sb(name, shape, dt=F32):
            n = 4 if dt != BF16 else 2
            for s in shape[1:]:
                n *= s
            t = at(name, shape, dt, place[0])
            place[0] += -(-n // 32) * 32
            return t

        xres = sb("xres", [P, TT, D])
        ln_g = sb("ln_g", [P, D])
        ln_b = sb("ln_b", [P, D])
        ident = sb("ident", [P, P])
        tri = sb("tri", [P, P], BF16)
        ones = sb("ones", [P, P], BF16)
        par = sb("par", [P, CT, PARAMS])
        c8 = sb("c8", [P, CT])
        nc8 = sb("nc8", [P, CT])
        sp = sb("sp", [P, 6, CT])
        wr = sb("wr", [P, KT, NR])
        rbias = sb("rbias", [P, NR])
        stats = sb("stats", [P, TT, 2, 6])
        moments = sb("moments", [P, TT, 2])
        rstd = sb("rstd", [P, TT])
        shift = sb("shift", [P, TT])
        logits = sb("logits", [P, TT, NR])
        gmax = sb("gmax", [P, TT])
        gkey = sb("gkey", [P, TT, N_GROUPS])
        gkmax = sb("gkmax", [P, TT])
        ghot = sb("ghot", [P, TT, N_GROUPS])
        vtop = sb("vtop", [P, TOP_K, TT])
        kkey = sb("kkey", [P, TOP_K, TT])
        chosen_b = sb("chosen_b", [P, TT, N_EXP], BF16)
        rank = sb("rank", [P, TOP_K * TT])
        expert = sb("expert", [P, TOP_K * TT])
        extra = sb("extra", [P, N_EXP])
        extra_sum = sb("extra_sum", [P, N_EXP])
        extra_base = sb("extra_base", [P, N_EXP])
        zeros = sb("zeros", [P, N_EXP])
        obase = sb("obase", [P, TOP_K * TT])
        blk = sb("blk", [P, TOP_K * TT])
        over = sb("over", [P, TOP_K * TT])
        item = sb("item", [P, TOP_K * TT])
        slot = sb("slot", [P, TOP_K * TT])
        x_rows = sb("x_rows", [P, ITEMS], U32)
        y_rows = sb("y_rows", [P, ITEMS], U32)
        x_row_now = sb("x_row_now", [P, 1], U32)
        y_row_now = sb("y_row_now", [P, 1], U32)
        held = sb("held", [P, 1])
        over_exp = sb("over_exp", [1, MAX_OVER])
        over_exp_i = sb("over_exp_i", [1, MAX_OVER], I32)
        n_over = sb("n_over", [1, 1], I32)
        gexp = sb("gexp", [P, TT, N_GROUPS])
        gsum = sb("gsum", [P, TT])
        ptop = sb("ptop", [P, TT])
        vdiff = sb("vdiff", [P, TT])
        vexp = sb("vexp", [P, TT])
        wsum = sb("wsum", [P, TT])
        weight = sb("weight", [P, TOP_K, TT])
        iota_f = sb("iota_f", [P, 160])
        down4, down32 = iota_f[:, 0:N_GROUPS], iota_f[:, 4:4 + N_EXP]
        up_slot = iota_f[:, 36:36 + BLOCK]
        pair1 = iota_f[:, 100:100 + TOP_K * TT]
        half = iota_f[:, 108:109]
        up_item = iota_f[:, 112:160]

        xg = [None] * 2
        xTg = [None] * 2
        shared = place[0]
        for b in range(2):
            xg[b] = sb(f"xg{b}", [P, H])
        for b in range(2):
            xTg[b] = sb(f"xTg{b}", [P, 4, P])
        gated = [sb(f"gated{b}", [BLOCK, F]) for b in range(2)]
        hid = [sb(f"hid{b}", [P, F]) for b in range(2)]
        hidT = [sb(f"hidT{b}", [P, 2, BLOCK]) for b in range(2)]
        ys = [sb(f"ys{b}", [P, H]) for b in range(2)]
        gelu_g = at("gelu_g", [P, CT, T], F32, shared)
        h1T = [at(f"h1T{b}", [P, KT, P], F32, shared + 4096 * b) for b in range(2)]
        shared_y = shared + 8192
        assert place[0] - shared_y >= 8192

        ring = place[0]
        SLOT = 24576
        wgu = [at(f"wgu{s}", [P, 2, KT, F], F32, ring + s * SLOT) for s in range(RING)]
        wdn = [at(f"wdn{s}", [P, 2, D], F32, ring + s * SLOT + 16384) for s in range(RING)]
        spare = ring + RING * SLOT
        assert spare + 16384 <= nc.sbuf_usable_end, (spare, nc.sbuf_usable_end)
        raw = [at(f"raw{b}", [P, CHUNK], F32, spare + 8192 * b) for b in range(2)]

        xT_hi = at("xT_hi", [P, KT, T], F32R, ring)
        xT_lo = at("xT_lo", [P, KT, T], F32R, ring + 16384)
        chan = ring + 32768
        PAD = RG_TAPS - 1
        rg_pad = [at(f"rg_pad{j}", [P, PAD + T], F32, chan + 2080 * j) for j in range(CT)]
        assert 2080 * CT <= 8320
        chan += 8320
        sc_c = [at(f"sc_c{j}", [P, T], F32, chan - 8320 + 2080 * j) for j in range(CT)]
        conv = [at(f"conv{j}", [P, T], F32, chan + 2080 * j) for j in range(CT)]
        sc_pad = [at(f"sc_pad{j}", [P, SC_TAPS - 1 + T], F32, chan + 2080 * j) for j in range(CT)]
        chan += 8320
        gr = [at(f"gr{j}", [P, T], F32, chan + 2048 * j) for j in range(CT)]
        sc_conv = [at(f"sc_conv{j}", [P, T], F32, chan + 2048 * j) for j in range(CT)]
        chan += 8192
        gi = [at(f"gi{j}", [P, T], F32, chan + 2048 * j) for j in range(CT)]
        y_sc = [at(f"y_sc{j}", [P, T], F32, chan + 2048 * j) for j in range(CT)]
        chan += 8192
        tanhs = at("tanhs", [P, 3, T], F32, chan)
        chan += 3 * 2048
        assert chan <= ring + 3 * SLOT
        w_hi = [at(f"w_hi{b}", [P, CHUNK], F32R, ring + (3 + b) * SLOT) for b in range(HL)]
        w_lo = [at(f"w_lo{b}", [P, CHUNK], F32R, ring + (3 + b) * SLOT + 8192) for b in range(HL)]
        y_at = [ring + (3 + s) * SLOT + 16384 + 4096 * h for s in range(3) for h in range(2)] + [shared_y, shared_y + 4096]
        y_hi = [at(f"y_hi{k}", [P, T], F32R, y_at[k]) for k in range(KT)]
        y_lo = [at(f"y_lo{k}", [P, T], F32R, y_at[k] + 2048) for k in range(KT)]

        par_rows = at("par_rows", [PARAMS, D_RG], F32, shared)
        iota_i = at("iota_i", [P, 160], I32, y_at[5])
        tanh3 = at("tanh3", [P, T], F32, y_at[6])
        wga = at("wga", [P, CT, 64], F32, y_at[7])
        wgx = at("wgx", [P, CT, 64], F32, y_at[7] + 2048)
        th = [tanhs[:, j, :] for j in range(3)] + [tanh3[:, :]]

        pair_y = [[at(f"pair_y{k}_{t}", [P, D], F32, ring + 2 * SLOT + 4096 * (TOP_K * t + k)) for k in range(TOP_K)] for t in range(TT)]

        hot_slot = at("hot_slot", [P, TOP_K * TT, P], F32, spare)
        hot_item = at("hot_item", [P, TOP_K * TT, ITEMS], F32, spare + 4096)
        over_cmp = at("over_cmp", [1, MAX_OVER, N_EXP], F32, spare + 6144)
        prod = at("prod", [P, TOP_K, TT, N_EXP], F32, spare + 8192)
        chosen = at("chosen", [P, TOP_K, TT, N_EXP], F32, spare + 9216)
        masked = at("masked", [P, TT, N_EXP], F32, spare + 10240)
        masked2 = at("masked2", [P, TT, N_EXP], F32, spare + 10752)
        ekey = at("ekey", [P, TT, N_EXP], F32, spare + 11264)
        table = at("table", [P, ITEMS], F32, spare + 11776)
        table_x = at("table_x", [P, ITEMS], F32, spare + 12032)
        empty = at("empty", [P, ITEMS], F32, spare + 12288)

        h1_rows = nc.dram_tensor("h1_rows", (2 * T, H), F32, kind="Internal").ap()
        y_pairs = nc.dram_tensor("y_pairs", (2 * TOP_K * T, H), F32, kind="Internal").ap()

        psum = [ctx.enter_context(nc.psum_tensor(f"bank{b}", [P, 512], F32)) for b in range(8)]

        def sem(name):
            return ctx.enter_context(nc.semaphore(name))

        params_in = sem("params_in")
        gates_in = sem("gates_in")
        x_in = [sem(f"x_in{t}") for t in range(TT)]
        raw_in = [sem(f"raw_in{b}") for b in range(2)]
        ln1_in = sem("ln1_in")
        ln2_in = sem("ln2_in")
        router_in = sem("router_in")
        gu_in = [sem(f"gu_in{s}") for s in range(RING)]
        dn_in = [sem(f"dn_in{s}") for s in range(RING)]
        over_gu_in = sem("over_gu_in")
        over_dn_in = sem("over_dn_in")
        ident_done = sem("ident_done")
        const_pool = sem("const_pool")
        const_done = sem("const_done")
        pads_zero = sem("pads_zero")
        par_turned = sem("par_turned")
        par_ready = sem("par_ready")
        x_turned = sem("x_turned")
        xT_hi_ready = sem("xT_hi_ready")
        xT_lo_ready = sem("xT_lo_ready")
        w_hi_ready = sem("w_hi_ready")
        w_lo_ready = sem("w_lo_ready")
        chunk_used = sem("chunk_used")
        projected = sem("projected")
        act_evacuated = sem("act_evacuated")
        dve_evacuated = sem("dve_evacuated")
        xc_ready = sem("xc_ready")
        gates_summed = sem("gates_summed")
        gates_ready = sem("gates_ready")
        decay_in = sem("decay_in")
        c8_ready = sem("c8_ready")
        lam_abs = sem("lam_abs")
        lam_exp = sem("lam_exp")
        drive_sq = sem("drive_sq")
        drive_root = sem("drive_root")
        y_ready = sem("y_ready")
        y_hi_ready = sem("y_hi_ready")
        y_lo_ready = sem("y_lo_ready")
        mixed = sem("mixed")
        mixed_used = sem("mixed_used")
        var_ready = sem("var_ready")
        dev_ready = sem("dev_ready")
        moments_ready = sem("moments_ready")
        normed = sem("normed")
        h1_ready = sem("h1_ready")
        h1_stored = sem("h1_stored")
        h1_turned = sem("h1_turned")
        h1T_ready = sem("h1T_ready")
        routed = sem("routed")
        logits_summed = sem("logits_summed")
        chosen_ready = sem("chosen_ready")
        counted = sem("counted")
        hot_ready = sem("hot_ready")
        table_summed = sem("table_summed")
        rows_ready = sem("rows_ready")
        gdiff_ready = sem("gdiff_ready")
        gexp_ready = sem("gexp_ready")
        dve = sem("dve_chain")
        act_chain = sem("act_chain")
        xg_zero = sem("xg_zero")
        hid_zero = sem("hid_zero")
        x_gathered = [sem(f"x_gathered{b}") for b in range(2)]
        y_scattered = [sem(f"y_scattered{b}") for b in range(2)]
        over_x = sem("over_x")
        over_y = sem("over_y")
        xg_turned = sem("xg_turned")
        xTg_ready = sem("xTg_ready")
        gu_summed = sem("gu_summed")
        gated_ready = sem("gated_ready")
        hid_ready = sem("hid_ready")
        hid_turned = sem("hid_turned")
        hidT_ready = sem("hidT_ready")
        dn_summed = sem("dn_summed")
        y_copied = sem("y_copied")
        pool_chain = sem("pool_chain")
        pairs_in = [sem(f"pairs_in{t}") for t in range(TT)]
        h1_scaled = sem("h1_scaled")
        var2_ready = sem("var2_ready")
        dev2_ready = sem("dev2_ready")
        moments2_ready = sem("moments2_ready")
        normed2 = sem("normed2")
        out_ready = sem("out_ready")
        out_scaled = sem("out_scaled")
        out_stored = sem("out_stored")

        x_rows_dram = x.rearrange("a t d -> (a t) d")
        out_rows = out.rearrange("a t d -> (a t) d")
        row = lambda v: v.rearrange("(a n) -> a n", a=1)

        BLOCK_ORDER = (0, 1, 3, 4, 2)

        def w_in_chunk(c):
            col = BLOCK_ORDER[c // PER_BLOCK] * D_RG + c % PER_BLOCK * WCOLS
            return w_in[:, col:col + WCOLS].rearrange("(k p) n -> p k n", p=P)

        def w_out_chunk(c):
            h, kh = divmod(c - N_IN, 2)
            return w_out[kh * 512:(kh + 1) * 512, h * 512:(h + 1) * 512].rearrange("(k p) n -> p k n", p=P)

        def static(i):
            return isinstance(i, int)

        def gu_of(w, e):
            w = w[e:e + 1] if static(e) else w[bass.ds(e, 1)]
            return w.rearrange("a (h p j) f -> p (a h) (j f)", h=2, p=P)

        def dn_of(e):
            w = exp_w_down[e:e + 1] if static(e) else exp_w_down[bass.ds(e, 1)]
            return w.rearrange("a (p j) d -> p (a j d)", p=P)

        def gu_place(s, which):
            return wgu[s][:, which, :, :].rearrange("p (h j) f -> p h (j f)", h=2)

        def rounds(engine, body):
            for u in range(RING):
                body(u, u, 0)
            with engine.Fori(1, N_EXP // RING) as r:
                for u in range(RING):
                    body(r * RING + u, u, r)
            for u in range(N_EXP % RING):
                body(N_EXP // RING * RING + u, u, N_EXP // RING)

        def overflow(engine, body):
            n = engine.value_load(n_over[0:1, 0:1], min_val=0, max_val=MAX_OVER)
            with engine.If(n > 0):
                with engine.Fori(0, n) as j:
                    body(j)

        def per_pair(i, b):
            return 8 * (i - b)

        def wait_free(eng, done, i, lag):
            if not static(i) or i >= lag:
                eng.wait_ge(done, i + 1 - lag)

        block = ctx.enter_context(nc.Block())

        @block.sync
        def _(sp_):
            for t in range(TT):
                sp_.dma_start(xres[:, t, :], x_rows_dram[t * P:(t + 1) * P, :]).then_inc(x_in[t], 16)
            for c in range(N_CHUNKS):
                if c >= 2:
                    sp_.wait_ge(w_hi_ready, c - 1)
                    sp_.wait_ge(w_lo_ready, c - 1)
                k = KT if c < N_IN else KT // 2
                sp_.dma_start(raw[c % 2][:, :].rearrange("p (k n) -> p k n", k=k),
                              w_in_chunk(c) if c < N_IN else w_out_chunk(c)).then_inc(raw_in[c % 2], 16)

            def load_gu(e, s, done):
                sp_.dma_start(gu_place(s, 0), gu_of(exp_w_gate, e)).then_inc(done, 16)
                sp_.dma_start(gu_place(s, 1), gu_of(exp_w_up, e)).then_inc(done, 16)

            def load_dn(e, s, done):
                sp_.dma_start(wdn[s][:, :, :].rearrange("p j d -> p (j d)"), dn_of(e)).then_inc(done, 16)

            sp_.wait_ge(chunk_used, N_IN)
            sp_.wait_ge(y_lo_ready, KT)
            for s in range(3):
                load_gu(s, s, gu_in[s])
                load_dn(s, s, dn_in[s])
            early = (N_CHUNKS - 3) % HL
            sp_.wait_ge(chunk_used, N_CHUNKS - 2)
            load_gu(3 + early, 3 + early, gu_in[3 + early])
            sp_.wait_ge(mixed, 2 * TT)
            for s in range(3, RING):
                if s != 3 + early:
                    load_gu(s, s, gu_in[s])
                load_dn(s, s, dn_in[s])

            def refill(i, u):
                sp_.wait_ge(gu_summed, i - RING + 1)
                load_gu(i, u, gu_in[u])
                sp_.wait_ge(dn_summed, i - RING + 1)
                load_dn(i, u, dn_in[u])

            with sp_.Fori(1, N_EXP // RING) as r:
                for u in range(RING):
                    refill(r * RING + u, u)
            for u in range(N_EXP % RING):
                refill(N_EXP // RING * RING + u, u)
            def load_over(j):
                e = sp_.value_load(over_exp_i[0:1, bass.ds(j, 1)], min_val=0, max_val=N_EXP - 1)
                sp_.wait_ge(dn_summed, j + N_EXP)
                load_gu(e, 0, gu_in[0])
                load_dn(e, 0, dn_in[0])

            overflow(sp_, load_over)
            sp_.wait_ge(y_scattered[1], 16 * (N_EXP // 2))
            n = sp_.value_load(n_over[0:1, 0:1], min_val=0, max_val=MAX_OVER)
            sp_.wait_ge(y_scattered[0], 16 * n + 16 * (N_EXP // 2))
            for t in range(TT):
                for k in range(TOP_K):
                    src = y_pairs[2 * (k * T + t * P):2 * (k * T + (t + 1) * P), :]
                    sp_.dma_start(pair_y[t][k][:, :], src.rearrange("(p a) h -> p (a h)", a=2)).then_inc(pairs_in[t], 16)
            for t in range(TT):
                sp_.wait_ge(out_ready, t + 1)
                sp_.dma_start(out_rows[t * P:(t + 1) * P, :], pair_y[t][1][:, :]).then_inc(out_stored, 16)
            sp_.wait_ge(out_stored, 16 * TT)

        @block.gpsimd
        def _(pool):
            for n, v in enumerate((rg_conv_w, row(rg_conv_b), row(rg_gate_a_b), row(rg_gate_x_b), row(rg_lambda), sc_conv_w)):
                at_row = (P_RGW, P_RGB, P_AB, P_XB, P_LAM, P_SCW)[n]
                pool.dma_start(par_rows[at_row:at_row + v.shape[0], :], v).then_inc(params_in, 16)
            pool.memset(ident[:, :], 0.0).then_inc(ident_done, 1)
            pool.wait_ge(ident_done, 1)
            pool.affine_select(out=ident[:, :], in_=ident[:, :], compare_op=ALU.not_equal, fill=1.0,
                               base=0, pattern=[[-1, P]], channel_multiplier=1).then_inc(ident_done, 1)
            for w, dst in ((rg_gate_a_w, wga), (rg_gate_x_w, wgx)):
                pool.dma_start(dst[:, :, :], w.rearrange("(a b) i j -> (b i) a j", b=2)).then_inc(gates_in, 16)
            pool.memset(tri[:, :], 1.0).then_inc(const_pool, 1)
            pool.memset(ones[:, :], 1.0).then_inc(const_pool, 1)
            pool.iota(iota_i[:, 0:N_GROUPS], pattern=[[-1, N_GROUPS]], base=N_GROUPS, channel_multiplier=0).then_inc(const_pool, 1)
            pool.iota(iota_i[:, 4:4 + N_EXP], pattern=[[-1, N_EXP]], base=N_EXP, channel_multiplier=0).then_inc(const_pool, 1)
            pool.iota(iota_i[:, 36:36 + BLOCK], pattern=[[1, BLOCK]], base=0, channel_multiplier=0).then_inc(const_pool, 1)
            pool.iota(iota_i[:, 100:108], pattern=[[2 * P, TOP_K * TT]], base=1, channel_multiplier=2).then_inc(const_pool, 1)
            pool.memset(iota_i[:, 108:112], 0).then_inc(const_pool, 1)
            pool.iota(iota_i[:, 112:160], pattern=[[1, ITEMS]], base=0, channel_multiplier=0).then_inc(const_pool, 1)
            pool.wait_ge(const_pool, 8)
            pool.affine_select(out=tri[:, :], in_=tri[:, :], compare_op=ALU.is_gt, fill=0.0,
                               base=0, pattern=[[1, P]], channel_multiplier=-1).then_inc(const_pool, 1)
            pool.wait_ge(const_pool, 9)
            pool.memset(iota_i[64:128, 108:109], 1).then_inc(const_pool, 1)
            pool.wait_ge(const_pool, 10)
            pool.memset(zeros[:, :], 0.0).then_inc(const_pool, 1)
            pool.memset(held[:, :], 1.0).then_inc(pool_chain, 1)
            pool.wait_ge(const_pool, 11)
            pool.tensor_copy(iota_f[:, :], iota_i[:, :]).then_inc(const_done, 1)
            for j in range(CT):
                pool.memset(rg_pad[j][:, 0:PAD], 0.0).then_inc(pads_zero, 1)
            pool.dma_start(ln_g[:, :], row(ln1_g).to_broadcast([P, D])).then_inc(ln1_in, 16)
            pool.dma_start(ln_b[:, :], row(ln1_b).to_broadcast([P, D])).then_inc(ln1_in, 16)
            pool.dma_start(wr[:, :, 0:N_GROUPS], router_group_w.rearrange("(k p) n -> p k n", p=P)).then_inc(router_in, 16)
            pool.dma_start(wr[:, :, N_GROUPS:NR], router_expert_w.rearrange("(k p) n -> p k n", p=P)).then_inc(router_in, 16)
            pool.dma_start(rbias[:, 0:N_GROUPS], row(router_group_b).to_broadcast([P, N_GROUPS])).then_inc(router_in, 16)
            pool.dma_start(rbias[:, N_GROUPS:NR], row(router_expert_b).to_broadcast([P, N_EXP])).then_inc(router_in, 16)
            pool.wait_ge(y_ready, CT)
            for j in range(CT):
                pool.memset(sc_pad[j][:, 0:SC_TAPS - 1], 0.0).then_inc(pads_zero, 1)
            for t in range(TT):
                pool.wait_ge(h1_ready, t + 1)
                pool.dma_start(h1_rows[2 * t * P:2 * (t + 1) * P, :].rearrange("(p a) h -> p (a h)", a=2), xres[:, t, :]).then_inc(h1_stored, 16)
            pool.wait_ge(routed, TT)
            for b in range(2):
                pool.memset(xg[b][:, :], 0.0).then_inc(xg_zero, 1)
                pool.memset(hid[b][:, :], 0.0).then_inc(hid_zero, 1)
            pool.wait_ge(xg_zero, 2)
            pool.wait_ge(rows_ready, 1)
            pool.wait_ge(h1_stored, 16 * TT)

            def gather(b, rows):
                pool.indirect_dma_start(out=xg[b][:, :], out_offset=None, in_=h1_rows,
                                        in_offset=bass.IndirectOffsetOnAxis(ap=rows, axis=0),
                                        bounds_check=2 * T - 1, oob_is_err=False).then_inc(x_gathered[b], 16)

            def scatter(b, rows):
                pool.indirect_dma_start(out=y_pairs, out_offset=bass.IndirectOffsetOnAxis(ap=rows, axis=0),
                                        in_=ys[b][:, :], in_offset=None,
                                        bounds_check=2 * TOP_K * T - 1, oob_is_err=False).then_inc(y_scattered[b], 16)

            for i in range(2):
                gather(i, x_rows[:, i:i + 1])
            pool.dma_start(ln_g[:, :], row(ln2_g).to_broadcast([P, D])).then_inc(ln2_in, 16)
            pool.dma_start(ln_b[:, :], row(ln2_b).to_broadcast([P, D])).then_inc(ln2_in, 16)
            for i in range(N_EXP):
                if i + 2 < N_EXP:
                    pool.wait_ge(xg_turned, i + 1)
                    gather(i % 2, x_rows[:, i + 2:i + 3])
                pool.wait_ge(y_copied, i + 1)
                scatter(i % 2, y_rows[:, i:i + 1])

            def over_rows(j):
                i, n = j + N_EXP, j * 5
                pool.wait_ge(pool_chain, n + 1)
                pool.tensor_tensor(held[:, :], held[:, :], held[:, :], ALU.mult).then_inc(pool_chain, 1)
                pool.tensor_copy(x_row_now[:, :], x_rows[:, bass.ds(i, 1)]).then_inc(pool_chain, 1)
                pool.tensor_copy(y_row_now[:, :], y_rows[:, bass.ds(i, 1)]).then_inc(pool_chain, 1)
                pool.wait_ge(pool_chain, n + 4)
                pool.wait_ge(xg_turned, i)
                pool.tensor_tensor(held[:, :], held[:, :], held[:, :], ALU.mult).then_inc(pool_chain, 1)
                gather(0, x_row_now[:, :])
                pool.wait_ge(pool_chain, n + 5)
                pool.wait_ge(y_copied, i + 1)
                pool.tensor_tensor(held[:, :], held[:, :], held[:, :], ALU.mult).then_inc(pool_chain, 1)
                scatter(0, y_row_now[:, :])
                pool.wait_ge(y_scattered[0], 16 * j + 16 * (N_EXP // 2 + 1))
                pool.wait_ge(pool_chain, n + 6)

            overflow(pool, over_rows)

        @block.scalar
        def _(act):
            for k in range(KT):
                act.wait_ge(x_turned, k + 1)
                act.activation(xT_hi[:, k, :], psum[k][:, :], ACT.Copy).then_inc(xT_hi_ready, 1)

            def split_hi(c):
                act.wait_ge(raw_in[c % 2], 16 * (c // 2 + 1))
                if c >= HL:
                    act.wait_ge(chunk_used, c - HL + 1)
                act.activation(w_hi[c % HL][:, :], raw[c % 2][:, :], ACT.Copy).then_inc(w_hi_ready, 1)

            def evacuate(c, func, dst):
                for n in range(2):
                    act.wait_ge(projected, 2 * c + n + 1)
                    act.activation(dst[2 * (c % 2) + n], psum[(2 * c + n) % 4][:, :], func).then_inc(act_evacuated, 1)

            def y_split_hi(k, src):
                act.wait_ge(y_ready, k + 1)
                act.activation(y_hi[k][:, :], src, ACT.Copy).then_inc(y_hi_ready, 1)

            split_hi(0)
            split_hi(1)
            act.wait_ge(par_ready, 1)
            act.activation(sp[:, 0, :], par[:, :, P_LAM], ACT.Abs).then_inc(lam_abs, 1)
            act.wait_ge(lam_abs, 1)
            act.activation(sp[:, 1, :], sp[:, 0, :], ACT.Exp, scale=-1.0).then_inc(lam_exp, 1)
            pad_dst = [t[:, PAD:PAD + T] for t in rg_pad]
            for s in range(N_CHUNKS - 2):
                split_hi(s + 2)
                if s in (1, 2):
                    evacuate(s - 1, ACT.Copy, pad_dst)
                if s in (3, 4):
                    evacuate(s - 1, ACT.Gelu_apprx_tanh, [gelu_g[:, j, :] for j in range(CT)])
                if s == 4:
                    for j in range(CT):
                        act.wait_ge(gates_summed, j + 1)
                        act.activation(gr[j][:, :], psum[4 + 2 * (j % 2)][:, :], ACT.Sigmoid, bias=par[:, j, P_AB:P_AB + 1]).then_inc(gates_ready, 1)
                        act.activation(gi[j][:, :], psum[5 + 2 * (j % 2)][:, :], ACT.Sigmoid, bias=par[:, j, P_XB:P_XB + 1]).then_inc(gates_ready, 1)
                if s == 6:
                    for j in range(CT):
                        act.wait_ge(drive_sq, j + 1)
                        act.activation(conv[j][:, 0:T], conv[j][:, 0:T], ACT.Sqrt).then_inc(drive_root, 1)
                if s in (5, 6):
                    act.wait_ge(xc_ready, CT)
                    evacuate(s - 1, ACT.Copy, [t[:, :] for t in sc_c])
                if s == 5:
                    act.wait_ge(c8_ready, 1)
                    for j in range(CT):
                        act.wait_ge(gates_ready, 2 * j + 1)
                        act.activation(th[j], gr[j][:, :], ACT.Tanh, scale=nc8[:, j:j + 1]).then_inc(act_chain, 1)
                        act.wait_ge(act_chain, j + 1)
                        act.activation(gr[j][:, :], gr[j][:, :], ACT.Exp, scale=c8[:, j:j + 1]).then_inc(decay_in, 1)
                if s == 7:
                    for j in range(CT):
                        y_split_hi(j, th[j])
                if s == 10:
                    for j in range(CT):
                        y_split_hi(CT + j, y_sc[j][:, :])
            def copy_h1T(t):
                for n in range(2):
                    act.wait_ge(h1_turned, 2 * t + n + 1)
                    if t >= 2:
                        act.wait_ge(logits_summed, t - 1)
                    act.activation(h1T[t % 2][:, 4 * n:4 * n + 4, :], psum[4 + 2 * (t % 2) + n][:, :], ACT.Copy).then_inc(h1T_ready, 1)

            for t in range(TT):
                act.wait_ge(var_ready, t + 1)
                act.activation(rstd[:, t:t + 1], rstd[:, t:t + 1], ACT.Sqrt).then_inc(dev_ready, 1)
                act.wait_ge(moments_ready, t + 1)
                act.activation(xres[:, t, :], xres[:, t, :], ACT.Identity, bias=shift[:, t:t + 1], scale=rstd[:, t:t + 1]).then_inc(normed, 1)
                if t >= 1:
                    copy_h1T(t - 1)
            copy_h1T(TT - 1)
            act.wait_ge(gdiff_ready, 2)
            act.activation(gexp[:, :, :], gexp[:, :, :], ACT.Exp).then_inc(gexp_ready, 1)
            act.activation(vexp[:, :], vdiff[:, :], ACT.Exp).then_inc(gexp_ready, 1)
            act.wait_ge(h1_stored, 16 * TT)
            for t in range(TT):
                act.activation(xres[:, t, :], xres[:, t, :], ACT.Copy, scale=ALPHA).then_inc(h1_scaled, 1)

            def gate(i, b, lag):
                act.wait_ge(gu_summed, i + 1)
                wait_free(act, hid_ready, i, lag)
                act.activation(gated[b][:, :], psum[2 + b][0:BLOCK, 0:F], ACT.Silu).then_inc(gated_ready, 1)

            def copy_y(i, b, lag, j=None):
                act.wait_ge(dn_summed, i + 1)
                if lag == 1:
                    act.wait_ge(y_scattered[b], 16 * j + 16 * (N_EXP // 2))
                elif not static(i) or i >= lag:
                    act.wait_ge(y_scattered[b], per_pair(i, b))
                act.activation(ys[b][:, :], psum[6 + b][:, :], ACT.Copy).then_inc(y_copied, 1)

            def act_item(i, u, r):
                gate(i, u % 2, 2)
                if not static(i) or i >= 1:
                    copy_y(i - 1, (u + 1) % 2, 2)

            rounds(act, act_item)
            copy_y(N_EXP - 1, (N_EXP - 1) % 2, 2)

            def act_over(j):
                gate(j + N_EXP, 0, 1)
                copy_y(j + N_EXP, 0, 1, j)

            overflow(act, act_over)
            for t in range(TT):
                act.wait_ge(var2_ready, t + 1)
                act.activation(rstd[:, t:t + 1], rstd[:, t:t + 1], ACT.Sqrt).then_inc(dev2_ready, 1)
                act.wait_ge(moments2_ready, t + 1)
                act.activation(pair_y[t][1][:, :], pair_y[t][1][:, :], ACT.Identity, bias=shift[:, t:t + 1], scale=rstd[:, t:t + 1]).then_inc(normed2, 1)

        @block.tensor
        def _(pe):
            pe.wait_ge(ident_done, 2)
            pe.wait_ge(params_in, 16 * 6)
            for j in range(CT):
                mm = pe.transpose(psum[7][:, j * PARAMS:(j + 1) * PARAMS], par_rows[:, j * P:(j + 1) * P], ident[0:PARAMS, 0:PARAMS])
            mm.then_inc(par_turned, 1)
            for k in range(KT):
                if k == 7:
                    pe.wait_ge(par_ready, 1)
                for t in range(TT):
                    if k == 0:
                        pe.wait_ge(x_in[t], 16)
                    mm = pe.transpose(psum[k][:, t * P:(t + 1) * P], xres[:, t, k * P:(k + 1) * P], ident[:, :])
                mm.then_inc(x_turned, 1)

            def products(dst, a_hi, a_lo, b_hi, b_lo, start, stop):
                pe.matmul(dst, a_hi, b_hi, start=start, stop=False)
                pe.matmul(dst, a_hi, b_lo, start=False, stop=False)
                return pe.matmul(dst, a_lo, b_hi, start=False, stop=stop)

            for c in range(N_IN):
                hi, lo = (w[c % HL][:, :].rearrange("p (k n) -> p k n", k=KT) for w in (w_hi, w_lo))
                pe.wait_ge(w_hi_ready, c + 1)
                pe.wait_ge(w_lo_ready, c + 1)
                for n in range(2):
                    if c < 2:
                        pe.wait_ge(xT_lo_ready, 2 * c + n + 1)
                    elif c < 8:
                        pe.wait_ge(act_evacuated, 2 * (c - 2) + n + 1)
                    else:
                        pe.wait_ge(dve_evacuated, 2 * (c - 8) + n + 1)
                    bank = psum[(2 * c + n) % 4]
                    for k in range(KT):
                        if c == 0 and n == 0:
                            pe.wait_ge(xT_hi_ready, k + 1)
                            pe.wait_ge(xT_lo_ready, k + 1)
                        mm = products(bank[:, :], hi[:, k, n * P:(n + 1) * P], lo[:, k, n * P:(n + 1) * P],
                                      xT_hi[:, k, :], xT_lo[:, k, :], k == 0, k == KT - 1)
                    mm.then_inc(projected, 1)
                pe.wait_ge(projected, 2 * c + 2)
                pe.nop().then_inc(chunk_used, 1)
                if c == 3:
                    pe.wait_ge(gates_in, 32)
                    for j in range(CT):
                        pe.wait_ge(xc_ready, j + 1)
                        if j >= 2:
                            pe.wait_ge(gates_ready, 2 * (j - 2) + 2)
                        for w, bank in ((wga, psum[4 + 2 * (j % 2)]), (wgx, psum[5 + 2 * (j % 2)])):
                            for q in range(2):
                                h = slice(64 * q, 64 * q + 64)
                                mm = pe.matmul(bank[h, :], w[h, j, :], conv[j][h, :], start=True, stop=True)
                        mm.then_inc(gates_summed, 1)

            def out_products(c, t, first, last):
                hi, lo = (w[c % HL][:, :].rearrange("p (k n) -> p k n", k=4) for w in (w_hi, w_lo))
                kh = (c - N_IN) % 2
                bank = psum[(4 if c - N_IN < 2 else 0) + t]
                for k in range(4):
                    y = slice(t * P, (t + 1) * P)
                    mm = products(bank[:, :], y_hi[4 * kh + k][:, y], y_lo[4 * kh + k][:, y], hi[:, k, :], lo[:, k, :],
                                  first and k == 0, last and k == 3)
                return mm

            for c in (N_IN, N_IN + 1):
                pe.wait_ge(w_hi_ready, c + 1)
                pe.wait_ge(w_lo_ready, c + 1)
                kh = (c - N_IN) % 2
                pe.wait_ge(y_hi_ready, CT * (kh + 1))
                pe.wait_ge(y_lo_ready, CT * (kh + 1))
                for t in range(TT):
                    mm = out_products(c, t, kh == 0, kh == 1)
                    if kh == 1:
                        mm.then_inc(mixed, 1)
                    elif t == TT - 1:
                        mm.then_inc(chunk_used, 1)
            pe.wait_ge(mixed, TT)
            pe.nop().then_inc(chunk_used, 1)
            for c in (N_IN + 2, N_IN + 3):
                pe.wait_ge(w_hi_ready, c + 1)
                pe.wait_ge(w_lo_ready, c + 1)

            def turn_h1(t):
                pe.wait_ge(h1_ready, t + 1)
                if t >= 2:
                    pe.wait_ge(h1T_ready, 2 * (t - 1))
                for n in range(2):
                    for k in range(4):
                        mm = pe.transpose(psum[4 + 2 * (t % 2) + n][:, k * P:(k + 1) * P], xres[:, t, (4 * n + k) * P:(4 * n + k + 1) * P], ident[:, :])
                    mm.then_inc(h1_turned, 1)

            def router(t):
                if t == 0:
                    pe.wait_ge(router_in, 16 * 4)
                pe.wait_ge(h1T_ready, 2 * t + 2)
                for k in range(KT):
                    mm = pe.matmul(psum[t][:, 0:NR], h1T[t % 2][:, k, :], wr[:, k, :], start=k == 0, stop=k == KT - 1)
                mm.then_inc(logits_summed, 1)

            for t in range(TT):
                out_products(N_IN + 2, t, True, False)
                out_products(N_IN + 3, t, False, True).then_inc(mixed, 1)
                if t >= 2:
                    turn_h1(t - 2)
                if t >= 3:
                    router(t - 3)
            turn_h1(TT - 2)
            router(TT - 3)
            turn_h1(TT - 1)
            router(TT - 2)
            router(TT - 1)

            pe.wait_ge(chosen_ready, 1)
            for t in range(TT + 1):
                dst = psum[0][:, t * N_EXP:(t + 1) * N_EXP]
                for q in range(min(t, TT)):
                    mm = pe.matmul(dst, ones[:, :], chosen_b[:, q, :], start=q == 0, stop=t == TT and q == TT - 1)
                if t < TT:
                    mm = pe.matmul(dst, tri[:, :], chosen_b[:, t, :], start=t == 0, stop=True)
            mm.then_inc(counted, 1)
            pe.wait_ge(hot_ready, 2)
            for n in range(TOP_K * TT):
                mm = pe.matmul(psum[1][:, 0:ITEMS], hot_slot[:, n, :], hot_item[:, n, :], start=n == 0, stop=n == TOP_K * TT - 1)
            mm.then_inc(table_summed, 1)

            def turn_x(i, b, lag, j=None):
                pe.wait_ge(x_gathered[b], 16 * j + 16 * (N_EXP // 2 + 1) if lag == 1 else per_pair(i, b) + 16)
                wait_free(pe, xTg_ready, i, lag)
                for j in range(4):
                    rows = xg[b][:, :].rearrange("p (m j) -> p j m", j=4)[:, j, :]
                    mm = pe.transpose(psum[b][:, j * P:(j + 1) * P], rows, ident[:, :])
                mm.then_inc(xg_turned, 1)

            def gate_up(i, s, b, lag, loads):
                pe.wait_ge(gu_in[s], 32 * loads)
                pe.wait_ge(xTg_ready, i + 1)
                wait_free(pe, hid_ready, i, lag)
                for k in range(KT):
                    h, j = divmod(k, 4)
                    for which in range(2):
                        mm = pe.matmul(psum[2 + b][BLOCK * which:BLOCK * which + BLOCK, 0:F],
                                       xTg[b][:, j, h * BLOCK:(h + 1) * BLOCK], wgu[s][:, which, k, :],
                                       start=k == 0, stop=k == KT - 1)
                mm.then_inc(gu_summed, 1)

            def turn_hid(i, b, lag):
                pe.wait_ge(hid_ready, i + 1)
                wait_free(pe, hidT_ready, i, lag)
                for j in range(2):
                    cols = hid[b][:, :].rearrange("p (m j) -> p j m", j=2)[:, j, :]
                    mm = pe.transpose(psum[4 + b][:, j * P:(j + 1) * P], cols, ident[:, :])
                mm.then_inc(hid_turned, 1)

            def down(i, s, b, lag, loads):
                pe.wait_ge(dn_in[s], 16 * loads)
                pe.wait_ge(hidT_ready, i + 1)
                wait_free(pe, y_copied, i, lag)
                for j in range(2):
                    for n in range(2):
                        mm = pe.matmul(psum[6 + b][BLOCK * n:BLOCK * n + BLOCK, :], hidT[b][:, j, :],
                                       wdn[s][:, j, n * H:(n + 1) * H], start=j == 0, stop=j == 1)
                mm.then_inc(dn_summed, 1)

            def pe_item(i, u, r):
                if not static(i) or i + 1 < N_EXP:
                    turn_x(i + 1, (u + 1) % 2, 2)
                gate_up(i, u, u % 2, 2, r + 1)
                if not static(i) or i >= 1:
                    down(i - 1, (u - 1) % RING, (u + 1) % 2, 2, r + 1 if u else r)
                turn_hid(i, u % 2, 2)

            turn_x(0, 0, 2)
            rounds(pe, pe_item)
            down(N_EXP - 1, (N_EXP - 1) % RING, (N_EXP - 1) % 2, 2, N_EXP // RING + 1)

            def pe_over(j):
                i, loads = j + N_EXP, j + (N_EXP // RING + 2)
                turn_x(i, 0, 1, j)
                gate_up(i, 0, 0, 1, loads)
                turn_hid(i, 0, 1)
                down(i, 0, 0, 1, loads)

            overflow(pe, pe_over)

        @block.vector
        def _(dve_):
            v = dve_
            chain = [0]

            def link(ins):
                chain[0] += 1
                ins.then_inc(dve, 1)
                v.wait_ge(dve, chain[0])

            v.wait_ge(par_turned, 1)
            v.tensor_copy(par[:, :, :], psum[7][:, 0:CT * PARAMS].rearrange("p (j n) -> p j n", j=CT)).then_inc(par_ready, 1)
            v.wait_ge(par_ready, 1)
            lam = par[:, :, P_LAM]
            for k in range(KT):
                v.wait_ge(xT_hi_ready, k + 1)
                v.tensor_tensor(xT_lo[:, k, :], psum[k][:, :], xT_hi[:, k, :], ALU.subtract).then_inc(xT_lo_ready, 1)

            def split_lo(c):
                v.wait_ge(w_hi_ready, c + 1)
                v.tensor_tensor(w_lo[c % HL][:, :], raw[c % 2][:, :], w_hi[c % HL][:, :], ALU.subtract).then_inc(w_lo_ready, 1)

            split_lo(0)
            split_lo(1)

            v.wait_ge(lam_exp, 1)
            e, q, q2, ser, tmp = sp[:, 1, :], sp[:, 2, :], sp[:, 3, :], sp[:, 4, :], sp[:, 5, :]
            link(v.tensor_scalar(tmp, e, 2.0, None, ALU.add))
            link(v.reciprocal(tmp, tmp))
            link(v.tensor_tensor(q, e, tmp, ALU.mult))
            link(v.tensor_tensor(q2, q, q, ALU.mult))
            link(v.tensor_scalar(ser, q2, 1.0 / (2 * LOG_TERMS + 1), None, ALU.mult))
            for n in range(LOG_TERMS - 1, 0, -1):
                link(v.scalar_tensor_tensor(out=ser, in0=ser, scalar=1.0 / (2 * n + 1), in1=q2, op0=ALU.add, op1=ALU.mult))
            link(v.scalar_tensor_tensor(out=ser, in0=ser, scalar=1.0, in1=q, op0=ALU.add, op1=ALU.mult))
            link(v.tensor_scalar(tmp, lam, -1.0, 0.0, ALU.mult, ALU.max))
            link(v.scalar_tensor_tensor(out=tmp, in0=ser, scalar=2.0, in1=tmp, op0=ALU.mult, op1=ALU.add))
            link(v.tensor_scalar(nc8[:, :], tmp, RG_C, None, ALU.mult))
            v.tensor_scalar(c8[:, :], tmp, -RG_C, None, ALU.mult).then_inc(c8_ready, 1)

            def taps(dst, src, j, first, n, bias, done=None):
                w = lambda i: par[:, j, first + i:first + i + 1]
                if bias is None:
                    link(v.tensor_scalar(dst, src(n - 1), w(n - 1), None, ALU.mult))
                else:
                    link(v.tensor_scalar(dst, src(n - 1), w(n - 1), bias, ALU.mult, ALU.add))
                for i in range(n - 1):
                    ins = v.scalar_tensor_tensor(out=dst, in0=src(i), scalar=w(i), in1=dst, op0=ALU.mult, op1=ALU.add)
                    if i == n - 2 and done is not None:
                        ins.then_inc(done, 1)
                    else:
                        link(ins)

            def rg_conv(j):
                v.wait_ge(act_evacuated, j + 1)
                v.wait_ge(pads_zero, j + 1)
                taps(conv[j][:, 0:T], lambda i: rg_pad[j][:, i:i + T], j, P_RGW, RG_TAPS, par[:, j, P_RGB:P_RGB + 1], xc_ready)

            def drive(j):
                a, u, m = gr[j][:, :], gi[j][:, :], conv[j][:, 0:T]
                v.wait_ge(decay_in, j + 1)
                link(v.tensor_tensor(u, u, m, ALU.mult))
                link(v.tensor_tensor(m, a, a, ALU.mult))
                v.scalar_tensor_tensor(out=m, in0=m, scalar=1.0, in1=th[j], op0=ALU.add, op1=ALU.mult).then_inc(drive_sq, 1)

            def recurrence(j):
                a, u, m = gr[j][:, :], gi[j][:, :], conv[j][:, 0:T]
                v.wait_ge(drive_root, j + 1)
                link(v.tensor_tensor(u, u, m, ALU.mult))
                link(v.tensor_tensor_scan(m, a, u, 0.0, ALU.mult, ALU.add))
                v.tensor_tensor(th[j], m, gelu_g[:, j, :], ALU.mult).then_inc(y_ready, 1)

            def short_conv(j):
                v.wait_ge(projected, 12 + j + 1)
                v.wait_ge(act_evacuated, 8 + j + 1)
                v.wait_ge(pads_zero, CT + j + 1)
                v.tensor_tensor(sc_pad[j][:, SC_TAPS - 1:SC_TAPS - 1 + T], psum[j % 4][:, :], sc_c[j][:, :], ALU.mult).then_inc(dve_evacuated, 1)
                v.wait_ge(dve_evacuated, j + 1)
                taps(sc_conv[j][:, :], lambda i: sc_pad[j][:, i:i + T], j, P_SCW, SC_TAPS, None)

            def y_short(j):
                v.wait_ge(projected, 16 + j + 1)
                v.tensor_tensor(y_sc[j][:, :], psum[j % 4][:, :], sc_conv[j][:, :], ALU.mult).then_inc(y_ready, 1)

            def y_split_lo(k, src):
                v.wait_ge(y_hi_ready, k + 1)
                v.tensor_tensor(y_lo[k][:, :], src, y_hi[k][:, :], ALU.subtract).then_inc(y_lo_ready, 1)

            for s in range(N_CHUNKS - 2):
                split_lo(s + 2)
                if s in (1, 2):
                    rg_conv(2 * s - 2)
                    rg_conv(2 * s - 1)
                if s == 5:
                    for j in range(CT):
                        drive(j)
                if s == 6:
                    for j in range(CT):
                        recurrence(j)
                if s == 7:
                    for j in range(CT):
                        y_split_lo(j, th[j])
                if s in (7, 8):
                    short_conv(2 * s - 14)
                    short_conv(2 * s - 13)
                if s in (9, 10):
                    y_short(2 * s - 18)
                    y_short(2 * s - 17)
                if s == 10:
                    for j in range(CT):
                        y_split_lo(CT + j, y_sc[j][:, :])

            def residual(n):
                h, t = divmod(n, TT)
                part = xres[:, t, h * H:(h + 1) * H]
                v.wait_ge(mixed, n + 1)
                link(v.scalar_tensor_tensor(out=part, in0=part, scalar=ALPHA, in1=psum[(4, 0)[h] + t][:, :], op0=ALU.mult, op1=ALU.add))
                link(v.bn_stats(stats[:, t, h, :], part))

            def finish_moments(t, var_done, dev_done, done):
                link(v.bn_aggr(moments[:, t, :], stats[:, t, :, :]))
                v.tensor_scalar(rstd[:, t:t + 1], moments[:, t, 1:2], LN_EPS, None, ALU.add).then_inc(var_done, 1)
                v.wait_ge(dev_done, t + 1)
                link(v.reciprocal(rstd[:, t:t + 1], rstd[:, t:t + 1]))
                v.scalar_tensor_tensor(out=shift[:, t:t + 1], in0=moments[:, t, 0:1], scalar=-1.0, in1=rstd[:, t:t + 1],
                                       op0=ALU.mult, op1=ALU.mult).then_inc(done, 1)

            def take_logits(t):
                v.wait_ge(logits_summed, t + 1)
                v.tensor_tensor(logits[:, t, :], psum[t][:, 0:NR], rbias[:, :], ALU.add).then_inc(routed, 1)

            for t in range(TT):
                residual(t)
            v.wait_ge(ln1_in, 32)
            for t in range(TT):
                residual(TT + t)
                finish_moments(t, var_ready, dev_ready, moments_ready)
                v.wait_ge(normed, t + 1)
                link(v.tensor_tensor(xres[:, t, :], xres[:, t, :], ln_g[:, :], ALU.mult))
                v.tensor_tensor(xres[:, t, :], xres[:, t, :], ln_b[:, :], ALU.add).then_inc(h1_ready, 1)
                if t == 0:
                    v.wait_ge(router_in, 16 * 4)
                if t == TT - 1:
                    take_logits(0)
            for t in range(1, TT):
                take_logits(t)
            v.wait_ge(routed, TT)

            v.wait_ge(const_done, 1)
            g_logits = logits[:, :, 0:N_GROUPS]
            e_logits = logits[:, :, N_GROUPS:NR]
            over_n = lambda ap, n: ap.unsqueeze(2).to_broadcast([P, ap.shape[1], n])
            down_of = lambda key, n: key.unsqueeze(1).to_broadcast([P, TT, n])

            def first_max(values, top, key, key_top, hot, key_down, n):
                link(v.tensor_reduce(top, values, AX, ALU.max))
                link(v.tensor_tensor(key, values, over_n(top, n), ALU.is_equal))
                link(v.tensor_tensor(key, key, down_of(key_down, n), ALU.mult))
                link(v.tensor_reduce(key_top, key, AX, ALU.max))
                link(v.tensor_tensor(hot, key, over_n(key_top, n), ALU.is_equal))

            first_max(g_logits, gmax[:, :], gkey[:, :, :], gkmax[:, :], ghot[:, :, :], down4, N_GROUPS)
            link(v.tensor_scalar(gkey[:, :, :], ghot[:, :, :], -1.0, FAR, ALU.add, ALU.mult))
            pushed = gkey[:, :, :].unsqueeze(3).to_broadcast([P, TT, N_GROUPS, PER_GROUP])
            link(v.tensor_tensor(masked[:, :, :].rearrange("p t (g n) -> p t g n", g=N_GROUPS),
                                 e_logits.rearrange("p t (g n) -> p t g n", g=N_GROUPS), pushed, ALU.add))
            first_max(masked[:, :, :], vtop[:, 0, :], ekey[:, :, :], kkey[:, 0, :], chosen[:, 0, :, :], down32, N_EXP)
            link(v.scalar_tensor_tensor(out=masked2[:, :, :], in0=chosen[:, 0, :, :], scalar=-3.0 * FAR, in1=masked[:, :, :], op0=ALU.mult, op1=ALU.add))
            first_max(masked2[:, :, :], vtop[:, 1, :], ekey[:, :, :], kkey[:, 1, :], chosen[:, 1, :, :], down32, N_EXP)
            v.tensor_tensor(chosen_b[:, :, :], chosen[:, 0, :, :], chosen[:, 1, :, :], ALU.add).then_inc(chosen_ready, 1)
            v.tensor_tensor(gexp[:, :, :], g_logits, over_n(gmax[:, :], N_GROUPS), ALU.subtract).then_inc(gdiff_ready, 1)
            v.tensor_tensor(vdiff[:, :], vtop[:, 1, :], vtop[:, 0, :], ALU.subtract).then_inc(gdiff_ready, 1)
            link(v.tensor_scalar(expert[:, :], kkey[:, :, :].rearrange("p k t -> p (k t)"), -1.0, float(N_EXP), ALU.mult, ALU.add))

            v.wait_ge(counted, 1)
            counts = psum[0][:, 0:TT * N_EXP].rearrange("p (t e) -> p t e", t=TT)
            for k in range(TOP_K):
                link(v.tensor_tensor(prod[:, k, :, :], counts, chosen[:, k, :, :], ALU.mult))
            link(v.tensor_reduce(rank[:, :], prod[:, :, :, :].rearrange("p k t e -> p (k t) e"), AX, ALU.add))
            down_half = (BLOCK - 1) / (2.0 * BLOCK)
            link(v.tensor_scalar(blk[:, :], rank[:, :], 1.0 / BLOCK, -down_half, ALU.mult, ALU.add))
            link(v.tensor_scalar(blk[:, :], blk[:, :], RNE, -RNE, ALU.add, ALU.add))
            link(v.tensor_scalar(extra[:, :], psum[0][:, TT * N_EXP:(TT + 1) * N_EXP], 1.0 / BLOCK, -1.0 / BLOCK - down_half, ALU.mult, ALU.add))
            link(v.tensor_scalar(extra[:, :], extra[:, :], RNE, -RNE, ALU.add, ALU.add))
            link(v.tensor_scalar(extra[:, :], extra[:, :], 0.0, None, ALU.max))
            link(v.tensor_tensor_scan(extra_sum[:, :], extra[:, :], zeros[:, :], 0.0, ALU.add, ALU.add))
            link(v.tensor_tensor(extra_base[:, :], extra_sum[:, :], extra[:, :], ALU.subtract))
            base_of = extra_base[:, :].unsqueeze(1).to_broadcast([P, TT, N_EXP])
            for k in range(TOP_K):
                link(v.tensor_tensor(prod[:, k, :, :], chosen[:, k, :, :], base_of, ALU.mult))
            link(v.tensor_reduce(obase[:, :], prod[:, :, :, :].rearrange("p k t e -> p (k t) e"), AX, ALU.add))
            link(v.tensor_scalar(over[:, :], blk[:, :], 1.0, None, ALU.min))
            link(v.tensor_tensor(item[:, :], obase[:, :], blk[:, :], ALU.add))
            link(v.scalar_tensor_tensor(out=item[:, :], in0=item[:, :], scalar=N_EXP - 1.0, in1=expert[:, :], op0=ALU.add, op1=ALU.subtract))
            link(v.tensor_tensor(item[:, :], item[:, :], over[:, :], ALU.mult))
            link(v.tensor_tensor(item[:, :], item[:, :], expert[:, :], ALU.add))
            link(v.scalar_tensor_tensor(out=slot[:, :], in0=blk[:, :], scalar=-float(BLOCK), in1=rank[:, :], op0=ALU.mult, op1=ALU.add))
            NP = TOP_K * TT
            v.tensor_tensor(hot_slot[:, :, :].rearrange("p n (h s) -> p n h s", h=2),
                            up_slot.unsqueeze(1).unsqueeze(1).to_broadcast([P, NP, 2, BLOCK]),
                            slot[:, :].unsqueeze(2).unsqueeze(3).to_broadcast([P, NP, 2, BLOCK]), ALU.is_equal).then_inc(hot_ready, 1)
            link(v.tensor_tensor(hot_item[:, :, :], up_item.unsqueeze(1).to_broadcast([P, NP, ITEMS]),
                                 item[:, :].unsqueeze(2).to_broadcast([P, NP, ITEMS]), ALU.is_equal))
            v.tensor_tensor(hot_item[:, :, :], hot_item[:, :, :], pair1.unsqueeze(2).to_broadcast([P, NP, ITEMS]), ALU.mult).then_inc(hot_ready, 1)
            link(v.tensor_copy(n_over[:, :], extra_sum[0:1, N_EXP - 1:N_EXP]))
            link(v.tensor_tensor(over_cmp[:, :, :], extra_sum[0:1, :].unsqueeze(1).to_broadcast([1, MAX_OVER, N_EXP]),
                                 up_slot[0:1, 0:MAX_OVER].unsqueeze(2).to_broadcast([1, MAX_OVER, N_EXP]), ALU.is_le))
            link(v.tensor_reduce(over_exp[:, :], over_cmp[:, :, :], AX, ALU.add))
            link(v.tensor_copy(over_exp_i[:, :], over_exp[:, :]))
            v.wait_ge(table_summed, 1)
            link(v.tensor_scalar(table[:, :], psum[1][:, 0:ITEMS], -1.0, half, ALU.add, ALU.add))
            link(v.tensor_scalar(empty[:, :], psum[1][:, 0:ITEMS], 0.0, NO_ROW, ALU.is_equal, ALU.mult))
            link(v.tensor_tensor(table[:, :], table[:, :], empty[:, :], ALU.add))
            link(v.tensor_scalar(table_x[:, :], table[:, :], 2.0 * T, -2.0 * T, ALU.is_ge, ALU.mult))
            link(v.tensor_tensor(x_rows[:, :], table_x[:, :], table[:, :], ALU.add))
            v.tensor_copy(y_rows[:, :], table[:, :]).then_inc(rows_ready, 1)

            v.wait_ge(gexp_ready, 2)
            link(v.tensor_reduce(gsum[:, :], gexp[:, :, :], AX, ALU.add))
            link(v.tensor_scalar(wsum[:, :], vexp[:, :], 1.0, None, ALU.add))
            link(v.tensor_tensor(wsum[:, :], wsum[:, :], gsum[:, :], ALU.mult))
            link(v.reciprocal(weight[:, 0, :], wsum[:, :]))
            link(v.tensor_tensor(weight[:, 1, :], weight[:, 0, :], vexp[:, :], ALU.mult))

            def copy_xT(i, b, lag):
                v.wait_ge(xg_turned, i + 1)
                wait_free(v, gu_summed, i, lag)
                v.tensor_copy(xTg[b][:, :, :], psum[b][:, :].rearrange("p (j m) -> p j m", j=4)).then_inc(xTg_ready, 1)

            def make_hid(i, b, lag):
                v.wait_ge(gated_ready, i + 1)
                wait_free(v, hid_turned, i, lag)
                v.tensor_tensor(hid[b][0:BLOCK, :], gated[b][:, :], psum[2 + b][BLOCK:2 * BLOCK, 0:F], ALU.mult).then_inc(hid_ready, 1)

            def copy_hidT(i, b, lag):
                v.wait_ge(hid_turned, i + 1)
                wait_free(v, dn_summed, i, lag)
                v.tensor_copy(hidT[b][:, :, :], psum[4 + b][:, 0:2 * P].rearrange("p (j m) -> p j m", j=2)[:, :, 0:BLOCK]).then_inc(hidT_ready, 1)

            def dve_item(i, u, r):
                if not static(i) or i + 1 < N_EXP:
                    copy_xT(i + 1, (u + 1) % 2, 2)
                make_hid(i, u % 2, 2)
                copy_hidT(i, u % 2, 2)

            v.wait_ge(hid_zero, 2)
            copy_xT(0, 0, 2)
            rounds(v, dve_item)

            def dve_over(j):
                i = j + N_EXP
                copy_xT(i, 0, 1)
                make_hid(i, 0, 1)
                copy_hidT(i, 0, 1)

            overflow(v, dve_over)

            v.wait_ge(ln2_in, 32)
            v.wait_ge(h1_scaled, TT)

            def combine(t):
                z0, z = pair_y[t][0], pair_y[t][1]
                v.wait_ge(pairs_in[t], 32)
                link(v.scalar_tensor_tensor(out=z0[:, :], in0=z0[:, :], scalar=weight[:, 0, t:t + 1], in1=xres[:, t, :], op0=ALU.mult, op1=ALU.add))
                link(v.scalar_tensor_tensor(out=z[:, :], in0=z[:, :], scalar=weight[:, 1, t:t + 1], in1=z0[:, :], op0=ALU.mult, op1=ALU.add))
                for h in range(2):
                    link(v.bn_stats(stats[:, t, h, :], z[:, h * H:(h + 1) * H]))
                finish_moments(t, var2_ready, dev2_ready, moments2_ready)

            def scale_out(t):
                z = pair_y[t][1]
                v.wait_ge(normed2, t + 1)
                link(v.tensor_tensor(z[:, :], z[:, :], ln_g[:, :], ALU.mult))
                v.tensor_tensor(z[:, :], z[:, :], ln_b[:, :], ALU.add).then_inc(out_ready, 1)

            for t in range(TT):
                combine(t)
                if t >= 1:
                    scale_out(t - 1)
            scale_out(TT - 1)


_INS = ["x", "w_in", "rg_conv_w", "rg_conv_b", "rg_gate_a_w", "rg_gate_a_b", "rg_gate_x_w", "rg_gate_x_b",
        "rg_lambda", "sc_conv_w", "w_out", "ln1_g", "ln1_b", "router_group_w", "router_group_b",
        "router_expert_w", "router_expert_b", "exp_w_gate", "exp_w_up", "exp_w_down", "ln2_g", "ln2_b"]


def kernel(**inputs):
    import numpy as _np
    import concourse.bacc as _bacc
    from concourse import mybir as _mybir
    from concourse.bass_utils import run_bass_kernel_spmd as _run

    nc = _bacc.Bacc("TRN2", target_bir_lowering=False, num_devices=1)
    arrays, args = {}, []
    for name in _INS:
        a = _np.ascontiguousarray(inputs[name])
        arrays[f"in_{name}"] = a
        args.append(nc.dram_tensor(f"in_{name}", a.shape, _mybir.dt.from_np(a.dtype), kind="ExternalInput").ap())
    shape = tuple(inputs["x"].shape)
    args.append(nc.dram_tensor("out_0", shape, _mybir.dt.float32, kind="ExternalOutput").ap())
    hybrid_moe_layer(nc, *args)
    r = _run(nc, [arrays], core_ids=[0])
    return r.results[0]["out_0"]
```

```python
from contextlib import ExitStack

import concourse.bass as bass
from concourse import mybir

F32 = mybir.dt.float32
F32R = mybir.dt.float32r
BF16 = mybir.dt.bfloat16
U32 = mybir.dt.uint32
I32 = mybir.dt.int32
ALU = mybir.AluOpType
ACT = mybir.ActivationFunctionType
AX = mybir.AxisListType.X

P = 128
BLOCK = 64
RING = 6
FIRST = RING + 1
TOP_K = 2
RG_C = 8.0
LN_EPS = 1e-5
ALPHA = 2.0 ** 0.25
FAR = 1e30
RNE = 12582912.0
NO_ROW = 1048576.0
LOG_TERMS = 9


def hybrid_moe_layer(
    nc, x, w_in, rg_conv_w, rg_conv_b, rg_gate_a_w, rg_gate_a_b, rg_gate_x_w, rg_gate_x_b,
    rg_lambda, sc_conv_w, w_out, ln1_g, ln1_b, router_group_w, router_group_b,
    router_expert_w, router_expert_b, exp_w_gate, exp_w_up, exp_w_down, ln2_g, ln2_b, out,
):
    _, T, D = x.shape
    RG_TAPS, D_RG = rg_conv_w.shape
    SC_TAPS, D_SC = sc_conv_w.shape
    N_GROUPS = router_group_w.shape[1]
    N_EXP, _, F = exp_w_gate.shape
    PER_GROUP = N_EXP // N_GROUPS
    NR = N_GROUPS + N_EXP
    TT = T // P
    KT = D // P
    CT = D_RG // P
    H = D // 2
    CHUNK = 2048
    WCOLS = CHUNK // KT
    N_IN = 5 * D_RG // WCOLS
    N_OUT = D * D // P // CHUNK
    N_CHUNKS = N_IN + N_OUT
    HL = 3
    PER_BLOCK = D_RG // WCOLS
    MAX_OVER = TOP_K * T // BLOCK
    ITEMS = N_EXP + MAX_OVER
    assert T == 512 and D == 1024 and D_RG == D_SC == 512 and F == 256 and N_OUT == 4
    PARAMS = RG_TAPS + 4 + SC_TAPS
    P_RGW, P_RGB, P_AB, P_XB, P_LAM, P_SCW = 0, RG_TAPS, RG_TAPS + 1, RG_TAPS + 2, RG_TAPS + 3, RG_TAPS + 4

    with ExitStack() as ctx:
        base = -(-nc.sbuf_base // 64) * 64
        place = [base]

        def at(name, shape, dt, offset):
            return nc.alloc_sbuf_tensor_at(name, shape, dt, offset=offset)

        def sb(name, shape, dt=F32):
            n = 4 if dt != BF16 else 2
            for s in shape[1:]:
                n *= s
            t = at(name, shape, dt, place[0])
            place[0] += -(-n // 32) * 32
            return t

        ident = sb("ident", [P, P])
        tri = sb("tri", [P, P], BF16)
        ones = sb("ones", [P, P], BF16)
        par = sb("par", [P, CT, PARAMS])
        c8 = sb("c8", [P, CT])
        nc8 = sb("nc8", [P, CT])
        sp = sb("sp", [P, 6, CT])
        wr = sb("wr", [P, KT, NR])
        rbias = sb("rbias", [P, NR])
        stats = sb("stats", [P, TT, 2, 6])
        moments = sb("moments", [P, TT, 2])
        rstd = sb("rstd", [P, TT])
        shift = sb("shift", [P, TT])
        logits = sb("logits", [P, TT, NR])
        gmax = sb("gmax", [P, TT])
        gkey = sb("gkey", [P, TT, N_GROUPS])
        gkmax = sb("gkmax", [P, TT])
        ghot = sb("ghot", [P, TT, N_GROUPS])
        vtop = sb("vtop", [P, TOP_K, TT])
        kkey = sb("kkey", [P, TOP_K, TT])
        chosen_b = sb("chosen_b", [P, TT, N_EXP], BF16)
        rank = sb("rank", [P, TOP_K * TT])
        expert = sb("expert", [P, TOP_K * TT])
        extra = sb("extra", [P, N_EXP])
        extra_sum = sb("extra_sum", [P, N_EXP])
        extra_base = sb("extra_base", [P, N_EXP])
        zeros = sb("zeros", [P, N_EXP])
        obase = sb("obase", [P, TOP_K * TT])
        blk = sb("blk", [P, TOP_K * TT])
        over = sb("over", [P, TOP_K * TT])
        item = sb("item", [P, TOP_K * TT])
        slot = sb("slot", [P, TOP_K * TT])
        x_rows = sb("x_rows", [P, ITEMS], U32)
        y_rows = sb("y_rows", [P, ITEMS], U32)
        x_row_now = sb("x_row_now", [P, 1], U32)
        y_row_now = sb("y_row_now", [P, 1], U32)
        held = sb("held", [P, 1])
        over_exp = sb("over_exp", [1, MAX_OVER])
        over_exp_i = sb("over_exp_i", [1, MAX_OVER], I32)
        n_over = sb("n_over", [1, 1], I32)
        gexp = sb("gexp", [P, TT, N_GROUPS])
        gsum = sb("gsum", [P, TT])
        ptop = sb("ptop", [P, TT])
        vdiff = sb("vdiff", [P, TT])
        vexp = sb("vexp", [P, TT])
        wsum = sb("wsum", [P, TT])
        weight = sb("weight", [P, TOP_K, TT])
        iota_f = sb("iota_f", [P, 160])
        down4, down32 = iota_f[:, 0:N_GROUPS], iota_f[:, 4:4 + N_EXP]
        up_slot = iota_f[:, 36:36 + BLOCK]
        pair1 = iota_f[:, 100:100 + TOP_K * TT]
        half = iota_f[:, 108:109]
        up_item = iota_f[:, 112:160]

        first_place = place[0]
        xres = sb("xres", [P, TT, D])
        ln_g = sb("ln_g", [P, D])
        ln_b = sb("ln_b", [P, D])
        wgu_first = at("wgu_first", [P, 2, KT, F], F32, first_place)
        wdn_first = at("wdn_first", [P, 2, D], F32, first_place + 16384)

        shared = place[0]
        xTg = [sb(f"xTg{b}", [P, 4, P]) for b in range(2)]
        gated = [sb(f"gated{b}", [BLOCK, F]) for b in range(2)]
        hid = [sb(f"hid{b}", [P, F]) for b in range(2)]
        hidT = [sb(f"hidT{b}", [P, 2, BLOCK]) for b in range(2)]
        ys = [sb(f"ys{b}", [P, H]) for b in range(4)]
        gelu_g = at("gelu_g", [P, CT, T], F32, shared)
        h1T = [at(f"h1T{b}", [P, KT, P], F32, shared + 4096 * b) for b in range(2)]
        shared_y = shared + 8192
        assert place[0] - shared_y >= 8192

        ring = place[0]
        SLOT = 24576
        wgu = [at(f"wgu{s}", [P, 2, KT, F], F32, ring + s * SLOT) for s in range(RING)]
        wdn = [at(f"wdn{s}", [P, 2, D], F32, ring + s * SLOT + 16384) for s in range(RING)]
        wgu.append(wgu_first)
        wdn.append(wdn_first)
        spare = ring + RING * SLOT
        assert spare + 16384 <= nc.sbuf_usable_end, (spare, nc.sbuf_usable_end)
        raw = [at(f"raw{b}", [P, CHUNK], F32, spare + 8192 * b) for b in range(2)]

        xT_hi = at("xT_hi", [P, KT, T], F32R, ring)
        xT_lo = at("xT_lo", [P, KT, T], F32R, ring + 16384)
        chan = ring + 32768
        PAD = RG_TAPS - 1
        rg_pad = [at(f"rg_pad{j}", [P, PAD + T], F32, chan + 2080 * j) for j in range(CT)]
        assert 2080 * CT <= 8320
        chan += 8320
        sc_c = [at(f"sc_c{j}", [P, T], F32, chan - 8320 + 2080 * j) for j in range(CT)]
        conv = [at(f"conv{j}", [P, T], F32, chan + 2080 * j) for j in range(CT)]
        sc_pad = [at(f"sc_pad{j}", [P, SC_TAPS - 1 + T], F32, chan + 2080 * j) for j in range(CT)]
        chan += 8320
        gr = [at(f"gr{j}", [P, T], F32, chan + 2048 * j) for j in range(CT)]
        sc_conv = [at(f"sc_conv{j}", [P, T], F32, chan + 2048 * j) for j in range(CT)]
        chan += 8192
        gi = [at(f"gi{j}", [P, T], F32, chan + 2048 * j) for j in range(CT)]
        y_sc = [at(f"y_sc{j}", [P, T], F32, chan + 2048 * j) for j in range(CT)]
        chan += 8192
        tanhs = at("tanhs", [P, 3, T], F32, chan)
        chan += 3 * 2048
        assert chan <= ring + 3 * SLOT
        w_hi = [at(f"w_hi{b}", [P, CHUNK], F32R, ring + (3 + b) * SLOT) for b in range(HL)]
        w_lo = [at(f"w_lo{b}", [P, CHUNK], F32R, ring + (3 + b) * SLOT + 8192) for b in range(HL)]
        y_at = [ring + (3 + s) * SLOT + 16384 + 4096 * h for s in range(3) for h in range(2)] + [shared_y, shared_y + 4096]
        y_hi = [at(f"y_hi{k}", [P, T], F32R, y_at[k]) for k in range(KT)]
        y_lo = [at(f"y_lo{k}", [P, T], F32R, y_at[k] + 2048) for k in range(KT)]

        par_rows = at("par_rows", [PARAMS, D_RG], F32, shared)
        iota_i = at("iota_i", [P, 160], I32, y_at[5])
        tanh3 = at("tanh3", [P, T], F32, y_at[6])
        wga = at("wga", [P, CT, 64], F32, y_at[7])
        wgx = at("wgx", [P, CT, 64], F32, y_at[7] + 2048)
        th = [tanhs[:, j, :] for j in range(3)] + [tanh3[:, :]]

        h1 = at("h1", [P, TT, D], F32, ring + SLOT)
        ln2g = at("ln2g", [P, D], F32, ring + SLOT + 16384)
        ln2b = at("ln2b", [P, D], F32, ring + SLOT + 20480)
        pair_y = [[at(f"pair_y{k}_{t}", [P, D], F32, ring + 2 * SLOT + 4096 * (TOP_K * t + k)) for k in range(TOP_K)] for t in range(TT)]

        xg = [at(f"xg{b}", [P, H], F32, spare + 2048 * b) for b in range(RING)]
        ys += [at(f"ys{b}", [P, H], F32, spare + 2048 * (RING + b - 4)) for b in range(4, RING)]

        assert 4096 + 4 * TOP_K * TT * ITEMS <= RING // 2 * 2048
        hot_slot = at("hot_slot", [P, TOP_K * TT, P], F32, spare)
        hot_item = at("hot_item", [P, TOP_K * TT, ITEMS], F32, spare + 4096)
        over_cmp = at("over_cmp", [1, MAX_OVER, N_EXP], F32, spare + 6144)
        prod = at("prod", [P, TOP_K, TT, N_EXP], F32, spare + 8192)
        chosen = at("chosen", [P, TOP_K, TT, N_EXP], F32, spare + 9216)
        masked = at("masked", [P, TT, N_EXP], F32, spare + 10240)
        masked2 = at("masked2", [P, TT, N_EXP], F32, spare + 10752)
        ekey = at("ekey", [P, TT, N_EXP], F32, spare + 11264)
        table = at("table", [P, ITEMS], F32, spare + 11776)
        table_x = at("table_x", [P, ITEMS], F32, spare + 12032)
        empty = at("empty", [P, ITEMS], F32, spare + 12288)

        h1_rows = nc.dram_tensor("h1_rows", (2 * T, H), F32, kind="Internal").ap()
        y_pairs = nc.dram_tensor("y_pairs", (2 * TOP_K * T, H), F32, kind="Internal").ap()

        psum = [ctx.enter_context(nc.psum_tensor(f"bank{b}", [P, 512], F32)) for b in range(8)]

        def sem(name):
            return ctx.enter_context(nc.semaphore(name))

        params_in = sem("params_in")
        gates_in = sem("gates_in")
        x_in = [sem(f"x_in{h}") for h in range(2)]
        raw_in = [sem(f"raw_in{b}") for b in range(2)]
        ln1_in = sem("ln1_in")
        ln2_in = sem("ln2_in")
        router_in = sem("router_in")
        gu_in = [sem(f"gu_in{s}") for s in range(RING + 1)]
        dn_in = [sem(f"dn_in{s}") for s in range(RING + 1)]
        over_gu_in = sem("over_gu_in")
        over_dn_in = sem("over_dn_in")
        ident_done = sem("ident_done")
        const_pool = sem("const_pool")
        const_done = sem("const_done")
        pads_zero = sem("pads_zero")
        par_turned = sem("par_turned")
        par_ready = sem("par_ready")
        x_turned = sem("x_turned")
        xT_hi_ready = sem("xT_hi_ready")
        xT_lo_ready = sem("xT_lo_ready")
        w_hi_ready = sem("w_hi_ready")
        w_lo_ready = sem("w_lo_ready")
        chunk_used = sem("chunk_used")
        projected = sem("projected")
        act_evacuated = sem("act_evacuated")
        dve_evacuated = sem("dve_evacuated")
        xc_ready = sem("xc_ready")
        gates_summed = sem("gates_summed")
        gates_ready = sem("gates_ready")
        decay_in = sem("decay_in")
        c8_ready = sem("c8_ready")
        lam_abs = sem("lam_abs")
        lam_exp = sem("lam_exp")
        drive_sq = sem("drive_sq")
        drive_root = sem("drive_root")
        y_ready = sem("y_ready")
        y_hi_ready = sem("y_hi_ready")
        y_lo_ready = sem("y_lo_ready")
        mixed = sem("mixed")
        mixed_used = sem("mixed_used")
        var_ready = sem("var_ready")
        dev_ready = sem("dev_ready")
        moments_ready = sem("moments_ready")
        normed = sem("normed")
        h1_ready = sem("h1_ready")
        h1_stored = sem("h1_stored")
        h1_turned = sem("h1_turned")
        h1T_ready = sem("h1T_ready")
        routed = sem("routed")
        logits_summed = sem("logits_summed")
        chosen_ready = sem("chosen_ready")
        counted = sem("counted")
        hot_ready = sem("hot_ready")
        table_summed = sem("table_summed")
        rows_ready = sem("rows_ready")
        gdiff_ready = sem("gdiff_ready")
        gexp_ready = sem("gexp_ready")
        weights_ready = sem("weights_ready")
        dve = sem("dve_chain")
        act_chain = sem("act_chain")
        xg_zero = sem("xg_zero")
        hid_zero = sem("hid_zero")
        x_gathered = [sem(f"x_gathered{b}") for b in range(RING)]
        y_scattered = [sem(f"y_scattered{b}") for b in range(RING)]
        over_x = sem("over_x")
        over_y = sem("over_y")
        xg_turned = sem("xg_turned")
        xTg_ready = sem("xTg_ready")
        gu_summed = sem("gu_summed")
        gated_ready = sem("gated_ready")
        hid_ready = sem("hid_ready")
        hid_turned = sem("hid_turned")
        hidT_ready = sem("hidT_ready")
        dn_summed = sem("dn_summed")
        y_copied = sem("y_copied")
        pool_chain = sem("pool_chain")
        pairs_in = [sem(f"pairs_in{t}") for t in range(TT)]
        h1_in = sem("h1_in")
        first_scaled = sem("first_scaled")
        var2_ready = sem("var2_ready")
        dev2_ready = sem("dev2_ready")
        moments2_ready = sem("moments2_ready")
        normed2 = sem("normed2")
        out_ready = sem("out_ready")
        out_ready_pool = sem("out_ready_pool")
        out_scaled = sem("out_scaled")
        out_stored = sem("out_stored")

        x_rows_dram = x.rearrange("a t d -> (a t) d")
        out_rows = out.rearrange("a t d -> (a t) d")
        row = lambda v: v.rearrange("(a n) -> a n", a=1)

        BLOCK_ORDER = (0, 1, 3, 4, 2)

        def w_in_chunk(c):
            col = BLOCK_ORDER[c // PER_BLOCK] * D_RG + c % PER_BLOCK * WCOLS
            return w_in[:, col:col + WCOLS].rearrange("(k p) n -> p k n", p=P)

        def w_out_chunk(c):
            h, kh = divmod(c - N_IN, 2)
            return w_out[kh * 512:(kh + 1) * 512, h * 512:(h + 1) * 512].rearrange("(k p) n -> p k n", p=P)

        def static(i):
            return isinstance(i, int)

        def gu_of(w, e):
            w = w[e:e + 1] if static(e) else w[bass.ds(e, 1)]
            return w.rearrange("a (h p j) f -> p (a h) (j f)", h=2, p=P)

        def dn_of(e):
            w = exp_w_down[e:e + 1] if static(e) else exp_w_down[bass.ds(e, 1)]
            return w.rearrange("a (p j) d -> p (a j d)", p=P)

        def gu_place(s, which):
            return wgu[s][:, which, :, :].rearrange("p (h j) f -> p h (j f)", h=2)

        def slot_of(q):
            return q if q < FIRST else (q - 1) % RING

        def loads_of(q, r):
            return r + (1 if q < FIRST else (q - 1) // RING + 1)

        def rounds(engine, body):
            head, turns = FIRST + 1, (N_EXP - 1 - (FIRST + 1)) // RING
            for q in range(head):
                body(q, 0)
            with engine.Fori(0, turns) as r:
                for u in range(RING):
                    body(head + u, r)
            for q in range(head + turns * RING, N_EXP):
                body(q, 0)

        def overflow(engine, body):
            n = engine.value_load(n_over[0:1, 0:1], min_val=0, max_val=MAX_OVER)
            with engine.If(n > 0):
                with engine.Fori(0, n) as j:
                    body(j)

        def before(q, r):
            return r * 16 + 16 * (q // RING) if not static(r) else 16 * (r + q // RING)

        def mains(b):
            return 16 * len(range(b, N_EXP, RING))

        def wait_free(eng, done, i, lag):
            if not static(i) or i >= lag:
                eng.wait_ge(done, i + 1 - lag)

        block = ctx.enter_context(nc.Block())

        @block.sync
        def _(sp_):
            def load_x(h):
                sp_.dma_start(xres[:, :, h * H:(h + 1) * H], x_rows_dram[:, h * H:(h + 1) * H].rearrange("(t p) d -> p t d", p=P)).then_inc(x_in[h], 16)

            for c in range(N_CHUNKS):
                if c == 1:
                    load_x(0)
                    load_x(1)
                if c >= 2:
                    sp_.wait_ge(w_hi_ready, c - 1)
                    sp_.wait_ge(w_lo_ready, c - 1)
                k = KT if c < N_IN else KT // 2
                sp_.dma_start(raw[c % 2][:, :].rearrange("p (k n) -> p k n", k=k),
                              w_in_chunk(c) if c < N_IN else w_out_chunk(c)).then_inc(raw_in[c % 2], 16)

            def load_gu(e, s, done):
                sp_.dma_start(gu_place(s, 0), gu_of(exp_w_gate, e)).then_inc(done, 16)
                sp_.dma_start(gu_place(s, 1), gu_of(exp_w_up, e)).then_inc(done, 16)

            def load_dn(e, s, done):
                sp_.dma_start(wdn[s][:, :, :].rearrange("p j d -> p (j d)"), dn_of(e)).then_inc(done, 16)

            sp_.wait_ge(chunk_used, N_IN)
            sp_.wait_ge(y_lo_ready, KT)
            for s in range(3):
                load_gu(s, s, gu_in[s])
                load_dn(s, s, dn_in[s])
            early = (N_CHUNKS - 3) % HL
            sp_.wait_ge(chunk_used, N_CHUNKS - 2)
            load_gu(3 + early, 3 + early, gu_in[3 + early])
            sp_.wait_ge(mixed, 2 * TT)
            for s in range(3, RING):
                if s != 3 + early:
                    load_gu(s, s, gu_in[s])
                load_dn(s, s, dn_in[s])

            sp_.wait_ge(h1_ready, TT)
            sp_.wait_ge(h1_turned, 2 * TT)
            sp_.wait_ge(h1_stored, 16 * TT)
            load_gu(RING, RING, gu_in[RING])
            load_dn(RING, RING, dn_in[RING])

            def refill(q, r):
                i = q + r * RING
                done = i - RING + (0 if static(r) and q < FIRST + RING else 1)
                s = slot_of(q)
                sp_.wait_ge(gu_summed, done)
                load_gu(i, s, gu_in[s])
                sp_.wait_ge(dn_summed, done)
                load_dn(i, s, dn_in[s])

            for q in range(FIRST, FIRST + RING):
                refill(q, 0)
            with sp_.Fori(0, (N_EXP - FIRST - RING) // RING) as r:
                for u in range(RING):
                    refill(FIRST + RING + u, r)
            for q in range(N_EXP - (N_EXP - FIRST) % RING, N_EXP):
                refill(q, 0)
            last_of_1 = max(q for q in range(N_EXP) if slot_of(q) == 1)
            sp_.wait_ge(dn_summed, last_of_1 + 1)
            sp_.dma_start(h1[:, :, :].rearrange("p t (a h) -> p t a h", a=2),
                          h1_rows.rearrange("(t p a) h -> p t a h", p=P, a=2)).then_inc(h1_in, 16)
            sp_.dma_start(ln2g[:, :], row(ln2_g).to_broadcast([P, D])).then_inc(ln2_in, 16)
            sp_.dma_start(ln2b[:, :], row(ln2_b).to_broadcast([P, D])).then_inc(ln2_in, 16)
            def load_over(j):
                e = sp_.value_load(over_exp_i[0:1, bass.ds(j, 1)], min_val=0, max_val=N_EXP - 1)
                sp_.wait_ge(dn_summed, j + N_EXP)
                load_gu(e, 0, gu_in[0])
                load_dn(e, 0, dn_in[0])

            overflow(sp_, load_over)
            for b in range(1, RING):
                sp_.wait_ge(y_scattered[b], mains(b))
            n = sp_.value_load(n_over[0:1, 0:1], min_val=0, max_val=MAX_OVER)
            sp_.wait_ge(y_scattered[0], 16 * n + mains(0))
            for t in range(TT):
                for k in range(TOP_K):
                    src = y_pairs[2 * (k * T + t * P):2 * (k * T + (t + 1) * P), :]
                    sp_.dma_start(pair_y[t][k][:, :], src.rearrange("(p a) h -> p (a h)", a=2)).then_inc(pairs_in[t], 16)
            for t in range(TT):
                if t == TT - 1:
                    sp_.wait_ge(out_ready, 1)
                sp_.wait_ge(out_ready_pool, t + 1)
                sp_.dma_start(out_rows[t * P:(t + 1) * P, :], pair_y[t][1][:, :]).then_inc(out_stored, 16)
            sp_.wait_ge(out_stored, 16 * TT)

        @block.gpsimd
        def _(pool):
            pool.memset(ident[:, :], 0.0).then_inc(ident_done, 1)
            pool.wait_ge(ident_done, 1)
            pool.affine_select(out=ident[:, :], in_=ident[:, :], compare_op=ALU.not_equal, fill=1.0,
                               base=0, pattern=[[-1, P]], channel_multiplier=1).then_inc(ident_done, 1)
            for w, dst in ((rg_gate_a_w, wga), (rg_gate_x_w, wgx)):
                pool.dma_start(dst[:, :, :], w.rearrange("(a b) i j -> (b i) a j", b=2)).then_inc(gates_in, 16)
            pool.memset(tri[:, :], 1.0).then_inc(const_pool, 1)
            pool.memset(ones[:, :], 1.0).then_inc(const_pool, 1)
            pool.iota(iota_i[:, 0:N_GROUPS], pattern=[[-1, N_GROUPS]], base=N_GROUPS, channel_multiplier=0).then_inc(const_pool, 1)
            pool.iota(iota_i[:, 4:4 + N_EXP], pattern=[[-1, N_EXP]], base=N_EXP, channel_multiplier=0).then_inc(const_pool, 1)
            pool.iota(iota_i[:, 36:36 + BLOCK], pattern=[[1, BLOCK]], base=0, channel_multiplier=0).then_inc(const_pool, 1)
            pool.iota(iota_i[:, 100:108], pattern=[[2 * P, TOP_K * TT]], base=1, channel_multiplier=2).then_inc(const_pool, 1)
            pool.memset(iota_i[:, 108:112], 0).then_inc(const_pool, 1)
            pool.iota(iota_i[:, 112:160], pattern=[[1, ITEMS]], base=0, channel_multiplier=0).then_inc(const_pool, 1)
            pool.wait_ge(const_pool, 8)
            pool.affine_select(out=tri[:, :], in_=tri[:, :], compare_op=ALU.is_gt, fill=0.0,
                               base=0, pattern=[[1, P]], channel_multiplier=-1).then_inc(const_pool, 1)
            pool.wait_ge(const_pool, 9)
            pool.memset(iota_i[64:128, 108:109], 1).then_inc(const_pool, 1)
            pool.wait_ge(const_pool, 10)
            pool.memset(zeros[:, :], 0.0).then_inc(const_pool, 1)
            pool.memset(held[:, :], 1.0).then_inc(pool_chain, 1)
            pool.wait_ge(const_pool, 11)
            pool.tensor_copy(iota_f[:, :], iota_i[:, :]).then_inc(const_done, 1)
            for j in range(CT):
                pool.memset(rg_pad[j][:, 0:PAD], 0.0).then_inc(pads_zero, 1)
            pool.dma_start(ln_g[:, :], row(ln1_g).to_broadcast([P, D])).then_inc(ln1_in, 16)
            pool.dma_start(ln_b[:, :], row(ln1_b).to_broadcast([P, D])).then_inc(ln1_in, 16)
            pool.dma_start(wr[:, :, 0:N_GROUPS], router_group_w.rearrange("(k p) n -> p k n", p=P)).then_inc(router_in, 16)
            pool.dma_start(wr[:, :, N_GROUPS:NR], router_expert_w.rearrange("(k p) n -> p k n", p=P)).then_inc(router_in, 16)
            pool.dma_start(rbias[:, 0:N_GROUPS], row(router_group_b).to_broadcast([P, N_GROUPS])).then_inc(router_in, 16)
            pool.dma_start(rbias[:, N_GROUPS:NR], row(router_expert_b).to_broadcast([P, N_EXP])).then_inc(router_in, 16)
            pool.wait_ge(y_ready, CT)
            for j in range(CT):
                pool.memset(sc_pad[j][:, 0:SC_TAPS - 1], 0.0).then_inc(pads_zero, 1)
            for t in range(TT):
                pool.wait_ge(h1_ready, t + 1)
                pool.dma_start(h1_rows[2 * t * P:2 * (t + 1) * P, :].rearrange("(p a) h -> p (a h)", a=2), xres[:, t, :]).then_inc(h1_stored, 16)
            pool.wait_ge(routed, TT)
            for b in range(2):
                pool.memset(hid[b][:, :], 0.0).then_inc(hid_zero, 1)
            pool.wait_ge(table_summed, 1)
            for b in range(RING // 2):
                pool.memset(xg[b][:, :], 0.0).then_inc(xg_zero, 1)
            pool.wait_ge(xg_zero, RING // 2)
            pool.wait_ge(rows_ready, 1)
            pool.wait_ge(h1_stored, 16 * TT)

            def gather(b, rows):
                pool.indirect_dma_start(out=xg[b][:, :], out_offset=None, in_=h1_rows,
                                        in_offset=bass.IndirectOffsetOnAxis(ap=rows, axis=0),
                                        bounds_check=2 * T - 1, oob_is_err=False).then_inc(x_gathered[b], 16)

            def scatter(b, rows):
                pool.indirect_dma_start(out=y_pairs, out_offset=bass.IndirectOffsetOnAxis(ap=rows, axis=0),
                                        in_=ys[b][:, :], in_offset=None,
                                        bounds_check=2 * TOP_K * T - 1, oob_is_err=False).then_inc(y_scattered[b], 16)

            for i in range(RING):
                if i == RING // 2:
                    for b in range(RING // 2, RING):
                        pool.memset(xg[b][:, :], 0.0).then_inc(xg_zero, 1)
                    pool.wait_ge(xg_zero, RING)
                gather(i, x_rows[:, i:i + 1])
            for i in range(N_EXP):
                if i + RING < N_EXP:
                    pool.wait_ge(xg_turned, i + 1)
                    gather(i % RING, x_rows[:, i + RING:i + RING + 1])
                pool.wait_ge(y_copied, i + 1)
                scatter(i % RING, y_rows[:, i:i + 1])

            def over_rows(j):
                i, n = j + N_EXP, j * 5
                pool.wait_ge(pool_chain, n + 1)
                pool.tensor_tensor(held[:, :], held[:, :], held[:, :], ALU.mult).then_inc(pool_chain, 1)
                pool.tensor_copy(x_row_now[:, :], x_rows[:, bass.ds(i, 1)]).then_inc(pool_chain, 1)
                pool.tensor_copy(y_row_now[:, :], y_rows[:, bass.ds(i, 1)]).then_inc(pool_chain, 1)
                pool.wait_ge(pool_chain, n + 4)
                pool.wait_ge(xg_turned, i)
                pool.tensor_tensor(held[:, :], held[:, :], held[:, :], ALU.mult).then_inc(pool_chain, 1)
                gather(0, x_row_now[:, :])
                pool.wait_ge(pool_chain, n + 5)
                pool.wait_ge(y_copied, i + 1)
                pool.tensor_tensor(held[:, :], held[:, :], held[:, :], ALU.mult).then_inc(pool_chain, 1)
                scatter(0, y_row_now[:, :])
                pool.wait_ge(y_scattered[0], 16 * j + 16 + mains(0))
                pool.wait_ge(pool_chain, n + 6)

            overflow(pool, over_rows)

            pool.wait_ge(ln2_in, 32)
            for t in range(TT):
                z = pair_y[t][1][:, H if t == TT - 1 else 0:D]
                part = slice(H if t == TT - 1 else 0, D)
                pool.wait_ge(normed2, t + 1)
                pool.tensor_tensor(z, z, ln2g[:, part], ALU.mult).then_inc(out_scaled, 1)
                pool.wait_ge(out_scaled, t + 1)
                pool.tensor_tensor(z, z, ln2b[:, part], ALU.add).then_inc(out_ready_pool, 1)

        @block.scalar
        def _(act):
            for n, v in enumerate((rg_conv_w, row(rg_conv_b), row(rg_gate_a_b), row(rg_gate_x_b), row(rg_lambda), sc_conv_w)):
                at_row = (P_RGW, P_RGB, P_AB, P_XB, P_LAM, P_SCW)[n]
                act.dma_start(par_rows[at_row:at_row + v.shape[0], :], v).then_inc(params_in, 16)

            def split_hi(c):
                act.wait_ge(raw_in[c % 2], 16 * (c // 2 + 1))
                if c >= HL:
                    act.wait_ge(chunk_used, c - HL + 1)
                act.activation(w_hi[c % HL][:, :], raw[c % 2][:, :], ACT.Copy).then_inc(w_hi_ready, 1)

            split_hi(0)
            for k in range(KT):
                act.wait_ge(x_turned, k + 1)
                act.activation(xT_hi[:, k, :], psum[k][:, :], ACT.Copy).then_inc(xT_hi_ready, 1)

            def evacuate(c, func, dst):
                for n in range(2):
                    act.wait_ge(projected, 2 * c + n + 1)
                    act.activation(dst[2 * (c % 2) + n], psum[(2 * c + n) % 4][:, :], func).then_inc(act_evacuated, 1)

            def y_split_hi(k, src):
                act.wait_ge(y_ready, k + 1)
                act.activation(y_hi[k][:, :], src, ACT.Copy).then_inc(y_hi_ready, 1)

            split_hi(1)
            act.wait_ge(par_ready, 1)
            act.activation(sp[:, 0, :], par[:, :, P_LAM], ACT.Abs).then_inc(lam_abs, 1)
            act.wait_ge(lam_abs, 1)
            act.activation(sp[:, 1, :], sp[:, 0, :], ACT.Exp, scale=-1.0).then_inc(lam_exp, 1)
            pad_dst = [t[:, PAD:PAD + T] for t in rg_pad]
            for s in range(N_CHUNKS - 2):
                split_hi(s + 2)
                if s in (1, 2):
                    evacuate(s - 1, ACT.Copy, pad_dst)
                if s in (3, 4):
                    evacuate(s - 1, ACT.Gelu_apprx_tanh, [gelu_g[:, j, :] for j in range(CT)])
                if s == 4:
                    for j in range(CT):
                        act.wait_ge(gates_summed, j + 1)
                        act.activation(gr[j][:, :], psum[4 + 2 * (j % 2)][:, :], ACT.Sigmoid, bias=par[:, j, P_AB:P_AB + 1]).then_inc(gates_ready, 1)
                        act.activation(gi[j][:, :], psum[5 + 2 * (j % 2)][:, :], ACT.Sigmoid, bias=par[:, j, P_XB:P_XB + 1]).then_inc(gates_ready, 1)
                if s == 6:
                    for j in range(CT):
                        act.wait_ge(drive_sq, j + 1)
                        act.activation(conv[j][:, 0:T], conv[j][:, 0:T], ACT.Sqrt).then_inc(drive_root, 1)
                if s in (5, 6):
                    act.wait_ge(xc_ready, CT)
                    evacuate(s - 1, ACT.Copy, [t[:, :] for t in sc_c])
                if s == 5:
                    act.wait_ge(c8_ready, 1)
                    for j in range(CT):
                        act.wait_ge(gates_ready, 2 * j + 1)
                        act.activation(th[j], gr[j][:, :], ACT.Tanh, scale=nc8[:, j:j + 1]).then_inc(act_chain, 1)
                        act.wait_ge(act_chain, j + 1)
                        act.activation(gr[j][:, :], gr[j][:, :], ACT.Exp, scale=c8[:, j:j + 1]).then_inc(decay_in, 1)
                if s == 7:
                    for j in range(CT):
                        y_split_hi(j, th[j])
                if s == 10:
                    for j in range(CT):
                        y_split_hi(CT + j, y_sc[j][:, :])
            def copy_h1T(t):
                for n in range(2):
                    act.wait_ge(h1_turned, 2 * t + n + 1)
                    if t >= 2:
                        act.wait_ge(logits_summed, t - 1)
                    act.activation(h1T[t % 2][:, 4 * n:4 * n + 4, :], psum[4 + 2 * (t % 2) + n][:, :], ACT.Copy).then_inc(h1T_ready, 1)

            for t in range(TT):
                act.wait_ge(var_ready, t + 1)
                act.activation(rstd[:, t:t + 1], rstd[:, t:t + 1], ACT.Sqrt).then_inc(dev_ready, 1)
                act.wait_ge(moments_ready, t + 1)
                act.activation(xres[:, t, :], xres[:, t, :], ACT.Identity, bias=shift[:, t:t + 1], scale=rstd[:, t:t + 1]).then_inc(normed, 1)
                if t >= 1:
                    copy_h1T(t - 1)
            copy_h1T(TT - 1)
            act.wait_ge(gdiff_ready, 2)
            act.activation(gexp[:, :, :], gexp[:, :, :], ACT.Exp).then_inc(gexp_ready, 1)
            act.activation(vexp[:, :], vdiff[:, :], ACT.Exp).then_inc(gexp_ready, 1)

            def gate(i, b, lag):
                act.wait_ge(gu_summed, i + 1)
                wait_free(act, hid_ready, i, lag)
                act.activation(gated[b][:, :], psum[2 + b][0:BLOCK, 0:F], ACT.Silu).then_inc(gated_ready, 1)

            def copy_y(i, b, yb, scattered):
                act.wait_ge(dn_summed, i + 1)
                if not static(scattered) or scattered > 0:
                    act.wait_ge(y_scattered[yb], scattered)
                act.activation(ys[yb][:, :], psum[6 + b][:, :], ACT.Copy).then_inc(y_copied, 1)

            def copy_main_y(q, r):
                copy_y(q + r * RING, q % 2, q % RING, before(q, r))

            def act_item(q, r):
                gate(q + r * RING, q % 2, 2)
                if q >= 1:
                    copy_main_y(q - 1, r)

            rounds(act, act_item)
            copy_main_y(N_EXP - 1, 0)

            def act_over(j):
                gate(j + N_EXP, 0, 1)
                copy_y(j + N_EXP, 0, 0, 16 * j + mains(0))

            overflow(act, act_over)
            def scale_first(t):
                act.wait_ge(pairs_in[t], 32)
                act.wait_ge(weights_ready, 1)
                act.activation(pair_y[t][0][:, :], pair_y[t][0][:, :], ACT.Copy, scale=weight[:, 0, t:t + 1]).then_inc(first_scaled, 1)

            scale_first(0)
            for t in range(TT):
                if t + 1 < TT:
                    scale_first(t + 1)
                act.wait_ge(var2_ready, t + 1)
                act.activation(rstd[:, t:t + 1], rstd[:, t:t + 1], ACT.Sqrt).then_inc(dev2_ready, 1)
                act.wait_ge(moments2_ready, t + 1)
                act.activation(pair_y[t][1][:, :], pair_y[t][1][:, :], ACT.Identity, bias=shift[:, t:t + 1], scale=rstd[:, t:t + 1]).then_inc(normed2, 1)

        @block.tensor
        def _(pe):
            pe.wait_ge(ident_done, 2)
            for k in range(KT):
                pe.wait_ge(x_in[k // 4], 16)
                for t in range(TT):
                    mm = pe.transpose(psum[k][:, t * P:(t + 1) * P], xres[:, t, k * P:(k + 1) * P], ident[:, :])
                mm.then_inc(x_turned, 1)

            def products(dst, a_hi, a_lo, b_hi, b_lo, start, stop):
                pe.matmul(dst, a_hi, b_hi, start=start, stop=False)
                pe.matmul(dst, a_hi, b_lo, start=False, stop=False)
                return pe.matmul(dst, a_lo, b_hi, start=False, stop=stop)

            for c in range(N_IN):
                hi, lo = (w[c % HL][:, :].rearrange("p (k n) -> p k n", k=KT) for w in (w_hi, w_lo))
                pe.wait_ge(w_hi_ready, c + 1)
                pe.wait_ge(w_lo_ready, c + 1)
                for n in range(2):
                    if c < 2:
                        pe.wait_ge(xT_lo_ready, 2 * c + n + 1)
                    elif c < 8:
                        pe.wait_ge(act_evacuated, 2 * (c - 2) + n + 1)
                    else:
                        pe.wait_ge(dve_evacuated, 2 * (c - 8) + n + 1)
                    bank = psum[(2 * c + n) % 4]
                    for k in range(KT):
                        if c == 0 and n == 0:
                            pe.wait_ge(xT_hi_ready, k + 1)
                            pe.wait_ge(xT_lo_ready, k + 1)
                        mm = products(bank[:, :], hi[:, k, n * P:(n + 1) * P], lo[:, k, n * P:(n + 1) * P],
                                      xT_hi[:, k, :], xT_lo[:, k, :], k == 0, k == KT - 1)
                    mm.then_inc(projected, 1)
                pe.wait_ge(projected, 2 * c + 2)
                pe.nop().then_inc(chunk_used, 1)
                if c == 0:
                    pe.wait_ge(params_in, 16 * 6)
                    for j in range(CT):
                        mm = pe.transpose(psum[7][:, j * PARAMS:(j + 1) * PARAMS], par_rows[:, j * P:(j + 1) * P], ident[0:PARAMS, 0:PARAMS])
                    mm.then_inc(par_turned, 1)
                if c == 3:
                    pe.wait_ge(gates_in, 32)
                    for j in range(CT):
                        pe.wait_ge(xc_ready, j + 1)
                        if j >= 2:
                            pe.wait_ge(gates_ready, 2 * (j - 2) + 2)
                        for w, bank in ((wga, psum[4 + 2 * (j % 2)]), (wgx, psum[5 + 2 * (j % 2)])):
                            for q in range(2):
                                h = slice(64 * q, 64 * q + 64)
                                mm = pe.matmul(bank[h, :], w[h, j, :], conv[j][h, :], start=True, stop=True)
                        mm.then_inc(gates_summed, 1)

            def out_products(c, t, first, last):
                hi, lo = (w[c % HL][:, :].rearrange("p (k n) -> p k n", k=4) for w in (w_hi, w_lo))
                kh = (c - N_IN) % 2
                bank = psum[(4 if c - N_IN < 2 else 0) + t]
                for k in range(4):
                    y = slice(t * P, (t + 1) * P)
                    mm = products(bank[:, :], y_hi[4 * kh + k][:, y], y_lo[4 * kh + k][:, y], hi[:, k, :], lo[:, k, :],
                                  first and k == 0, last and k == 3)
                return mm

            for c in (N_IN, N_IN + 1):
                pe.wait_ge(w_hi_ready, c + 1)
                pe.wait_ge(w_lo_ready, c + 1)
                kh = (c - N_IN) % 2
                pe.wait_ge(y_hi_ready, CT * (kh + 1))
                pe.wait_ge(y_lo_ready, CT * (kh + 1))
                for t in range(TT):
                    mm = out_products(c, t, kh == 0, kh == 1)
                    if kh == 1:
                        mm.then_inc(mixed, 1)
                    elif t == TT - 1:
                        mm.then_inc(chunk_used, 1)
            pe.wait_ge(mixed, TT)
            pe.nop().then_inc(chunk_used, 1)
            for c in (N_IN + 2, N_IN + 3):
                pe.wait_ge(w_hi_ready, c + 1)
                pe.wait_ge(w_lo_ready, c + 1)

            def turn_h1(t):
                pe.wait_ge(h1_ready, t + 1)
                if t >= 2:
                    pe.wait_ge(h1T_ready, 2 * (t - 1))
                for n in range(2):
                    for k in range(4):
                        mm = pe.transpose(psum[4 + 2 * (t % 2) + n][:, k * P:(k + 1) * P], xres[:, t, (4 * n + k) * P:(4 * n + k + 1) * P], ident[:, :])
                    mm.then_inc(h1_turned, 1)

            def router(t):
                if t == 0:
                    pe.wait_ge(router_in, 16 * 4)
                pe.wait_ge(h1T_ready, 2 * t + 2)
                for k in range(KT):
                    mm = pe.matmul(psum[t][:, 0:NR], h1T[t % 2][:, k, :], wr[:, k, :], start=k == 0, stop=k == KT - 1)
                mm.then_inc(logits_summed, 1)

            for t in range(TT):
                out_products(N_IN + 2, t, True, False)
                out_products(N_IN + 3, t, False, True).then_inc(mixed, 1)
                if t >= 2:
                    turn_h1(t - 2)
                if t >= 3:
                    router(t - 3)
            turn_h1(TT - 2)
            router(TT - 3)
            turn_h1(TT - 1)
            router(TT - 2)
            router(TT - 1)

            pe.wait_ge(chosen_ready, 1)
            for t in range(TT + 1):
                dst = psum[0][:, t * N_EXP:(t + 1) * N_EXP]
                for q in range(min(t, TT)):
                    mm = pe.matmul(dst, ones[:, :], chosen_b[:, q, :], start=q == 0, stop=t == TT and q == TT - 1)
                if t < TT:
                    mm = pe.matmul(dst, tri[:, :], chosen_b[:, t, :], start=t == 0, stop=True)
            mm.then_inc(counted, 1)
            pe.wait_ge(hot_ready, 2)
            for n in range(TOP_K * TT):
                mm = pe.matmul(psum[1][:, 0:ITEMS], hot_slot[:, n, :], hot_item[:, n, :], start=n == 0, stop=n == TOP_K * TT - 1)
            mm.then_inc(table_summed, 1)

            def turn_x(i, b, g, lag, gathered):
                pe.wait_ge(x_gathered[g], gathered)
                wait_free(pe, xTg_ready, i, lag)
                for j in range(4):
                    rows = xg[g][:, :].rearrange("p (m j) -> p j m", j=4)[:, j, :]
                    mm = pe.transpose(psum[b][:, j * P:(j + 1) * P], rows, ident[:, :])
                mm.then_inc(xg_turned, 1)

            def gate_up(i, s, b, lag, loads):
                pe.wait_ge(gu_in[s], 32 * loads)
                pe.wait_ge(xTg_ready, i + 1)
                wait_free(pe, hid_ready, i, lag)
                for k in range(KT):
                    h, j = divmod(k, 4)
                    for which in range(2):
                        mm = pe.matmul(psum[2 + b][BLOCK * which:BLOCK * which + BLOCK, 0:F],
                                       xTg[b][:, j, h * BLOCK:(h + 1) * BLOCK], wgu[s][:, which, k, :],
                                       start=k == 0, stop=k == KT - 1)
                mm.then_inc(gu_summed, 1)

            def turn_hid(i, b, lag):
                pe.wait_ge(hid_ready, i + 1)
                wait_free(pe, hidT_ready, i, lag)
                for j in range(2):
                    cols = hid[b][:, :].rearrange("p (m j) -> p j m", j=2)[:, j, :]
                    mm = pe.transpose(psum[4 + b][:, j * P:(j + 1) * P], cols, ident[:, :])
                mm.then_inc(hid_turned, 1)

            def down(i, s, b, lag, loads):
                pe.wait_ge(dn_in[s], 16 * loads)
                pe.wait_ge(hidT_ready, i + 1)
                wait_free(pe, y_copied, i, lag)
                for j in range(2):
                    for n in range(2):
                        mm = pe.matmul(psum[6 + b][BLOCK * n:BLOCK * n + BLOCK, :], hidT[b][:, j, :],
                                       wdn[s][:, j, n * H:(n + 1) * H], start=j == 0, stop=j == 1)
                mm.then_inc(dn_summed, 1)

            def turn_main_x(q, r):
                turn_x(q + r * RING, q % 2, q % RING, 2, before(q, r) + 16)

            def main_down(q, r):
                down(q + r * RING, slot_of(q), q % 2, 2, loads_of(q, r))

            def pe_item(q, r):
                if not static(r) or q + 1 < N_EXP:
                    turn_main_x(q + 1, r)
                gate_up(q + r * RING, slot_of(q), q % 2, 2, loads_of(q, r))
                if q >= 1:
                    main_down(q - 1, r)
                turn_hid(q + r * RING, q % 2, 2)

            turn_main_x(0, 0)
            rounds(pe, pe_item)
            main_down(N_EXP - 1, 0)

            def pe_over(j):
                i, loads = j + N_EXP, j + 1 + sum(slot_of(q) == 0 for q in range(N_EXP))
                turn_x(i, 0, 0, 1, 16 * j + 16 + mains(0))
                gate_up(i, 0, 0, 1, loads)
                turn_hid(i, 0, 1)
                down(i, 0, 0, 1, loads)

            overflow(pe, pe_over)

        @block.vector
        def _(dve_):
            v = dve_
            chain = [0]

            def link(ins):
                chain[0] += 1
                ins.then_inc(dve, 1)
                v.wait_ge(dve, chain[0])

            def split_lo(c):
                v.wait_ge(w_hi_ready, c + 1)
                v.tensor_tensor(w_lo[c % HL][:, :], raw[c % 2][:, :], w_hi[c % HL][:, :], ALU.subtract).then_inc(w_lo_ready, 1)

            split_lo(0)
            for k in range(KT):
                v.wait_ge(xT_hi_ready, k + 1)
                v.tensor_tensor(xT_lo[:, k, :], psum[k][:, :], xT_hi[:, k, :], ALU.subtract).then_inc(xT_lo_ready, 1)

            split_lo(1)
            v.wait_ge(par_turned, 1)
            v.tensor_copy(par[:, :, :], psum[7][:, 0:CT * PARAMS].rearrange("p (j n) -> p j n", j=CT)).then_inc(par_ready, 1)
            v.wait_ge(par_ready, 1)
            lam = par[:, :, P_LAM]

            v.wait_ge(lam_exp, 1)
            e, q, q2, ser, tmp = sp[:, 1, :], sp[:, 2, :], sp[:, 3, :], sp[:, 4, :], sp[:, 5, :]
            link(v.tensor_scalar(tmp, e, 2.0, None, ALU.add))
            link(v.reciprocal(tmp, tmp))
            link(v.tensor_tensor(q, e, tmp, ALU.mult))
            link(v.tensor_tensor(q2, q, q, ALU.mult))
            link(v.tensor_scalar(ser, q2, 1.0 / (2 * LOG_TERMS + 1), None, ALU.mult))
            for n in range(LOG_TERMS - 1, 0, -1):
                link(v.scalar_tensor_tensor(out=ser, in0=ser, scalar=1.0 / (2 * n + 1), in1=q2, op0=ALU.add, op1=ALU.mult))
            link(v.scalar_tensor_tensor(out=ser, in0=ser, scalar=1.0, in1=q, op0=ALU.add, op1=ALU.mult))
            link(v.tensor_scalar(tmp, lam, -1.0, 0.0, ALU.mult, ALU.max))
            link(v.scalar_tensor_tensor(out=tmp, in0=ser, scalar=2.0, in1=tmp, op0=ALU.mult, op1=ALU.add))
            link(v.tensor_scalar(nc8[:, :], tmp, RG_C, None, ALU.mult))
            v.tensor_scalar(c8[:, :], tmp, -RG_C, None, ALU.mult).then_inc(c8_ready, 1)

            def taps(dst, src, j, first, n, bias, done=None):
                w = lambda i: par[:, j, first + i:first + i + 1]
                if bias is None:
                    link(v.tensor_scalar(dst, src(n - 1), w(n - 1), None, ALU.mult))
                else:
                    link(v.tensor_scalar(dst, src(n - 1), w(n - 1), bias, ALU.mult, ALU.add))
                for i in range(n - 1):
                    ins = v.scalar_tensor_tensor(out=dst, in0=src(i), scalar=w(i), in1=dst, op0=ALU.mult, op1=ALU.add)
                    if i == n - 2 and done is not None:
                        ins.then_inc(done, 1)
                    else:
                        link(ins)

            def rg_conv(j):
                v.wait_ge(act_evacuated, j + 1)
                v.wait_ge(pads_zero, j + 1)
                taps(conv[j][:, 0:T], lambda i: rg_pad[j][:, i:i + T], j, P_RGW, RG_TAPS, par[:, j, P_RGB:P_RGB + 1], xc_ready)

            def drive(j):
                a, u, m = gr[j][:, :], gi[j][:, :], conv[j][:, 0:T]
                v.wait_ge(decay_in, j + 1)
                link(v.tensor_tensor(u, u, m, ALU.mult))
                link(v.tensor_tensor(m, a, a, ALU.mult))
                v.scalar_tensor_tensor(out=m, in0=m, scalar=1.0, in1=th[j], op0=ALU.add, op1=ALU.mult).then_inc(drive_sq, 1)

            def recurrence(j):
                a, u, m = gr[j][:, :], gi[j][:, :], conv[j][:, 0:T]
                v.wait_ge(drive_root, j + 1)
                link(v.tensor_tensor(u, u, m, ALU.mult))
                link(v.tensor_tensor_scan(m, a, u, 0.0, ALU.mult, ALU.add))
                v.tensor_tensor(th[j], m, gelu_g[:, j, :], ALU.mult).then_inc(y_ready, 1)

            def short_conv(j):
                v.wait_ge(projected, 12 + j + 1)
                v.wait_ge(act_evacuated, 8 + j + 1)
                v.wait_ge(pads_zero, CT + j + 1)
                v.tensor_tensor(sc_pad[j][:, SC_TAPS - 1:SC_TAPS - 1 + T], psum[j % 4][:, :], sc_c[j][:, :], ALU.mult).then_inc(dve_evacuated, 1)
                v.wait_ge(dve_evacuated, j + 1)
                taps(sc_conv[j][:, :], lambda i: sc_pad[j][:, i:i + T], j, P_SCW, SC_TAPS, None)

            def y_short(j):
                v.wait_ge(projected, 16 + j + 1)
                v.tensor_tensor(y_sc[j][:, :], psum[j % 4][:, :], sc_conv[j][:, :], ALU.mult).then_inc(y_ready, 1)

            def y_split_lo(k, src):
                v.wait_ge(y_hi_ready, k + 1)
                v.tensor_tensor(y_lo[k][:, :], src, y_hi[k][:, :], ALU.subtract).then_inc(y_lo_ready, 1)

            for s in range(N_CHUNKS - 2):
                split_lo(s + 2)
                if s in (1, 2):
                    rg_conv(2 * s - 2)
                    rg_conv(2 * s - 1)
                if s == 5:
                    for j in range(CT):
                        drive(j)
                if s == 6:
                    for j in range(CT):
                        recurrence(j)
                if s == 7:
                    for j in range(CT):
                        y_split_lo(j, th[j])
                if s in (7, 8):
                    short_conv(2 * s - 14)
                    short_conv(2 * s - 13)
                if s in (9, 10):
                    y_short(2 * s - 18)
                    y_short(2 * s - 17)
                if s == 10:
                    for j in range(CT):
                        y_split_lo(CT + j, y_sc[j][:, :])

            def residual(n):
                h, t = divmod(n, TT)
                part = xres[:, t, h * H:(h + 1) * H]
                v.wait_ge(mixed, n + 1)
                link(v.scalar_tensor_tensor(out=part, in0=part, scalar=ALPHA, in1=psum[(4, 0)[h] + t][:, :], op0=ALU.mult, op1=ALU.add))
                link(v.bn_stats(stats[:, t, h, :], part))

            def finish_moments(t, var_done, dev_done, done):
                link(v.bn_aggr(moments[:, t, :], stats[:, t, :, :]))
                v.tensor_scalar(rstd[:, t:t + 1], moments[:, t, 1:2], LN_EPS, None, ALU.add).then_inc(var_done, 1)
                v.wait_ge(dev_done, t + 1)
                link(v.reciprocal(rstd[:, t:t + 1], rstd[:, t:t + 1]))
                v.scalar_tensor_tensor(out=shift[:, t:t + 1], in0=moments[:, t, 0:1], scalar=-1.0, in1=rstd[:, t:t + 1],
                                       op0=ALU.mult, op1=ALU.mult).then_inc(done, 1)

            def take_logits(t):
                v.wait_ge(logits_summed, t + 1)
                v.tensor_tensor(logits[:, t, :], psum[t][:, 0:NR], rbias[:, :], ALU.add).then_inc(routed, 1)

            for t in range(TT):
                residual(t)
            v.wait_ge(ln1_in, 32)
            for t in range(TT):
                residual(TT + t)
                finish_moments(t, var_ready, dev_ready, moments_ready)
                v.wait_ge(normed, t + 1)
                link(v.tensor_tensor(xres[:, t, :], xres[:, t, :], ln_g[:, :], ALU.mult))
                v.tensor_tensor(xres[:, t, :], xres[:, t, :], ln_b[:, :], ALU.add).then_inc(h1_ready, 1)
                if t == 0:
                    v.wait_ge(router_in, 16 * 4)
                if t == TT - 1:
                    take_logits(0)
            for t in range(1, TT):
                take_logits(t)
            v.wait_ge(routed, TT)

            v.wait_ge(const_done, 1)
            g_logits = logits[:, :, 0:N_GROUPS]
            e_logits = logits[:, :, N_GROUPS:NR]
            over_n = lambda ap, n: ap.unsqueeze(2).to_broadcast([P, ap.shape[1], n])
            down_of = lambda key, n: key.unsqueeze(1).to_broadcast([P, TT, n])

            def first_max(values, top, key, key_top, hot, key_down, n):
                link(v.tensor_reduce(top, values, AX, ALU.max))
                link(v.tensor_tensor(key, values, over_n(top, n), ALU.is_equal))
                link(v.tensor_tensor(key, key, down_of(key_down, n), ALU.mult))
                link(v.tensor_reduce(key_top, key, AX, ALU.max))
                link(v.tensor_tensor(hot, key, over_n(key_top, n), ALU.is_equal))

            first_max(g_logits, gmax[:, :], gkey[:, :, :], gkmax[:, :], ghot[:, :, :], down4, N_GROUPS)
            link(v.tensor_scalar(gkey[:, :, :], ghot[:, :, :], -1.0, FAR, ALU.add, ALU.mult))
            pushed = gkey[:, :, :].unsqueeze(3).to_broadcast([P, TT, N_GROUPS, PER_GROUP])
            link(v.tensor_tensor(masked[:, :, :].rearrange("p t (g n) -> p t g n", g=N_GROUPS),
                                 e_logits.rearrange("p t (g n) -> p t g n", g=N_GROUPS), pushed, ALU.add))
            first_max(masked[:, :, :], vtop[:, 0, :], ekey[:, :, :], kkey[:, 0, :], chosen[:, 0, :, :], down32, N_EXP)
            link(v.scalar_tensor_tensor(out=masked2[:, :, :], in0=chosen[:, 0, :, :], scalar=-3.0 * FAR, in1=masked[:, :, :], op0=ALU.mult, op1=ALU.add))
            first_max(masked2[:, :, :], vtop[:, 1, :], ekey[:, :, :], kkey[:, 1, :], chosen[:, 1, :, :], down32, N_EXP)
            v.tensor_tensor(chosen_b[:, :, :], chosen[:, 0, :, :], chosen[:, 1, :, :], ALU.add).then_inc(chosen_ready, 1)
            v.tensor_tensor(gexp[:, :, :], g_logits, over_n(gmax[:, :], N_GROUPS), ALU.subtract).then_inc(gdiff_ready, 1)
            v.tensor_tensor(vdiff[:, :], vtop[:, 1, :], vtop[:, 0, :], ALU.subtract).then_inc(gdiff_ready, 1)
            link(v.tensor_scalar(expert[:, :], kkey[:, :, :].rearrange("p k t -> p (k t)"), -1.0, float(N_EXP), ALU.mult, ALU.add))

            v.wait_ge(counted, 1)
            counts = psum[0][:, 0:TT * N_EXP].rearrange("p (t e) -> p t e", t=TT)
            for k in range(TOP_K):
                link(v.tensor_tensor(prod[:, k, :, :], counts, chosen[:, k, :, :], ALU.mult))
            link(v.tensor_reduce(rank[:, :], prod[:, :, :, :].rearrange("p k t e -> p (k t) e"), AX, ALU.add))
            down_half = (BLOCK - 1) / (2.0 * BLOCK)
            link(v.tensor_scalar(blk[:, :], rank[:, :], 1.0 / BLOCK, -down_half, ALU.mult, ALU.add))
            link(v.tensor_scalar(blk[:, :], blk[:, :], RNE, -RNE, ALU.add, ALU.add))
            link(v.tensor_scalar(extra[:, :], psum[0][:, TT * N_EXP:(TT + 1) * N_EXP], 1.0 / BLOCK, -1.0 / BLOCK - down_half, ALU.mult, ALU.add))
            link(v.tensor_scalar(extra[:, :], extra[:, :], RNE, -RNE, ALU.add, ALU.add))
            link(v.tensor_scalar(extra[:, :], extra[:, :], 0.0, None, ALU.max))
            link(v.tensor_tensor_scan(extra_sum[:, :], extra[:, :], zeros[:, :], 0.0, ALU.add, ALU.add))
            link(v.tensor_tensor(extra_base[:, :], extra_sum[:, :], extra[:, :], ALU.subtract))
            base_of = extra_base[:, :].unsqueeze(1).to_broadcast([P, TT, N_EXP])
            for k in range(TOP_K):
                link(v.tensor_tensor(prod[:, k, :, :], chosen[:, k, :, :], base_of, ALU.mult))
            link(v.tensor_reduce(obase[:, :], prod[:, :, :, :].rearrange("p k t e -> p (k t) e"), AX, ALU.add))
            link(v.tensor_scalar(over[:, :], blk[:, :], 1.0, None, ALU.min))
            link(v.tensor_tensor(item[:, :], obase[:, :], blk[:, :], ALU.add))
            link(v.scalar_tensor_tensor(out=item[:, :], in0=item[:, :], scalar=N_EXP - 1.0, in1=expert[:, :], op0=ALU.add, op1=ALU.subtract))
            link(v.tensor_tensor(item[:, :], item[:, :], over[:, :], ALU.mult))
            link(v.tensor_tensor(item[:, :], item[:, :], expert[:, :], ALU.add))
            link(v.scalar_tensor_tensor(out=slot[:, :], in0=blk[:, :], scalar=-float(BLOCK), in1=rank[:, :], op0=ALU.mult, op1=ALU.add))
            NP = TOP_K * TT
            v.tensor_tensor(hot_slot[:, :, :].rearrange("p n (h s) -> p n h s", h=2),
                            up_slot.unsqueeze(1).unsqueeze(1).to_broadcast([P, NP, 2, BLOCK]),
                            slot[:, :].unsqueeze(2).unsqueeze(3).to_broadcast([P, NP, 2, BLOCK]), ALU.is_equal).then_inc(hot_ready, 1)
            link(v.tensor_tensor(hot_item[:, :, :], up_item.unsqueeze(1).to_broadcast([P, NP, ITEMS]),
                                 item[:, :].unsqueeze(2).to_broadcast([P, NP, ITEMS]), ALU.is_equal))
            v.tensor_tensor(hot_item[:, :, :], hot_item[:, :, :], pair1.unsqueeze(2).to_broadcast([P, NP, ITEMS]), ALU.mult).then_inc(hot_ready, 1)
            link(v.tensor_copy(n_over[:, :], extra_sum[0:1, N_EXP - 1:N_EXP]))
            link(v.tensor_tensor(over_cmp[:, :, :], extra_sum[0:1, :].unsqueeze(1).to_broadcast([1, MAX_OVER, N_EXP]),
                                 up_slot[0:1, 0:MAX_OVER].unsqueeze(2).to_broadcast([1, MAX_OVER, N_EXP]), ALU.is_le))
            link(v.tensor_reduce(over_exp[:, :], over_cmp[:, :, :], AX, ALU.add))
            link(v.tensor_copy(over_exp_i[:, :], over_exp[:, :]))
            v.wait_ge(table_summed, 1)
            link(v.tensor_scalar(table[:, :], psum[1][:, 0:ITEMS], -1.0, half, ALU.add, ALU.add))
            link(v.tensor_scalar(empty[:, :], psum[1][:, 0:ITEMS], 0.0, NO_ROW, ALU.is_equal, ALU.mult))
            link(v.tensor_tensor(table[:, :], table[:, :], empty[:, :], ALU.add))
            link(v.tensor_scalar(table_x[:, :], table[:, :], 2.0 * T, -2.0 * T, ALU.is_ge, ALU.mult))
            link(v.tensor_tensor(x_rows[:, :], table_x[:, :], table[:, :], ALU.add))
            v.tensor_copy(y_rows[:, :], table[:, :]).then_inc(rows_ready, 1)

            v.wait_ge(gexp_ready, 2)
            link(v.tensor_reduce(gsum[:, :], gexp[:, :, :], AX, ALU.add))
            link(v.tensor_scalar(wsum[:, :], vexp[:, :], 1.0, None, ALU.add))
            link(v.tensor_tensor(wsum[:, :], wsum[:, :], gsum[:, :], ALU.mult))
            link(v.reciprocal(weight[:, 0, :], wsum[:, :]))
            v.tensor_tensor(weight[:, 1, :], weight[:, 0, :], vexp[:, :], ALU.mult).then_inc(weights_ready, 1)

            def copy_xT(i, b, lag):
                v.wait_ge(xg_turned, i + 1)
                wait_free(v, gu_summed, i, lag)
                v.tensor_copy(xTg[b][:, :, :], psum[b][:, :].rearrange("p (j m) -> p j m", j=4)).then_inc(xTg_ready, 1)

            def make_hid(i, b, lag):
                v.wait_ge(gated_ready, i + 1)
                wait_free(v, hid_turned, i, lag)
                v.tensor_tensor(hid[b][0:BLOCK, :], gated[b][:, :], psum[2 + b][BLOCK:2 * BLOCK, 0:F], ALU.mult).then_inc(hid_ready, 1)

            def copy_hidT(i, b, lag):
                v.wait_ge(hid_turned, i + 1)
                wait_free(v, dn_summed, i, lag)
                v.tensor_copy(hidT[b][:, :, :], psum[4 + b][:, 0:2 * P].rearrange("p (j m) -> p j m", j=2)[:, :, 0:BLOCK]).then_inc(hidT_ready, 1)

            def dve_item(q, r):
                i = q + r * RING
                if not static(r) or q + 1 < N_EXP:
                    copy_xT(i + 1, (q + 1) % 2, 2)
                make_hid(i, q % 2, 2)
                copy_hidT(i, q % 2, 2)

            v.wait_ge(hid_zero, 2)
            copy_xT(0, 0, 2)
            rounds(v, dve_item)

            def dve_over(j):
                i = j + N_EXP
                copy_xT(i, 0, 1)
                make_hid(i, 0, 1)
                copy_hidT(i, 0, 1)

            overflow(v, dve_over)

            v.wait_ge(h1_in, 16)
            v.wait_ge(weights_ready, 1)

            def combine(t):
                y0, z = pair_y[t][0][:, :], pair_y[t][1]
                v.wait_ge(pairs_in[t], 32)
                v.wait_ge(first_scaled, t + 1)
                link(v.scalar_tensor_tensor(out=y0, in0=h1[:, t, :], scalar=ALPHA, in1=y0, op0=ALU.mult, op1=ALU.add))
                link(v.scalar_tensor_tensor(out=z[:, :], in0=z[:, :], scalar=weight[:, 1, t:t + 1], in1=y0, op0=ALU.mult, op1=ALU.add))
                for h in range(2):
                    link(v.bn_stats(stats[:, t, h, :], z[:, h * H:(h + 1) * H]))
                finish_moments(t, var2_ready, dev2_ready, moments2_ready)

            for t in range(TT):
                combine(t)
            z = pair_y[TT - 1][1][:, 0:H]
            v.wait_ge(normed2, TT)
            v.wait_ge(ln2_in, 32)
            link(v.tensor_tensor(z, z, ln2g[:, 0:H], ALU.mult))
            v.tensor_tensor(z, z, ln2b[:, 0:H], ALU.add).then_inc(out_ready, 1)


_INS = ["x", "w_in", "rg_conv_w", "rg_conv_b", "rg_gate_a_w", "rg_gate_a_b", "rg_gate_x_w", "rg_gate_x_b",
        "rg_lambda", "sc_conv_w", "w_out", "ln1_g", "ln1_b", "router_group_w", "router_group_b",
        "router_expert_w", "router_expert_b", "exp_w_gate", "exp_w_up", "exp_w_down", "ln2_g", "ln2_b"]


def kernel(**inputs):
    import numpy as _np
    import concourse.bacc as _bacc
    from concourse import mybir as _mybir
    from concourse.bass_utils import run_bass_kernel_spmd as _run

    nc = _bacc.Bacc("TRN2", target_bir_lowering=False, num_devices=1)
    arrays, args = {}, []
    for name in _INS:
        a = _np.ascontiguousarray(inputs[name])
        arrays[f"in_{name}"] = a
        args.append(nc.dram_tensor(f"in_{name}", a.shape, _mybir.dt.from_np(a.dtype), kind="ExternalInput").ap())
    shape = tuple(inputs["x"].shape)
    args.append(nc.dram_tensor("out_0", shape, _mybir.dt.float32, kind="ExternalOutput").ap())
    hybrid_moe_layer(nc, *args)
    r = _run(nc, [arrays], core_ids=[0])
    return r.results[0]["out_0"]
```

```python
from contextlib import ExitStack

import concourse.bass as bass
from concourse import mybir

F32 = mybir.dt.float32
F32R = mybir.dt.float32r
BF16 = mybir.dt.bfloat16
U32 = mybir.dt.uint32
I32 = mybir.dt.int32
ALU = mybir.AluOpType
ACT = mybir.ActivationFunctionType
AX = mybir.AxisListType.X

P = 128
BLOCK = 64
RING = 6
FIRST = RING + 1
TOP_K = 2
RG_C = 8.0
LN_EPS = 1e-5
ALPHA = 2.0 ** 0.25
FAR = 1e30
RNE = 12582912.0
NO_ROW = 1048576.0
WARM_UP_START = 28
WARM_UP_COUNTS = 30
WARM_UP_TABLE = 46
WARM_UP_EXPERTS = 50
LOG_TERMS = 9


def hybrid_moe_layer(
    nc, x, w_in, rg_conv_w, rg_conv_b, rg_gate_a_w, rg_gate_a_b, rg_gate_x_w, rg_gate_x_b,
    rg_lambda, sc_conv_w, w_out, ln1_g, ln1_b, router_group_w, router_group_b,
    router_expert_w, router_expert_b, exp_w_gate, exp_w_up, exp_w_down, ln2_g, ln2_b, out,
):
    _, T, D = x.shape
    RG_TAPS, D_RG = rg_conv_w.shape
    SC_TAPS, D_SC = sc_conv_w.shape
    N_GROUPS = router_group_w.shape[1]
    N_EXP, _, F = exp_w_gate.shape
    PER_GROUP = N_EXP // N_GROUPS
    NR = N_GROUPS + N_EXP
    TT = T // P
    KT = D // P
    CT = D_RG // P
    H = D // 2
    CHUNK = 2048
    WCOLS = CHUNK // KT
    N_IN = 5 * D_RG // WCOLS
    N_OUT = D * D // P // CHUNK
    N_CHUNKS = N_IN + N_OUT
    HL = 3
    PER_BLOCK = D_RG // WCOLS
    MAX_OVER = TOP_K * T // BLOCK
    ITEMS = N_EXP + MAX_OVER
    assert T == 512 and D == 1024 and D_RG == D_SC == 512 and F == 256 and N_OUT == 4
    PARAMS = RG_TAPS + 4 + SC_TAPS
    P_RGW, P_RGB, P_AB, P_XB, P_LAM, P_SCW = 0, RG_TAPS, RG_TAPS + 1, RG_TAPS + 2, RG_TAPS + 3, RG_TAPS + 4

    with ExitStack() as ctx:
        base = -(-nc.sbuf_base // 64) * 64
        place = [base]

        def at(name, shape, dt, offset):
            return nc.alloc_sbuf_tensor_at(name, shape, dt, offset=offset)

        def sb(name, shape, dt=F32):
            n = 4 if dt != BF16 else 2
            for s in shape[1:]:
                n *= s
            t = at(name, shape, dt, place[0])
            place[0] += -(-n // 32) * 32
            return t

        ident = sb("ident", [P, P])
        tri = sb("tri", [P, P], BF16)
        ones = sb("ones", [P, P], BF16)
        par = sb("par", [P, CT, PARAMS])
        c8 = sb("c8", [P, CT])
        nc8 = sb("nc8", [P, CT])
        sp = sb("sp", [P, 6, CT])
        wr = sb("wr", [P, KT, NR])
        rbias = sb("rbias", [P, NR])
        stats = sb("stats", [P, TT, 2, 6])
        moments = sb("moments", [P, TT, 2])
        rstd = sb("rstd", [P, TT])
        shift = sb("shift", [P, TT])
        logits = sb("logits", [P, TT, NR])
        gmax = sb("gmax", [P, TT])
        gkey = sb("gkey", [P, TT, N_GROUPS])
        gkmax = sb("gkmax", [P, TT])
        ghot = sb("ghot", [P, TT, N_GROUPS])
        vtop = sb("vtop", [P, TOP_K, TT])
        kkey = sb("kkey", [P, TOP_K, TT])
        chosen_b = sb("chosen_b", [P, TT, N_EXP], BF16)
        rank = sb("rank", [P, TOP_K * TT])
        expert = sb("expert", [P, TOP_K * TT])
        extra = sb("extra", [P, N_EXP])
        extra_sum = sb("extra_sum", [P, N_EXP])
        extra_base = sb("extra_base", [P, N_EXP])
        zeros = sb("zeros", [P, N_EXP])
        obase = sb("obase", [P, TOP_K * TT])
        blk = sb("blk", [P, TOP_K * TT])
        item = sb("item", [P, TOP_K * TT])
        slot = sb("slot", [P, TOP_K * TT])
        x_rows = sb("x_rows", [P, ITEMS], U32)
        y_rows = sb("y_rows", [P, ITEMS], U32)
        x_row_now = sb("x_row_now", [P, 1], U32)
        y_row_now = sb("y_row_now", [P, 1], U32)
        held = sb("held", [P, 1])
        over_exp = sb("over_exp", [1, MAX_OVER])
        over_exp_i = sb("over_exp_i", [1, MAX_OVER], I32)
        n_over = sb("n_over", [1, 1], I32)
        gexp = sb("gexp", [P, TT, N_GROUPS])
        gsum = sb("gsum", [P, TT])
        ptop = sb("ptop", [P, TT])
        vdiff = sb("vdiff", [P, TT])
        vexp = sb("vexp", [P, TT])
        wsum = sb("wsum", [P, TT])
        weight = sb("weight", [P, TOP_K, TT])
        iota_f = sb("iota_f", [P, 160])
        down4, down32 = iota_f[:, 0:N_GROUPS], iota_f[:, 4:4 + N_EXP]
        up_slot = iota_f[:, 36:36 + BLOCK]
        pair1 = iota_f[:, 100:100 + TOP_K * TT]
        half_less_1 = iota_f[:, 108:109]
        up_item = iota_f[:, 112:160]

        first_place = place[0]
        xres = sb("xres", [P, TT, D])
        ln_g = sb("ln_g", [P, D])
        ln_b = sb("ln_b", [P, D])
        wgu_first = at("wgu_first", [P, 2, KT, F], F32, first_place)
        wdn_first = at("wdn_first", [P, 2, D], F32, first_place + 16384)

        shared = place[0]
        xTg = [sb(f"xTg{b}", [P, 4, P]) for b in range(2)]
        gated = [sb(f"gated{b}", [BLOCK, F]) for b in range(2)]
        hid = [sb(f"hid{b}", [P, F]) for b in range(2)]
        hidT = [sb(f"hidT{b}", [P, 2, BLOCK]) for b in range(2)]
        ys = [sb(f"ys{b}", [P, H]) for b in range(4)]
        gelu_g = at("gelu_g", [P, CT, T], F32, shared)
        h1T = [at(f"h1T{b}", [P, KT, P], F32, shared + 4096 * b) for b in range(2)]
        shared_y = shared + 8192
        assert place[0] - shared_y >= 8192

        ring = place[0]
        SLOT = 24576
        wgu = [at(f"wgu{s}", [P, 2, KT, F], F32, ring + s * SLOT) for s in range(RING)]
        wdn = [at(f"wdn{s}", [P, 2, D], F32, ring + s * SLOT + 16384) for s in range(RING)]
        wgu.append(wgu_first)
        wdn.append(wdn_first)
        spare = ring + RING * SLOT
        assert spare + 16384 <= nc.sbuf_usable_end, (spare, nc.sbuf_usable_end)
        raw = [at(f"raw{b}", [P, CHUNK], F32, spare + 8192 * b) for b in range(2)]

        xT_hi = at("xT_hi", [P, KT, T], F32R, ring)
        xT_lo = at("xT_lo", [P, KT, T], F32R, ring + 16384)
        chan = ring + 32768
        PAD = RG_TAPS - 1
        rg_pad = [at(f"rg_pad{j}", [P, PAD + T], F32, chan + 2080 * j) for j in range(CT)]
        assert 2080 * CT <= 8320
        chan += 8320
        sc_c = [at(f"sc_c{j}", [P, T], F32, chan - 8320 + 2080 * j) for j in range(CT)]
        conv = [at(f"conv{j}", [P, T], F32, chan + 2080 * j) for j in range(CT)]
        sc_pad = [at(f"sc_pad{j}", [P, SC_TAPS - 1 + T], F32, chan + 2080 * j) for j in range(CT)]
        chan += 8320
        gr = [at(f"gr{j}", [P, T], F32, chan + 2048 * j) for j in range(CT)]
        sc_conv = [at(f"sc_conv{j}", [P, T], F32, chan + 2048 * j) for j in range(CT)]
        chan += 8192
        gi = [at(f"gi{j}", [P, T], F32, chan + 2048 * j) for j in range(CT)]
        y_sc = [at(f"y_sc{j}", [P, T], F32, chan + 2048 * j) for j in range(CT)]
        chan += 8192
        tanhs = at("tanhs", [P, 3, T], F32, chan)
        chan += 3 * 2048
        assert chan <= ring + 3 * SLOT
        w_hi = [at(f"w_hi{b}", [P, CHUNK], F32R, ring + (3 + b) * SLOT) for b in range(HL)]
        w_lo = [at(f"w_lo{b}", [P, CHUNK], F32R, ring + (3 + b) * SLOT + 8192) for b in range(HL)]
        w_hi = [w_hi[c % HL] for c in range(N_CHUNKS - 1)] + [at("w_hi_last", [P, CHUNK], F32R, spare + 8192 * (N_CHUNKS % 2))]
        w_lo = [w_lo[c % HL] for c in range(N_CHUNKS - 1)] + [at("w_lo_last", [P, CHUNK], F32R, spare + 8192 * (1 - N_CHUNKS % 2))]
        y_at = [ring + (3 + s) * SLOT + 16384 + 4096 * h for s in range(3) for h in range(2)] + [shared_y, shared_y + 4096]
        y_hi = [at(f"y_hi{k}", [P, T], F32R, y_at[k]) for k in range(KT)]
        y_lo = [at(f"y_lo{k}", [P, T], F32R, y_at[k] + 2048) for k in range(KT)]

        par_rows = at("par_rows", [PARAMS, D_RG], F32, shared)
        iota_i = at("iota_i", [P, 160], I32, y_at[5])
        tanh3 = at("tanh3", [P, T], F32, y_at[6])
        wga = at("wga", [P, CT, 64], F32, y_at[7])
        wgx = at("wgx", [P, CT, 64], F32, y_at[7] + 2048)
        th = [tanhs[:, j, :] for j in range(3)] + [tanh3[:, :]]

        h1 = at("h1", [P, TT, D], F32, ring + SLOT)
        ln2g = at("ln2g", [P, D], F32, ring + SLOT + 16384)
        ln2b = at("ln2b", [P, D], F32, ring + SLOT + 20480)
        pair_y = [[at(f"pair_y{k}_{t}", [P, D], F32, ring + 2 * SLOT + 4096 * (TOP_K * t + k)) for k in range(TOP_K)] for t in range(TT)]

        diag = at("diag", [P, 1 + TOP_K * TT, P], F32, ring + 3 * SLOT + 8192)
        xg = [at(f"xg{b}", [P, H], F32, spare + 2048 * b) for b in range(RING)]
        ys += [at(f"ys{b}", [P, H], F32, spare + 2048 * (RING + b - 4)) for b in range(4, RING)]

        assert 4096 + 4 * TOP_K * TT * ITEMS <= RING // 2 * 2048
        hot_slot = at("hot_slot", [P, TOP_K * TT, P], F32R, spare)
        hot_item = at("hot_item", [P, TOP_K * TT, ITEMS], F32R, spare + 4096)
        item_match = at("item_match", [P, TOP_K * TT, ITEMS], F32, spare + 12800)
        over_cmp = at("over_cmp", [1, MAX_OVER, N_EXP], F32, spare + 6144)
        prod = at("prod", [P, TOP_K, TT, N_EXP], F32, spare + 8192)
        chosen = at("chosen", [P, TOP_K, TT, N_EXP], F32, spare + 9216)
        masked = at("masked", [P, TT, N_EXP], F32, spare + 10240)
        masked2 = at("masked2", [P, TT, N_EXP], F32, spare + 10752)
        ekey = at("ekey", [P, TT, N_EXP], F32, spare + 11264)
        table = at("table", [P, ITEMS], F32, spare + 11776)
        table_x = at("table_x", [P, ITEMS], F32, spare + 12032)
        empty = at("empty", [P, ITEMS], F32, spare + 12288)

        DVE_ADDED = 1

        def z_of(t, h):
            return pair_y[t][1][:, h * H:(h + 1) * H] if t < DVE_ADDED else psum[2 * t + h][:, :]

        h1_rows = nc.dram_tensor("h1_rows", (2 * T, H), F32, kind="Internal").ap()
        y_pairs = nc.dram_tensor("y_pairs", (2 * TOP_K * T, H), F32, kind="Internal").ap()

        psum = [ctx.enter_context(nc.psum_tensor(f"bank{b}", [P, 512], F32)) for b in range(8)]

        def sem(name):
            return ctx.enter_context(nc.semaphore(name))

        params_in = sem("params_in")
        gates_in = sem("gates_in")
        x_in = [sem(f"x_in{h}") for h in range(2)]
        raw_in = [sem(f"raw_in{b}") for b in range(2)]
        ln1_in = sem("ln1_in")
        ln2_in = sem("ln2_in")
        router_in = sem("router_in")
        gu_in = [sem(f"gu_in{s}") for s in range(RING + 1)]
        dn_in = [sem(f"dn_in{s}") for s in range(RING + 1)]
        over_gu_in = sem("over_gu_in")
        over_dn_in = sem("over_dn_in")
        ident_done = sem("ident_done")
        const_pool = sem("const_pool")
        const_done = sem("const_done")
        pads_zero = sem("pads_zero")
        par_turned = sem("par_turned")
        par_ready = sem("par_ready")
        x_turned = sem("x_turned")
        xT_hi_ready = sem("xT_hi_ready")
        xT_lo_ready = sem("xT_lo_ready")
        w_hi_ready = sem("w_hi_ready")
        w_lo_ready = sem("w_lo_ready")
        projected = sem("projected")
        act_evacuated = sem("act_evacuated")
        dve_evacuated = sem("dve_evacuated")
        xc_ready = sem("xc_ready")
        gates_summed = sem("gates_summed")
        gates_ready = sem("gates_ready")
        decay_in = sem("decay_in")
        c8_ready = sem("c8_ready")
        lam_abs = sem("lam_abs")
        lam_exp = sem("lam_exp")
        drive_sq = sem("drive_sq")
        drive_root = sem("drive_root")
        y_ready = sem("y_ready")
        y_hi_ready = sem("y_hi_ready")
        y_lo_ready = sem("y_lo_ready")
        out_half = sem("out_half")
        mixed = sem("mixed")
        mixed_used = sem("mixed_used")
        var_ready = sem("var_ready")
        dev_ready = sem("dev_ready")
        h1_ready = sem("h1_ready")
        h1_stored = sem("h1_stored")
        h1_turned = sem("h1_turned")
        h1T_ready = sem("h1T_ready")
        routed = sem("routed")
        logits_summed = sem("logits_summed")
        chosen_ready = sem("chosen_ready")
        counted = sem("counted")
        hot_ready = sem("hot_ready")
        hot_copied = sem("hot_copied")
        table_summed = sem("table_summed")
        rows_ready = sem("rows_ready")
        gdiff_ready = sem("gdiff_ready")
        gexp_ready = sem("gexp_ready")
        weights_ready = sem("weights_ready")
        dve = sem("dve_chain")
        act_chain = sem("act_chain")
        xg_zero = sem("xg_zero")
        hid_zero = sem("hid_zero")
        x_gathered = [sem(f"x_gathered{b}") for b in range(RING)]
        y_scattered = [sem(f"y_scattered{b}") for b in range(RING)]
        over_x = sem("over_x")
        over_y = sem("over_y")
        xg_turned = sem("xg_turned")
        xTg_ready = sem("xTg_ready")
        gu_summed = sem("gu_summed")
        gated_ready = sem("gated_ready")
        hid_ready = sem("hid_ready")
        hid_turned = sem("hid_turned")
        hidT_ready = sem("hidT_ready")
        dn_summed = sem("dn_summed")
        y_copied = sem("y_copied")
        pool_chain = sem("pool_chain")
        pairs_in = [[sem(f"pairs_in{t}_{k}") for k in range(TOP_K)] for t in range(TT)]
        h1_in = sem("h1_in")
        diag_ready = sem("diag_ready")
        z_summed = sem("z_summed")
        var2_ready = sem("var2_ready")
        dev2_ready = sem("dev2_ready")
        moments2_ready = sem("moments2_ready")
        normed2 = sem("normed2")
        out_ready = sem("out_ready")
        out_ready_pool = sem("out_ready_pool")
        out_scaled = sem("out_scaled")
        out_stored = sem("out_stored")

        x_rows_dram = x.rearrange("a t d -> (a t) d")
        out_rows = out.rearrange("a t d -> (a t) d")
        row = lambda v: v.rearrange("(a n) -> a n", a=1)

        BLOCK_ORDER = (0, 1, 3, 4, 2)

        def w_in_chunk(c):
            col = BLOCK_ORDER[c // PER_BLOCK] * D_RG + c % PER_BLOCK * WCOLS
            return w_in[:, col:col + WCOLS].rearrange("(k p) n -> p k n", p=P)

        def w_out_chunk(c):
            h, kh = divmod(c - N_IN, 2)
            return w_out[kh * 512:(kh + 1) * 512, h * 512:(h + 1) * 512].rearrange("(k p) n -> p k n", p=P)

        def chunks_used(eng, n):
            if n <= N_IN:
                eng.wait_ge(projected, 2 * n)
            elif n == N_IN + 1:
                eng.wait_ge(out_half, 1)
            else:
                eng.wait_ge(mixed, TT)

        def static(i):
            return isinstance(i, int)

        def gu_of(w, e):
            w = w[e:e + 1] if static(e) else w[bass.ds(e, 1)]
            return w.rearrange("a (h p j) f -> p (a h) (j f)", h=2, p=P)

        def dn_of(e):
            w = exp_w_down[e:e + 1] if static(e) else exp_w_down[bass.ds(e, 1)]
            return w.rearrange("a (p j) d -> p (a j d)", p=P)

        def gu_place(s, which):
            return wgu[s][:, which, :, :].rearrange("p (h j) f -> p h (j f)", h=2)

        def slot_of(q):
            return q if q < FIRST else (q - 1) % RING

        def loads_of(q, r):
            return r + (1 if q < FIRST else (q - 1) // RING + 1)

        def rounds(engine, body):
            head, turns = FIRST + 1, (N_EXP - 1 - (FIRST + 1)) // RING
            for q in range(head):
                body(q, 0)
            with engine.Fori(0, turns) as r:
                for u in range(RING):
                    body(head + u, r)
            for q in range(head + turns * RING, N_EXP):
                body(q, 0)

        def overflow(engine, body):
            n = engine.value_load(n_over[0:1, 0:1], min_val=0, max_val=MAX_OVER)
            with engine.If(n > 0):
                with engine.Fori(0, n) as j:
                    body(j)

        def before(q, r):
            return r * 16 + 16 * (q // RING) if not static(r) else 16 * (r + q // RING)

        def mains(b):
            return 16 * len(range(b, N_EXP, RING))

        def wait_free(eng, done, i, lag):
            if not static(i) or i >= lag:
                eng.wait_ge(done, i + 1 - lag)

        block = ctx.enter_context(nc.Block())

        @block.sync
        def _(sp_):
            def load_x(h):
                sp_.dma_start(xres[:, :, h * H:(h + 1) * H], x_rows_dram[:, h * H:(h + 1) * H].rearrange("(t p) d -> p t d", p=P)).then_inc(x_in[h], 16)

            for c in range(N_CHUNKS):
                if c == 1:
                    load_x(0)
                    load_x(1)
                if c >= 2:
                    sp_.wait_ge(w_hi_ready, c - 1)
                    sp_.wait_ge(w_lo_ready, c - 1)
                k = KT if c < N_IN else KT // 2
                sp_.dma_start(raw[c % 2][:, :].rearrange("p (k n) -> p k n", k=k),
                              w_in_chunk(c) if c < N_IN else w_out_chunk(c)).then_inc(raw_in[c % 2], 16)

            def load_gu(e, s, done):
                sp_.dma_start(gu_place(s, 0), gu_of(exp_w_gate, e)).then_inc(done, 16)
                sp_.dma_start(gu_place(s, 1), gu_of(exp_w_up, e)).then_inc(done, 16)

            def load_dn(e, s, done):
                sp_.dma_start(wdn[s][:, :, :].rearrange("p j d -> p (j d)"), dn_of(e)).then_inc(done, 16)

            chunks_used(sp_, N_IN)
            load_gu(0, 0, gu_in[0])
            load_dn(0, 0, dn_in[0])
            sp_.wait_ge(y_lo_ready, KT)
            for s in range(1, 3):
                load_gu(s, s, gu_in[s])
                load_dn(s, s, dn_in[s])
            first, second = (3 + c % HL for c in (N_IN, N_IN + 1))
            last, = {3, 4, 5} - {first, second}
            chunks_used(sp_, N_IN + 1)
            load_gu(first, first, gu_in[first])
            chunks_used(sp_, N_IN + 2)
            load_gu(second, second, gu_in[second])
            sp_.wait_ge(mixed, 2 * TT)
            load_gu(last, last, gu_in[last])
            sp_.wait_ge(h1_ready, 2 * TT)
            for s in range(3, RING):
                load_dn(s, s, dn_in[s])

            sp_.wait_ge(h1_turned, 2 * TT)
            sp_.wait_ge(h1_stored, 16 * TT)
            load_gu(RING, RING, gu_in[RING])
            sp_.wait_ge(x_gathered[0], 16)
            load_dn(RING, RING, dn_in[RING])

            def refill(q, r):
                i = q + r * RING
                done = i - RING + (0 if static(r) and q < FIRST + RING else 1)
                s = slot_of(q)
                sp_.wait_ge(gu_summed, done)
                load_gu(i, s, gu_in[s])
                sp_.wait_ge(dn_summed, done)
                load_dn(i, s, dn_in[s])

            for q in range(FIRST, FIRST + RING):
                refill(q, 0)
            with sp_.Fori(0, (N_EXP - FIRST - RING) // RING) as r:
                for u in range(RING):
                    refill(FIRST + RING + u, r)
            for q in range(N_EXP - (N_EXP - FIRST) % RING, N_EXP):
                refill(q, 0)
            last_of_1 = max(q for q in range(N_EXP) if slot_of(q) == 1)
            sp_.wait_ge(dn_summed, last_of_1 + 1)
            sp_.dma_start(h1[:, :, :].rearrange("p t (a h) -> p t a h", a=2),
                          h1_rows.rearrange("(t p a) h -> p t a h", p=P, a=2)).then_inc(h1_in, 16)
            def load_over(j):
                e = sp_.value_load(over_exp_i[0:1, bass.ds(j, 1)], min_val=0, max_val=N_EXP - 1)
                sp_.wait_ge(dn_summed, j + N_EXP)
                load_gu(e, 0, gu_in[0])
                load_dn(e, 0, dn_in[0])

            overflow(sp_, load_over)
            sp_.wait_ge(y_scattered[(N_EXP - 4) % RING], mains((N_EXP - 4) % RING))
            sp_.dma_start(ln2g[:, :], row(ln2_g).to_broadcast([P, D])).then_inc(ln2_in, 16)
            sp_.dma_start(ln2b[:, :], row(ln2_b).to_broadcast([P, D])).then_inc(ln2_in, 16)
            n = sp_.value_load(n_over[0:1, 0:1], min_val=0, max_val=MAX_OVER)
            sp_.wait_ge(y_scattered[0], 16 * n + mains(0))
            for i in range(N_EXP - RING, N_EXP):
                if i % RING:
                    sp_.wait_ge(y_scattered[i % RING], mains(i % RING))
            for t in range(TT):
                for k in range(TOP_K):
                    src = y_pairs[2 * (k * T + t * P):2 * (k * T + (t + 1) * P), :]
                    sp_.dma_start(pair_y[t][k][:, :], src.rearrange("(p a) h -> p (a h)", a=2)).then_inc(pairs_in[t][k], 16)
            for t in range(TT - 1):
                sp_.wait_ge(out_ready_pool, t + 1)
                sp_.wait_ge(out_ready, t + 1)
                sp_.dma_start(out_rows[t * P:(t + 1) * P, :], pair_y[t][1][:, :]).then_inc(out_stored, 16)
            for h in range(2):
                sp_.wait_ge(out_ready, TT + h)
                cols = slice(h * H, (h + 1) * H)
                sp_.dma_start(out_rows[(TT - 1) * P:, cols], pair_y[TT - 1][1][:, cols]).then_inc(out_stored, 16)
            sp_.wait_ge(out_stored, 16 * (TT + 1))

        @block.gpsimd
        def _(pool):
            pool.memset(ident[:, :], 0.0).then_inc(ident_done, 1)
            pool.wait_ge(ident_done, 1)
            pool.affine_select(out=ident[:, :], in_=ident[:, :], compare_op=ALU.not_equal, fill=1.0,
                               base=0, pattern=[[-1, P]], channel_multiplier=1).then_inc(ident_done, 1)
            for w, dst in ((rg_gate_a_w, wga), (rg_gate_x_w, wgx)):
                pool.dma_start(dst[:, :, :], w.rearrange("(a b) i j -> (b i) a j", b=2)).then_inc(gates_in, 16)
            pool.memset(tri[:, :], 1.0).then_inc(const_pool, 1)
            pool.memset(ones[:, :], 1.0).then_inc(const_pool, 1)
            pool.iota(iota_i[:, 0:N_GROUPS], pattern=[[-1, N_GROUPS]], base=N_GROUPS, channel_multiplier=0).then_inc(const_pool, 1)
            pool.iota(iota_i[:, 4:4 + N_EXP], pattern=[[-1, N_EXP]], base=N_EXP, channel_multiplier=0).then_inc(const_pool, 1)
            pool.iota(iota_i[:, 36:36 + BLOCK], pattern=[[1, BLOCK]], base=0, channel_multiplier=0).then_inc(const_pool, 1)
            pool.iota(iota_i[:, 100:108], pattern=[[2 * P, TOP_K * TT]], base=1, channel_multiplier=2).then_inc(const_pool, 1)
            pool.memset(iota_i[:, 108:112], -1).then_inc(const_pool, 1)
            pool.iota(iota_i[:, 112:160], pattern=[[1, ITEMS]], base=0, channel_multiplier=0).then_inc(const_pool, 1)
            pool.wait_ge(const_pool, 8)
            pool.affine_select(out=tri[:, :], in_=tri[:, :], compare_op=ALU.is_gt, fill=0.0,
                               base=0, pattern=[[1, P]], channel_multiplier=-1).then_inc(const_pool, 1)
            pool.wait_ge(const_pool, 9)
            pool.memset(iota_i[64:128, 108:109], 0).then_inc(const_pool, 1)
            pool.wait_ge(const_pool, 10)
            pool.memset(zeros[:, :], 0.0).then_inc(const_pool, 1)
            pool.memset(held[:, :], 1.0).then_inc(pool_chain, 1)
            pool.wait_ge(const_pool, 11)
            pool.tensor_copy(iota_f[:, :], iota_i[:, :]).then_inc(const_done, 1)
            for j in range(CT):
                pool.memset(rg_pad[j][:, 0:PAD], 0.0).then_inc(pads_zero, 1)
            pool.dma_start(ln_g[:, :], row(ln1_g).to_broadcast([P, D])).then_inc(ln1_in, 16)
            pool.dma_start(ln_b[:, :], row(ln1_b).to_broadcast([P, D])).then_inc(ln1_in, 16)
            pool.dma_start(wr[:, :, 0:N_GROUPS], router_group_w.rearrange("(k p) n -> p k n", p=P)).then_inc(router_in, 16)
            pool.dma_start(wr[:, :, N_GROUPS:NR], router_expert_w.rearrange("(k p) n -> p k n", p=P)).then_inc(router_in, 16)
            pool.dma_start(rbias[:, 0:N_GROUPS], row(router_group_b).to_broadcast([P, N_GROUPS])).then_inc(router_in, 16)
            pool.dma_start(rbias[:, N_GROUPS:NR], row(router_expert_b).to_broadcast([P, N_EXP])).then_inc(router_in, 16)
            pool.wait_ge(y_ready, CT)
            for j in range(CT):
                pool.memset(sc_pad[j][:, 0:SC_TAPS - 1], 0.0).then_inc(pads_zero, 1)
            for t in range(TT):
                pool.wait_ge(h1_ready, 2 * t + 2)
                pool.dma_start(h1_rows[2 * t * P:2 * (t + 1) * P, :].rearrange("(p a) h -> p (a h)", a=2), xres[:, t, :]).then_inc(h1_stored, 16)
            pool.wait_ge(routed, TT)
            for b in range(2):
                pool.memset(hid[b][:, :], 0.0).then_inc(hid_zero, 1)
            pool.wait_ge(table_summed, 1)
            for b in range(RING // 2):
                pool.memset(xg[b][:, :], 0.0).then_inc(xg_zero, 1)
            pool.wait_ge(xg_zero, RING // 2)
            pool.wait_ge(rows_ready, 1)
            pool.wait_ge(h1_stored, 16 * TT)

            def gather(b, rows):
                pool.indirect_dma_start(out=xg[b][:, :], out_offset=None, in_=h1_rows,
                                        in_offset=bass.IndirectOffsetOnAxis(ap=rows, axis=0),
                                        bounds_check=2 * T - 1, oob_is_err=False).then_inc(x_gathered[b], 16)

            def scatter(b, rows):
                pool.indirect_dma_start(out=y_pairs, out_offset=bass.IndirectOffsetOnAxis(ap=rows, axis=0),
                                        in_=ys[b][:, :], in_offset=None,
                                        bounds_check=2 * TOP_K * T - 1, oob_is_err=False).then_inc(y_scattered[b], 16)

            for i in range(RING):
                if i == RING // 2:
                    for b in range(RING // 2, RING):
                        pool.memset(xg[b][:, :], 0.0).then_inc(xg_zero, 1)
                    pool.wait_ge(xg_zero, RING)
                gather(i, x_rows[:, i:i + 1])
            SCATTER_LAG = 2
            for i in range(N_EXP + SCATTER_LAG):
                if i + RING < N_EXP:
                    pool.wait_ge(xg_turned, i + 1)
                    gather(i % RING, x_rows[:, i + RING:i + RING + 1])
                done = i - SCATTER_LAG
                if done >= 0:
                    pool.wait_ge(y_copied, done + 1)
                    scatter(done % RING, y_rows[:, done:done + 1])

            def over_rows(j):
                i, n = j + N_EXP, j * 5
                pool.wait_ge(pool_chain, n + 1)
                pool.tensor_tensor(held[:, :], held[:, :], held[:, :], ALU.mult).then_inc(pool_chain, 1)
                pool.tensor_copy(x_row_now[:, :], x_rows[:, bass.ds(i, 1)]).then_inc(pool_chain, 1)
                pool.tensor_copy(y_row_now[:, :], y_rows[:, bass.ds(i, 1)]).then_inc(pool_chain, 1)
                pool.wait_ge(pool_chain, n + 4)
                pool.wait_ge(xg_turned, i)
                pool.tensor_tensor(held[:, :], held[:, :], held[:, :], ALU.mult).then_inc(pool_chain, 1)
                gather(0, x_row_now[:, :])
                pool.wait_ge(pool_chain, n + 5)
                pool.wait_ge(y_copied, i + 1)
                pool.tensor_tensor(held[:, :], held[:, :], held[:, :], ALU.mult).then_inc(pool_chain, 1)
                scatter(0, y_row_now[:, :])
                pool.wait_ge(y_scattered[0], 16 * j + 16 + mains(0))
                pool.wait_ge(pool_chain, n + 6)

            overflow(pool, over_rows)

            pool.wait_ge(ln2_in, 32)
            for t in range(TT - 1):
                z = pair_y[t][1][:, 0:H]
                pool.wait_ge(normed2, t + 1)
                pool.tensor_tensor(z, z, ln2g[:, 0:H], ALU.mult).then_inc(out_scaled, 1)
                pool.wait_ge(out_scaled, t + 1)
                pool.tensor_tensor(z, z, ln2b[:, 0:H], ALU.add).then_inc(out_ready_pool, 1)

        @block.scalar
        def _(act):
            for n, v in enumerate((rg_conv_w, row(rg_conv_b), row(rg_gate_a_b), row(rg_gate_x_b), row(rg_lambda), sc_conv_w)):
                at_row = (P_RGW, P_RGB, P_AB, P_XB, P_LAM, P_SCW)[n]
                act.dma_start(par_rows[at_row:at_row + v.shape[0], :], v).then_inc(params_in, 16)

            def split_hi(c):
                act.wait_ge(raw_in[c % 2], 16 * (c // 2 + 1))
                if c == N_CHUNKS - 1:
                    act.wait_ge(w_lo_ready, c)
                elif c >= HL:
                    chunks_used(act, c - HL + 1)
                act.activation(w_hi[c][:, :], raw[c % 2][:, :], ACT.Copy).then_inc(w_hi_ready, 1)

            split_hi(0)
            for k in range(KT):
                act.wait_ge(x_turned, k + 1)
                act.activation(xT_hi[:, k, :], psum[k][:, :], ACT.Copy).then_inc(xT_hi_ready, 1)

            def evacuate(c, func, dst):
                for n in range(2):
                    act.wait_ge(projected, 2 * c + n + 1)
                    act.activation(dst[2 * (c % 2) + n], psum[(2 * c + n) % 4][:, :], func).then_inc(act_evacuated, 1)

            def y_split_hi(k, src):
                act.wait_ge(y_ready, k + 1)
                act.activation(y_hi[k][:, :], src, ACT.Copy).then_inc(y_hi_ready, 1)

            split_hi(1)
            act.wait_ge(par_ready, 1)
            act.activation(sp[:, 0, :], par[:, :, P_LAM], ACT.Abs).then_inc(lam_abs, 1)
            act.wait_ge(lam_abs, 1)
            act.activation(sp[:, 1, :], sp[:, 0, :], ACT.Exp, scale=-1.0).then_inc(lam_exp, 1)
            pad_dst = [t[:, PAD:PAD + T] for t in rg_pad]
            for s in range(N_CHUNKS - 2):
                split_hi(s + 2)
                if s in (1, 2):
                    evacuate(s - 1, ACT.Copy, pad_dst)
                if s in (3, 4):
                    evacuate(s - 1, ACT.Gelu_apprx_tanh, [gelu_g[:, j, :] for j in range(CT)])
                if s in (4, 5):
                    if s == 5:
                        act.wait_ge(xc_ready, CT)
                        evacuate(s - 1, ACT.Copy, [t[:, :] for t in sc_c])
                    for j in range(2 * s - 8, 2 * s - 6):
                        act.wait_ge(gates_summed, j + 1)
                        act.activation(gr[j][:, :], psum[4 + 2 * (j % 2)][:, :], ACT.Sigmoid, bias=par[:, j, P_AB:P_AB + 1]).then_inc(gates_ready, 1)
                        act.activation(gi[j][:, :], psum[5 + 2 * (j % 2)][:, :], ACT.Sigmoid, bias=par[:, j, P_XB:P_XB + 1]).then_inc(gates_ready, 1)
                if s == 6:
                    for j in range(CT):
                        act.wait_ge(drive_sq, j + 1)
                        act.activation(conv[j][:, 0:T], conv[j][:, 0:T], ACT.Sqrt).then_inc(drive_root, 1)
                if s == 6:
                    evacuate(s - 1, ACT.Copy, [t[:, :] for t in sc_c])
                if s == 5:
                    act.wait_ge(c8_ready, 1)
                    for j in range(CT):
                        act.wait_ge(gates_ready, 2 * j + 1)
                        act.activation(th[j], gr[j][:, :], ACT.Tanh, scale=nc8[:, j:j + 1]).then_inc(act_chain, 1)
                        act.wait_ge(act_chain, j + 1)
                        act.activation(gr[j][:, :], gr[j][:, :], ACT.Exp, scale=c8[:, j:j + 1]).then_inc(decay_in, 1)
                if s == 7:
                    for j in range(CT):
                        y_split_hi(j, th[j])
                if s == 10:
                    for j in range(CT):
                        y_split_hi(CT + j, y_sc[j][:, :])
            def copy_h1T(t):
                for n in range(2):
                    act.wait_ge(h1_turned, 2 * t + n + 1)
                    if t >= 2:
                        act.wait_ge(logits_summed, t - 1)
                    act.activation(h1T[t % 2][:, 4 * n:4 * n + 4, :], psum[4 + 2 * (t % 2) + n][:, :], ACT.Copy).then_inc(h1T_ready, 1)

            for t in range(TT):
                act.wait_ge(var_ready, t + 1)
                act.activation(rstd[:, t:t + 1], rstd[:, t:t + 1], ACT.Sqrt).then_inc(dev_ready, 1)
                if t >= 1:
                    copy_h1T(t - 1)
            copy_h1T(TT - 1)
            act.wait_ge(gdiff_ready, 2)
            act.activation(gexp[:, :, :], gexp[:, :, :], ACT.Exp).then_inc(gexp_ready, 1)
            act.activation(vexp[:, :], vdiff[:, :], ACT.Exp).then_inc(gexp_ready, 1)
            act.wait_ge(hot_ready, 1)
            act.activation(hot_slot[:, :, BLOCK:P], hot_slot[:, :, 0:BLOCK], ACT.Copy).then_inc(hot_copied, 1)

            def gate(i, b, lag):
                act.wait_ge(gu_summed, i + 1)
                wait_free(act, hid_ready, i, lag)
                act.activation(gated[b][:, :], psum[2 + b][0:BLOCK, 0:F], ACT.Silu).then_inc(gated_ready, 1)

            def copy_y(i, b, yb, scattered):
                act.wait_ge(dn_summed, i + 1)
                if not static(scattered) or scattered > 0:
                    act.wait_ge(y_scattered[yb], scattered)
                act.activation(ys[yb][:, :], psum[6 + b][:, :], ACT.Copy).then_inc(y_copied, 1)

            def copy_main_y(q, r):
                copy_y(q + r * RING, q % 2, q % RING, before(q, r))

            def act_item(q, r):
                if q == N_EXP - 1:
                    copy_main_y(q - 1, r)
                gate(q + r * RING, q % 2, 2)
                if 1 <= q < N_EXP - 1:
                    copy_main_y(q - 1, r)

            rounds(act, act_item)
            copy_main_y(N_EXP - 1, 0)

            def act_over(j):
                gate(j + N_EXP, 0, 1)
                copy_y(j + N_EXP, 0, 0, 16 * j + mains(0))

            overflow(act, act_over)
            act.activation(diag[:, 0, :], ident[:, :], ACT.Copy, scale=ALPHA).then_inc(diag_ready, 1)
            act.wait_ge(weights_ready, 1)
            for t in range(TT):
                for k in range(TOP_K):
                    act.activation(diag[:, 1 + TOP_K * t + k, :], ident[:, :], ACT.Copy, scale=weight[:, k, t:t + 1]).then_inc(diag_ready, 1)
            for t in range(TT):
                act.wait_ge(var2_ready, t + 1)
                act.activation(rstd[:, t:t + 1], rstd[:, t:t + 1], ACT.Sqrt).then_inc(dev2_ready, 1)
                if t < TT - 1:
                    act.wait_ge(moments2_ready, t + 1)
                    act.activation(pair_y[t][1][:, 0:H], z_of(t, 0), ACT.Identity,
                                   bias=shift[:, t:t + 1], scale=rstd[:, t:t + 1]).then_inc(normed2, 1)

        @block.tensor
        def _(pe):
            def keep_busy(bank, n):
                for _ in range(n):
                    pe.transpose(bank[:, 0:P], ident[:, :], ident[:, :])

            pe.wait_ge(ident_done, 2)
            keep_busy(psum[7], WARM_UP_START)

            def turn_x_columns(h):
                pe.wait_ge(x_in[h], 16)
                for k in range(h * KT // 2, (h + 1) * KT // 2):
                    for t in range(TT):
                        mm = pe.transpose(psum[k][:, t * P:(t + 1) * P], xres[:, t, k * P:(k + 1) * P], ident[:, :])
                    mm.then_inc(x_turned, 1)

            turn_x_columns(0)

            def products(dst, a_hi, a_lo, b_hi, b_lo, start, stop):
                pe.matmul(dst, a_hi, b_hi, start=start, stop=False)
                pe.matmul(dst, a_hi, b_lo, start=False, stop=False)
                return pe.matmul(dst, a_lo, b_hi, start=False, stop=stop)

            for c in range(N_IN):
                hi, lo = (w[c][:, :].rearrange("p (k n) -> p k n", k=KT) for w in (w_hi, w_lo))
                pe.wait_ge(w_hi_ready, c + 1)
                pe.wait_ge(w_lo_ready, c + 1)
                for n in range(2):
                    if c < 2:
                        pe.wait_ge(xT_lo_ready, 2 * c + n + 1)
                    elif c < 8:
                        pe.wait_ge(act_evacuated, 2 * (c - 2) + n + 1)
                    else:
                        pe.wait_ge(dve_evacuated, 2 * (c - 8) + n + 1)
                    bank = psum[(2 * c + n) % 4]
                    for k in range(KT):
                        if c == 0 and n == 0:
                            if k == KT // 4:
                                turn_x_columns(1)
                            pe.wait_ge(xT_hi_ready, k + 1)
                            pe.wait_ge(xT_lo_ready, k + 1)
                        mm = products(bank[:, :], hi[:, k, n * P:(n + 1) * P], lo[:, k, n * P:(n + 1) * P],
                                      xT_hi[:, k, :], xT_lo[:, k, :], k == 0, k == KT - 1)
                    mm.then_inc(projected, 1)
                if c == 0:
                    pe.wait_ge(params_in, 16 * 6)
                    for j in range(CT):
                        mm = pe.transpose(psum[7][:, j * PARAMS:(j + 1) * PARAMS], par_rows[:, j * P:(j + 1) * P], ident[0:PARAMS, 0:PARAMS])
                    mm.then_inc(par_turned, 1)
                if c in (3, 4):
                    pe.wait_ge(gates_in, 32)
                    for j in range(2 * c - 6, 2 * c - 4):
                        pe.wait_ge(xc_ready, j + 1)
                        if j >= 2:
                            pe.wait_ge(gates_ready, 2 * (j - 2) + 2)
                        for w, bank in ((wga, psum[4 + 2 * (j % 2)]), (wgx, psum[5 + 2 * (j % 2)])):
                            for q in range(2):
                                h = slice(64 * q, 64 * q + 64)
                                mm = pe.matmul(bank[h, :], w[h, j, :], conv[j][h, :], start=True, stop=True)
                        mm.then_inc(gates_summed, 1)

            def out_products(c, t, first, last):
                hi, lo = (w[c][:, :].rearrange("p (k n) -> p k n", k=4) for w in (w_hi, w_lo))
                kh = (c - N_IN) % 2
                bank = psum[(4 if c - N_IN < 2 else 0) + t]
                for k in range(4):
                    y = slice(t * P, (t + 1) * P)
                    mm = products(bank[:, :], y_hi[4 * kh + k][:, y], y_lo[4 * kh + k][:, y], hi[:, k, :], lo[:, k, :],
                                  first and k == 0, last and k == 3)
                return mm

            for c in (N_IN, N_IN + 1):
                pe.wait_ge(w_hi_ready, c + 1)
                pe.wait_ge(w_lo_ready, c + 1)
                kh = (c - N_IN) % 2
                pe.wait_ge(y_hi_ready, CT * (kh + 1))
                pe.wait_ge(y_lo_ready, CT * (kh + 1))
                for t in range(TT):
                    mm = out_products(c, t, kh == 0, kh == 1)
                    if kh == 1:
                        mm.then_inc(mixed, 1)
                    elif t == TT - 1:
                        mm.then_inc(out_half, 1)
            for c in (N_IN + 2, N_IN + 3):
                pe.wait_ge(w_hi_ready, c + 1)
                pe.wait_ge(w_lo_ready, c + 1)

            def turn_h1(t):
                if t >= 2:
                    pe.wait_ge(h1T_ready, 2 * (t - 1))
                for n in range(2):
                    pe.wait_ge(h1_ready, 2 * t + n + 1)
                    for k in range(4):
                        mm = pe.transpose(psum[4 + 2 * (t % 2) + n][:, k * P:(k + 1) * P], xres[:, t, (4 * n + k) * P:(4 * n + k + 1) * P], ident[:, :])
                    mm.then_inc(h1_turned, 1)

            def router(t):
                if t == 0:
                    pe.wait_ge(router_in, 16 * 4)
                pe.wait_ge(h1T_ready, 2 * t + 2)
                for k in range(KT):
                    for q in range(2):
                        toks = slice(64 * q, 64 * q + 64)
                        mm = pe.matmul(psum[t][toks, 0:NR], h1T[t % 2][:, k, toks], wr[:, k, :], start=k == 0, stop=k == KT - 1)
                mm.then_inc(logits_summed, 1)

            for t in range(TT):
                out_products(N_IN + 2, t, True, False)
                out_products(N_IN + 3, t, False, True).then_inc(mixed, 1)
                if t >= 2:
                    turn_h1(t - 2)
                if t >= 3:
                    router(t - 3)
            turn_h1(TT - 2)
            router(TT - 3)
            router(TT - 2)
            turn_h1(TT - 1)
            router(TT - 1)

            keep_busy(psum[7], WARM_UP_COUNTS)
            pe.wait_ge(chosen_ready, 1)
            for t in range(TT + 1):
                dst = psum[0][:, t * N_EXP:(t + 1) * N_EXP]
                for q in range(min(t, TT)):
                    mm = pe.matmul(dst, ones[:, :], chosen_b[:, q, :], start=q == 0, stop=t == TT and q == TT - 1)
                if t < TT:
                    mm = pe.matmul(dst, tri[:, :], chosen_b[:, t, :], start=t == 0, stop=True)
            mm.then_inc(counted, 1)
            keep_busy(psum[7], WARM_UP_TABLE)
            pe.wait_ge(hot_ready, 2)
            pe.wait_ge(hot_copied, 1)
            for n in range(TOP_K * TT):
                mm = pe.matmul(psum[1][:, 0:ITEMS], hot_slot[:, n, :], hot_item[:, n, :], start=n == 0, stop=n == TOP_K * TT - 1)
            mm.then_inc(table_summed, 1)

            def turn_x(i, b, g, lag, gathered):
                pe.wait_ge(x_gathered[g], gathered)
                wait_free(pe, xTg_ready, i, lag)
                for j in range(4):
                    rows = xg[g][:, :].rearrange("p (m j) -> p j m", j=4)[:, j, :]
                    mm = pe.transpose(psum[b][:, j * P:(j + 1) * P], rows, ident[:, :])
                mm.then_inc(xg_turned, 1)

            def gate_up(i, s, b, lag, loads):
                pe.wait_ge(gu_in[s], 32 * loads)
                pe.wait_ge(xTg_ready, i + 1)
                wait_free(pe, hid_ready, i, lag)
                for k in range(KT):
                    h, j = divmod(k, 4)
                    for which in range(2):
                        mm = pe.matmul(psum[2 + b][BLOCK * which:BLOCK * which + BLOCK, 0:F],
                                       xTg[b][:, j, h * BLOCK:(h + 1) * BLOCK], wgu[s][:, which, k, :],
                                       start=k == 0, stop=k == KT - 1)
                mm.then_inc(gu_summed, 1)

            def turn_hid(i, b, lag):
                pe.wait_ge(hid_ready, i + 1)
                wait_free(pe, hidT_ready, i, lag)
                for j in range(2):
                    cols = hid[b][:, :].rearrange("p (m j) -> p j m", j=2)[:, j, :]
                    mm = pe.transpose(psum[4 + b][:, j * P:(j + 1) * P], cols, ident[:, :])
                mm.then_inc(hid_turned, 1)

            def down(i, s, b, lag, loads):
                pe.wait_ge(dn_in[s], 16 * loads)
                pe.wait_ge(hidT_ready, i + 1)
                wait_free(pe, y_copied, i, lag)
                for j in range(2):
                    for n in range(2):
                        mm = pe.matmul(psum[6 + b][BLOCK * n:BLOCK * n + BLOCK, :], hidT[b][:, j, :],
                                       wdn[s][:, j, n * H:(n + 1) * H], start=j == 0, stop=j == 1)
                mm.then_inc(dn_summed, 1)

            def turn_main_x(q, r):
                turn_x(q + r * RING, q % 2, q % RING, 2, before(q, r) + 16)

            def main_down(q, r):
                down(q + r * RING, slot_of(q), q % 2, 2, loads_of(q, r))

            def pe_item(q, r):
                if q > 0 and (not static(r) or q + 1 < N_EXP):
                    turn_main_x(q + 1, r)
                if q == N_EXP - 1:
                    main_down(q - 1, r)
                gate_up(q + r * RING, slot_of(q), q % 2, 2, loads_of(q, r))
                if q == 0:
                    turn_main_x(1, 0)
                if 1 <= q < N_EXP - 1:
                    main_down(q - 1, r)
                turn_hid(q + r * RING, q % 2, 2)

            keep_busy(psum[7], WARM_UP_EXPERTS)
            turn_main_x(0, 0)
            rounds(pe, pe_item)
            main_down(N_EXP - 1, 0)

            def pe_over(j):
                i, loads = j + N_EXP, j + 1 + sum(slot_of(q) == 0 for q in range(N_EXP))
                turn_x(i, 0, 0, 1, 16 * j + 16 + mains(0))
                gate_up(i, 0, 0, 1, loads)
                turn_hid(i, 0, 1)
                down(i, 0, 0, 1, loads)

            overflow(pe, pe_over)

            n = pe.value_load(n_over[0:1, 0:1], min_val=0, max_val=MAX_OVER)
            pe.wait_ge(y_copied, n + N_EXP)
            pe.wait_ge(h1_in, 16)
            pe.wait_ge(diag_ready, 1)
            for t in range(TT):
                for h in range(2):
                    pe.matmul(psum[2 * t + h][:, :], diag[:, 0, :], h1[:, t, h * H:(h + 1) * H], start=True, stop=False)
            pe.wait_ge(diag_ready, 1 + TOP_K * TT)
            for t in range(TT):
                last = 0 if t < DVE_ADDED else TOP_K - 1
                for k in range(last + 1):
                    pe.wait_ge(pairs_in[t][k], 16)
                    for h in range(2):
                        mm = pe.matmul(psum[2 * t + h][:, :], diag[:, 1 + TOP_K * t + k, :], pair_y[t][k][:, h * H:(h + 1) * H],
                                       start=False, stop=k == last)
                        if k == last:
                            mm.then_inc(z_summed, 1)

        @block.vector
        def _(dve_):
            v = dve_
            chain = [0]

            def link(ins):
                chain[0] += 1
                ins.then_inc(dve, 1)
                v.wait_ge(dve, chain[0])

            def split_lo(c):
                v.wait_ge(w_hi_ready, c + 1)
                v.tensor_tensor(w_lo[c][:, :], raw[c % 2][:, :], w_hi[c][:, :], ALU.subtract).then_inc(w_lo_ready, 1)

            def step(ins):
                chain[0] += 1
                ins.then_inc(dve, 1)

            def before_last():
                v.wait_ge(dve, chain[0] - 1)

            split_lo(0)
            for k in range(KT):
                v.wait_ge(xT_hi_ready, k + 1)
                v.tensor_tensor(xT_lo[:, k, :], psum[k][:, :], xT_hi[:, k, :], ALU.subtract).then_inc(xT_lo_ready, 1)

            split_lo(1)
            v.wait_ge(par_turned, 1)
            v.tensor_copy(par[:, :, :], psum[7][:, 0:CT * PARAMS].rearrange("p (j n) -> p j n", j=CT)).then_inc(par_ready, 1)
            v.wait_ge(par_ready, 1)
            lam = par[:, :, P_LAM]

            v.wait_ge(lam_exp, 1)
            e, q, q2, ser, tmp = sp[:, 1, :], sp[:, 2, :], sp[:, 3, :], sp[:, 4, :], sp[:, 5, :]
            link(v.tensor_scalar(tmp, e, 2.0, None, ALU.add))
            link(v.reciprocal(tmp, tmp))
            link(v.tensor_tensor(q, e, tmp, ALU.mult))
            link(v.tensor_tensor(q2, q, q, ALU.mult))
            link(v.tensor_scalar(ser, q2, 1.0 / (2 * LOG_TERMS + 1), None, ALU.mult))
            for n in range(LOG_TERMS - 1, 0, -1):
                link(v.scalar_tensor_tensor(out=ser, in0=ser, scalar=1.0 / (2 * n + 1), in1=q2, op0=ALU.add, op1=ALU.mult))
            link(v.scalar_tensor_tensor(out=ser, in0=ser, scalar=1.0, in1=q, op0=ALU.add, op1=ALU.mult))
            link(v.tensor_scalar(tmp, lam, -1.0, 0.0, ALU.mult, ALU.max))
            link(v.scalar_tensor_tensor(out=tmp, in0=ser, scalar=2.0, in1=tmp, op0=ALU.mult, op1=ALU.add))
            link(v.tensor_scalar(nc8[:, :], tmp, RG_C, None, ALU.mult))
            v.tensor_scalar(c8[:, :], tmp, -RG_C, None, ALU.mult).then_inc(c8_ready, 1)

            def taps(dst, src, j, first, n, bias, done=None):
                w = lambda i: par[:, j, first + i:first + i + 1]
                if bias is None:
                    link(v.tensor_scalar(dst, src(n - 1), w(n - 1), None, ALU.mult))
                else:
                    link(v.tensor_scalar(dst, src(n - 1), w(n - 1), bias, ALU.mult, ALU.add))
                for i in range(n - 1):
                    ins = v.scalar_tensor_tensor(out=dst, in0=src(i), scalar=w(i), in1=dst, op0=ALU.mult, op1=ALU.add)
                    if i == n - 2 and done is not None:
                        ins.then_inc(done, 1)
                    else:
                        link(ins)

            def rg_conv(j):
                v.wait_ge(act_evacuated, j + 1)
                v.wait_ge(pads_zero, j + 1)
                taps(conv[j][:, 0:T], lambda i: rg_pad[j][:, i:i + T], j, P_RGW, RG_TAPS, par[:, j, P_RGB:P_RGB + 1], xc_ready)

            def drive(j):
                a, u, m = gr[j][:, :], gi[j][:, :], conv[j][:, 0:T]
                v.wait_ge(decay_in, j + 1)
                link(v.tensor_tensor(u, u, m, ALU.mult))
                link(v.tensor_tensor(m, a, a, ALU.mult))
                v.scalar_tensor_tensor(out=m, in0=m, scalar=1.0, in1=th[j], op0=ALU.add, op1=ALU.mult).then_inc(drive_sq, 1)

            def recurrence(j):
                a, u, m = gr[j][:, :], gi[j][:, :], conv[j][:, 0:T]
                v.wait_ge(drive_root, j + 1)
                link(v.tensor_tensor(u, u, m, ALU.mult))
                link(v.tensor_tensor_scan(m, a, u, 0.0, ALU.mult, ALU.add))
                v.tensor_tensor(th[j], m, gelu_g[:, j, :], ALU.mult).then_inc(y_ready, 1)

            def short_conv(j):
                v.wait_ge(projected, 12 + j + 1)
                v.wait_ge(act_evacuated, 8 + j + 1)
                v.wait_ge(pads_zero, CT + j + 1)
                v.tensor_tensor(sc_pad[j][:, SC_TAPS - 1:SC_TAPS - 1 + T], psum[j % 4][:, :], sc_c[j][:, :], ALU.mult).then_inc(dve_evacuated, 1)
                v.wait_ge(dve_evacuated, j + 1)
                taps(sc_conv[j][:, :], lambda i: sc_pad[j][:, i:i + T], j, P_SCW, SC_TAPS, None)

            def y_short(j):
                v.wait_ge(projected, 16 + j + 1)
                v.tensor_tensor(y_sc[j][:, :], psum[j % 4][:, :], sc_conv[j][:, :], ALU.mult).then_inc(y_ready, 1)

            def y_split_lo(k, src):
                v.wait_ge(y_hi_ready, k + 1)
                v.tensor_tensor(y_lo[k][:, :], src, y_hi[k][:, :], ALU.subtract).then_inc(y_lo_ready, 1)

            for s in range(N_CHUNKS - 2):
                split_lo(s + 2)
                if s in (1, 2):
                    rg_conv(2 * s - 2)
                    rg_conv(2 * s - 1)
                if s == 5:
                    for j in range(CT):
                        drive(j)
                if s == 6:
                    for j in range(CT):
                        recurrence(j)
                if s == 7:
                    for j in range(CT):
                        y_split_lo(j, th[j])
                if s in (7, 8):
                    short_conv(2 * s - 14)
                    short_conv(2 * s - 13)
                if s in (9, 10):
                    y_short(2 * s - 18)
                    y_short(2 * s - 17)
                if s == 10:
                    for j in range(CT):
                        y_split_lo(CT + j, y_sc[j][:, :])

            def residual(n):
                h, t = divmod(n, TT)
                part = xres[:, t, h * H:(h + 1) * H]
                v.wait_ge(mixed, n + 1)
                link(v.scalar_tensor_tensor(out=part, in0=part, scalar=ALPHA, in1=psum[(4, 0)[h] + t][:, :], op0=ALU.mult, op1=ALU.add))
                link(v.bn_stats(stats[:, t, h, :], part))

            def take_moments(t, var_done):
                link(v.bn_aggr(moments[:, t, :], stats[:, t, :, :]))
                v.tensor_scalar(rstd[:, t:t + 1], moments[:, t, 1:2], LN_EPS, None, ALU.add).then_inc(var_done, 1)

            def take_logits(t):
                v.wait_ge(logits_summed, t + 1)
                v.tensor_tensor(logits[:, t, :], psum[t][:, 0:NR], rbias[:, :], ALU.add).then_inc(routed, 1)

            for t in range(TT):
                residual(t)
            v.wait_ge(ln1_in, 32)
            for t in range(TT):
                residual(TT + t)
                take_moments(t, var_ready)
                link(v.scalar_tensor_tensor(out=xres[:, t, :], in0=xres[:, t, :], scalar=moments[:, t, 0:1], in1=ln_g[:, :], op0=ALU.subtract, op1=ALU.mult))
                v.wait_ge(dev_ready, t + 1)
                link(v.reciprocal(rstd[:, t:t + 1], rstd[:, t:t + 1]))
                for h in range(2):
                    part = xres[:, t, h * H:(h + 1) * H]
                    v.scalar_tensor_tensor(out=part, in0=part, scalar=rstd[:, t:t + 1], in1=ln_b[:, h * H:(h + 1) * H],
                                           op0=ALU.mult, op1=ALU.add).then_inc(h1_ready, 1)
                if t == 0:
                    v.wait_ge(router_in, 16 * 4)
                if t == TT - 1:
                    take_logits(0)
            for t in range(1, TT):
                take_logits(t)
            v.wait_ge(routed, TT)

            v.wait_ge(const_done, 1)
            over_n = lambda ap, n: ap.unsqueeze(2).to_broadcast([P, TT // 2, n])
            down_of = lambda key, n: key.unsqueeze(1).to_broadcast([P, TT // 2, n])
            HALVES = [slice(0, TT // 2), slice(TT // 2, TT)]
            by_group = lambda ap: ap.rearrange("p t (g n) -> p t g n", g=N_GROUPS)

            def in_halves(instruction):
                for ts in HALVES:
                    before_last()
                    step(instruction(ts))

            def first_max(values, top, key, key_top, hot, key_down, n):
                in_halves(lambda ts: v.tensor_reduce(top[:, ts], values[:, ts, :], AX, ALU.max))
                in_halves(lambda ts: v.tensor_tensor(key[:, ts, :], values[:, ts, :], over_n(top[:, ts], n), ALU.is_equal))
                in_halves(lambda ts: v.tensor_tensor(key[:, ts, :], key[:, ts, :], down_of(key_down, n), ALU.mult))
                in_halves(lambda ts: v.tensor_reduce(key_top[:, ts], key[:, ts, :], AX, ALU.max))
                in_halves(lambda ts: v.tensor_tensor(hot[:, ts, :], key[:, ts, :], over_n(key_top[:, ts], n), ALU.is_equal))

            first_max(logits[:, :, 0:N_GROUPS], gmax, gkey, gkmax, ghot, down4, N_GROUPS)
            in_halves(lambda ts: v.tensor_scalar(gkey[:, ts, :], ghot[:, ts, :], -1.0, FAR, ALU.add, ALU.mult))
            in_halves(lambda ts: v.tensor_tensor(by_group(masked[:, ts, :]), by_group(logits[:, ts, N_GROUPS:NR]),
                                                 gkey[:, ts, :].unsqueeze(3).to_broadcast([P, TT // 2, N_GROUPS, PER_GROUP]), ALU.add))
            first_max(masked, vtop[:, 0, :], ekey, kkey[:, 0, :], chosen[:, 0, :, :], down32, N_EXP)
            in_halves(lambda ts: v.scalar_tensor_tensor(out=masked2[:, ts, :], in0=chosen[:, 0, ts, :], scalar=-3.0 * FAR, in1=masked[:, ts, :],
                                                        op0=ALU.mult, op1=ALU.add))
            first_max(masked2, vtop[:, 1, :], ekey, kkey[:, 1, :], chosen[:, 1, :, :], down32, N_EXP)
            v.wait_ge(dve, chain[0])
            g_logits = logits[:, :, 0:N_GROUPS]
            v.tensor_tensor(chosen_b[:, :, :], chosen[:, 0, :, :], chosen[:, 1, :, :], ALU.add).then_inc(chosen_ready, 1)
            v.tensor_tensor(gexp[:, :, :], g_logits, gmax[:, :].unsqueeze(2).to_broadcast([P, TT, N_GROUPS]), ALU.subtract).then_inc(gdiff_ready, 1)
            v.tensor_tensor(vdiff[:, :], vtop[:, 1, :], vtop[:, 0, :], ALU.subtract).then_inc(gdiff_ready, 1)
            link(v.tensor_scalar(expert[:, :], kkey[:, :, :].rearrange("p k t -> p (k t)"), -1.0, float(N_EXP), ALU.mult, ALU.add))

            v.wait_ge(counted, 1)
            counts = psum[0][:, 0:TT * N_EXP].rearrange("p (t e) -> p t e", t=TT).unsqueeze(1).to_broadcast([P, TOP_K, TT, N_EXP])
            totals = psum[0][:, TT * N_EXP:(TT + 1) * N_EXP]
            down_half = (BLOCK - 1) / (2.0 * BLOCK)
            step(v.tensor_scalar(extra[:, :], totals, 1.0 / BLOCK, -1.0 / BLOCK - down_half, ALU.mult, ALU.add))
            step(v.tensor_tensor(prod[:, :, :, :], counts, chosen[:, :, :, :], ALU.mult))
            before_last()
            step(v.tensor_scalar(extra[:, :], extra[:, :], RNE, -RNE, ALU.add, ALU.add))
            before_last()
            step(v.tensor_reduce(rank[:, :], prod[:, :, :, :].rearrange("p k t e -> p (k t) e"), AX, ALU.add))
            before_last()
            step(v.tensor_scalar(extra[:, :], extra[:, :], 0.0, None, ALU.max))
            before_last()
            step(v.tensor_scalar(blk[:, :], rank[:, :], 1.0 / BLOCK, -down_half, ALU.mult, ALU.add))
            before_last()
            step(v.tensor_tensor_scan(extra_sum[:, :], extra[:, :], zeros[:, :], 0.0, ALU.add, ALU.add))
            before_last()
            step(v.tensor_scalar(blk[:, :], blk[:, :], RNE, -RNE, ALU.add, ALU.add))
            before_last()
            step(v.tensor_tensor(extra_base[:, :], extra_sum[:, :], extra[:, :], ALU.subtract))
            before_last()
            link(v.scalar_tensor_tensor(out=slot[:, :], in0=blk[:, :], scalar=-float(BLOCK), in1=rank[:, :], op0=ALU.mult, op1=ALU.add))
            NP = TOP_K * TT
            link(v.tensor_tensor(prod[:, :, :, :].rearrange("p k t e -> p (k t) e"), chosen[:, :, :, :].rearrange("p k t e -> p (k t) e"),
                                 extra_base[:, :].unsqueeze(1).to_broadcast([P, NP, N_EXP]), ALU.mult))
            step(v.tensor_reduce(obase[:, :], prod[:, :, :, :].rearrange("p k t e -> p (k t) e"), AX, ALU.add))
            v.tensor_tensor(hot_slot[:, :, 0:BLOCK], up_slot.unsqueeze(1).to_broadcast([P, NP, BLOCK]),
                            slot[:, :].unsqueeze(2).to_broadcast([P, NP, BLOCK]), ALU.is_equal).then_inc(hot_ready, 1)
            v.wait_ge(dve, chain[0])
            link(v.scalar_tensor_tensor(out=item[:, :], in0=obase[:, :], scalar=N_EXP - 1.0, in1=expert[:, :], op0=ALU.add, op1=ALU.subtract))
            link(v.tensor_tensor(item[:, :], item[:, :], blk[:, :], ALU.add))
            link(v.scalar_tensor_tensor(out=item[:, :], in0=blk[:, :], scalar=0.0, in1=item[:, :], op0=ALU.is_gt, op1=ALU.mult))
            link(v.tensor_tensor(item[:, :], item[:, :], expert[:, :], ALU.add))
            link(v.tensor_tensor(item_match[:, :, :], up_item.unsqueeze(1).to_broadcast([P, NP, ITEMS]),
                                 item[:, :].unsqueeze(2).to_broadcast([P, NP, ITEMS]), ALU.is_equal))
            v.tensor_tensor(hot_item[:, :, :], item_match[:, :, :], pair1.unsqueeze(2).to_broadcast([P, NP, ITEMS]), ALU.mult).then_inc(hot_ready, 1)
            link(v.tensor_copy(n_over[:, :], extra_sum[0:1, N_EXP - 1:N_EXP]))
            link(v.tensor_tensor(over_cmp[:, :, :], extra_sum[0:1, :].unsqueeze(1).to_broadcast([1, MAX_OVER, N_EXP]),
                                 up_slot[0:1, 0:MAX_OVER].unsqueeze(2).to_broadcast([1, MAX_OVER, N_EXP]), ALU.is_le))
            link(v.tensor_reduce(over_exp[:, :], over_cmp[:, :, :], AX, ALU.add))
            link(v.tensor_copy(over_exp_i[:, :], over_exp[:, :]))
            v.wait_ge(table_summed, 1)
            link(v.tensor_scalar(empty[:, :], psum[1][:, 0:ITEMS], 0.0, NO_ROW, ALU.is_equal, ALU.mult))
            step(v.scalar_tensor_tensor(out=table[:, :], in0=psum[1][:, 0:ITEMS], scalar=half_less_1, in1=empty[:, :], op0=ALU.add, op1=ALU.add))
            step(v.scalar_tensor_tensor(out=y_rows[:, :], in0=psum[1][:, 0:ITEMS], scalar=half_less_1, in1=empty[:, :], op0=ALU.add, op1=ALU.add))
            before_last()
            link(v.tensor_scalar(table_x[:, :], table[:, :], 2.0 * T, -2.0 * T, ALU.is_ge, ALU.mult))
            v.tensor_tensor(x_rows[:, :], table_x[:, :], table[:, :], ALU.add).then_inc(rows_ready, 1)

            v.wait_ge(gexp_ready, 2)
            link(v.tensor_reduce(gsum[:, :], gexp[:, :, :], AX, ALU.add))
            link(v.tensor_scalar(wsum[:, :], vexp[:, :], 1.0, None, ALU.add))
            link(v.tensor_tensor(wsum[:, :], wsum[:, :], gsum[:, :], ALU.mult))
            link(v.reciprocal(weight[:, 0, :], wsum[:, :]))
            v.tensor_tensor(weight[:, 1, :], weight[:, 0, :], vexp[:, :], ALU.mult).then_inc(weights_ready, 1)

            def copy_xT(i, b, lag):
                v.wait_ge(xg_turned, i + 1)
                wait_free(v, gu_summed, i, lag)
                v.tensor_copy(xTg[b][:, :, :], psum[b][:, :].rearrange("p (j m) -> p j m", j=4)).then_inc(xTg_ready, 1)

            def make_hid(i, b, lag):
                v.wait_ge(gated_ready, i + 1)
                wait_free(v, hid_turned, i, lag)
                v.tensor_tensor(hid[b][0:BLOCK, :], gated[b][:, :], psum[2 + b][BLOCK:2 * BLOCK, 0:F], ALU.mult).then_inc(hid_ready, 1)

            def copy_hidT(i, b, lag):
                v.wait_ge(hid_turned, i + 1)
                wait_free(v, dn_summed, i, lag)
                v.tensor_copy(hidT[b][:, :, :], psum[4 + b][:, 0:2 * P].rearrange("p (j m) -> p j m", j=2)[:, :, 0:BLOCK]).then_inc(hidT_ready, 1)

            def dve_item(q, r):
                i = q + r * RING
                if not static(r) or q + 1 < N_EXP:
                    copy_xT(i + 1, (q + 1) % 2, 2)
                make_hid(i, q % 2, 2)
                copy_hidT(i, q % 2, 2)

            v.wait_ge(hid_zero, 2)
            copy_xT(0, 0, 2)
            rounds(v, dve_item)

            def dve_over(j):
                i = j + N_EXP
                copy_xT(i, 0, 1)
                make_hid(i, 0, 1)
                copy_hidT(i, 0, 1)

            overflow(v, dve_over)

            v.wait_ge(ln2_in, 32)
            for t in range(TT):
                if t < DVE_ADDED:
                    v.wait_ge(pairs_in[t][1], 16)
                    for h in range(2):
                        v.wait_ge(z_summed, 2 * t + h + 1)
                        step(v.scalar_tensor_tensor(out=z_of(t, h), in0=z_of(t, h), scalar=weight[:, 1, t:t + 1], in1=psum[2 * t + h][:, :],
                                                    op0=ALU.mult, op1=ALU.add))
                    v.wait_ge(dve, chain[0])
                for h in range(2):
                    v.wait_ge(z_summed, 2 * t + h + 1)
                    step(v.bn_stats(stats[:, t, h, :], z_of(t, h)))
                v.wait_ge(dve, chain[0])
                link(v.bn_aggr(moments[:, t, :], stats[:, t, :, :]))
                v.tensor_scalar(rstd[:, t:t + 1], moments[:, t, 1:2], LN_EPS, None, ALU.add).then_inc(var2_ready, 1)
                halves = (0, 1) if t == TT - 1 else (1,)
                for h in halves:
                    cols = slice(h * H, (h + 1) * H)
                    step(v.scalar_tensor_tensor(out=pair_y[t][1][:, cols], in0=z_of(t, h), scalar=moments[:, t, 0:1],
                                                in1=ln2g[:, cols], op0=ALU.subtract, op1=ALU.mult))
                v.wait_ge(dev2_ready, t + 1)
                link(v.reciprocal(rstd[:, t:t + 1], rstd[:, t:t + 1]))
                if t < TT - 1:
                    v.scalar_tensor_tensor(out=shift[:, t:t + 1], in0=moments[:, t, 0:1], scalar=-1.0, in1=rstd[:, t:t + 1],
                                           op0=ALU.mult, op1=ALU.mult).then_inc(moments2_ready, 1)
                for h in halves:
                    z = pair_y[t][1][:, h * H:(h + 1) * H]
                    v.scalar_tensor_tensor(out=z, in0=z, scalar=rstd[:, t:t + 1], in1=ln2b[:, h * H:(h + 1) * H],
                                           op0=ALU.mult, op1=ALU.add).then_inc(out_ready, 1)


_INS = ["x", "w_in", "rg_conv_w", "rg_conv_b", "rg_gate_a_w", "rg_gate_a_b", "rg_gate_x_w", "rg_gate_x_b",
        "rg_lambda", "sc_conv_w", "w_out", "ln1_g", "ln1_b", "router_group_w", "router_group_b",
        "router_expert_w", "router_expert_b", "exp_w_gate", "exp_w_up", "exp_w_down", "ln2_g", "ln2_b"]


def kernel(**inputs):
    import numpy as _np
    import concourse.bacc as _bacc
    from concourse import mybir as _mybir
    from concourse.bass_utils import run_bass_kernel_spmd as _run

    nc = _bacc.Bacc("TRN2", target_bir_lowering=False, num_devices=1)
    arrays, args = {}, []
    for name in _INS:
        a = _np.ascontiguousarray(inputs[name])
        arrays[f"in_{name}"] = a
        args.append(nc.dram_tensor(f"in_{name}", a.shape, _mybir.dt.from_np(a.dtype), kind="ExternalInput").ap())
    shape = tuple(inputs["x"].shape)
    args.append(nc.dram_tensor("out_0", shape, _mybir.dt.float32, kind="ExternalOutput").ap())
    hybrid_moe_layer(nc, *args)
    r = _run(nc, [arrays], core_ids=[0])
    return r.results[0]["out_0"]
```
